# Optimizing a Trainium2 kernel written in Bass

```python
import jax, jax.numpy as jnp
from jax import lax
import numpy as np
import math
import jax
import jax.numpy as jnp

D_MODEL = 1024
BATCH = 1
SEQ = 512
DEPTH = 2

HEAD_DIM = 64
NSA_HEADS = 8
NSA_KV_GROUPS = 1
NSA_HPG = NSA_HEADS // NSA_KV_GROUPS
SB_HEADS = 4
SB_HEAD_DIM = 128
ROPE_THETA = 500000.0
ROT_DIM = HEAD_DIM // 4
CMP_BLOCK = 32
CMP_STRIDE = 16
CMP_HIDDEN = 256
SEL_BLOCK = 64
SEL_TOP_N = 8
WINDOW = 512
Q_BLOCK = 128
D_FF = 4 * D_MODEL
RMS_EPS = 1e-6
NSA_W = NSA_HEADS * HEAD_DIM
KV_W = NSA_KV_GROUPS * HEAD_DIM
SB_W = SB_HEADS * SB_HEAD_DIM
IN_W = NSA_W + 6 * KV_W + 3 * NSA_HEADS + 3 * SB_W + 2 * D_MODEL


def rms_norm(x, g):
    xf = x.astype(jnp.float32)
    y = xf * lax.rsqrt(jnp.mean(xf * xf, axis=-1, keepdims=True) + RMS_EPS)
    return (y * g.astype(jnp.float32)).astype(x.dtype)

def to_heads(t, n, dh):
    b, s = t.shape[:2]
    return t.reshape(b, s, n, dh).transpose(0, 2, 1, 3)

def partial_rope(x, positions):
    half = ROT_DIM // 2
    inv_freq = jnp.power(ROPE_THETA, jnp.arange(half, dtype=jnp.float32) * (-2.0 / ROT_DIM))
    ang = positions.astype(jnp.float32)[:, None, :, None] * inv_freq
    cos, sin = jnp.cos(ang), jnp.sin(ang)
    xf = x.astype(jnp.float32)
    x1, x2, rest = xf[..., :half], xf[..., half:ROT_DIM], xf[..., ROT_DIM:]
    out = jnp.concatenate([x1 * cos - x2 * sin, x2 * cos + x1 * sin, rest], axis=-1)
    return out.astype(x.dtype)

def compress_blocks(kv, pe, w1, w2):
    s = kv.shape[2]
    nc = (s - CMP_BLOCK) // CMP_STRIDE + 1
    idx = CMP_STRIDE * jnp.arange(nc)[:, None] + jnp.arange(CMP_BLOCK)[None, :]
    blocks = kv[:, :, idx] + pe
    flat = blocks.reshape(blocks.shape[:3] + (CMP_BLOCK * HEAD_DIM,))
    return jax.nn.gelu(flat @ w1) @ w2

def nsa_attention(q_rope, q_plain, k_cmp, v_cmp, k_slc, v_slc, k_win, v_win, gates):
    out_dtype = q_rope.dtype
    f32 = jnp.float32
    scale = HEAD_DIM ** -0.5
    q_rope, q_plain, gates = q_rope.astype(f32) * scale, q_plain.astype(f32) * scale, gates.astype(f32)
    k_cmp, v_cmp = k_cmp.astype(f32), v_cmp.astype(f32)
    b, g, h, s, dh = q_rope.shape
    nb = s // Q_BLOCK
    nc = k_cmp.shape[2]
    ns = s // SEL_BLOCK
    n_sel = min(SEL_TOP_N, ns)
    cmp_last = CMP_STRIDE * jnp.arange(nc) + CMP_BLOCK - 1
    c_start = CMP_STRIDE * jnp.arange(nc)[:, None]
    s_start = SEL_BLOCK * jnp.arange(ns)[None, :]
    overlap = ((c_start < s_start + SEL_BLOCK) & (c_start + CMP_BLOCK > s_start)).astype(f32)
    ks_blocks = k_slc.astype(f32).reshape(b, g, ns, SEL_BLOCK, dh)
    vs_blocks = v_slc.astype(f32).reshape(b, g, ns, SEL_BLOCK, dh)
    pad = ((0, 0), (0, 0), (WINDOW, 0), (0, 0))
    kw_pad = jnp.pad(k_win.astype(f32), pad)
    vw_pad = jnp.pad(v_win.astype(f32), pad)
    b_ix = jnp.arange(b)[:, None, None, None]
    g_ix = jnp.arange(g)[None, :, None, None]
    blk = jnp.arange(ns)

    def block(i):
        q0 = i * Q_BLOCK
        t = q0 + jnp.arange(Q_BLOCK)
        qr = lax.dynamic_slice_in_dim(q_rope, q0, Q_BLOCK, axis=3)
        qp = lax.dynamic_slice_in_dim(q_plain, q0, Q_BLOCK, axis=3)
        gt = lax.dynamic_slice_in_dim(gates, q0, Q_BLOCK, axis=3)
        vis_c = cmp_last[None, :] <= t[:, None]
        s_c = jnp.einsum('bghqd,bgcd->bghqc', qp, k_cmp)
        p_c = jax.nn.softmax(jnp.where(vis_c, s_c, -1e30), axis=-1) * vis_c.astype(f32)
        o_c = jnp.einsum('bghqc,bgcd->bghqd', p_c, v_cmp)
        imp = jnp.einsum('bghqc,cn->bgqn', p_c, overlap)
        cur = t // SEL_BLOCK
        valid = blk[None, :] <= cur[:, None]
        forced = (blk[None, :] == 0) | (blk[None, :] == cur[:, None]) | (blk[None, :] == cur[:, None] - 1)
        score = jnp.where(valid, jnp.where(forced, jnp.inf, imp), -1.0)
        _, sel = lax.top_k(score, n_sel)
        k_g = ks_blocks[b_ix, g_ix, sel].reshape(b, g, Q_BLOCK, n_sel * SEL_BLOCK, dh)
        v_g = vs_blocks[b_ix, g_ix, sel].reshape(b, g, Q_BLOCK, n_sel * SEL_BLOCK, dh)
        pos = sel[..., None] * SEL_BLOCK + jnp.arange(SEL_BLOCK)
        vis_s = (pos <= t[:, None, None]).reshape(b, g, Q_BLOCK, n_sel * SEL_BLOCK)
        s_s = jnp.einsum('bghqd,bgqkd->bghqk', qr, k_g)
        p_s = jax.nn.softmax(jnp.where(vis_s[:, :, None], s_s, -1e30), axis=-1)
        o_s = jnp.einsum('bghqk,bgqkd->bghqd', p_s, v_g)
        kw = lax.dynamic_slice_in_dim(kw_pad, q0, Q_BLOCK + WINDOW, axis=2)
        vw = lax.dynamic_slice_in_dim(vw_pad, q0, Q_BLOCK + WINDOW, axis=2)
        kpos = q0 - WINDOW + jnp.arange(Q_BLOCK + WINDOW)
        vis_w = (kpos[None, :] <= t[:, None]) & (kpos[None, :] > t[:, None] - WINDOW) & (kpos[None, :] >= 0)
        s_w = jnp.einsum('bghqd,bgkd->bghqk', qr, kw)
        p_w = jax.nn.softmax(jnp.where(vis_w, s_w, -1e30), axis=-1)
        o_w = jnp.einsum('bghqk,bgkd->bghqd', p_w, vw)
        return gt[..., 0:1] * o_c + gt[..., 1:2] * o_s + gt[..., 2:3] * o_w

    out = lax.map(block, jnp.arange(nb))
    out = out.transpose(1, 0, 4, 2, 3, 5).reshape(b, s, g * h * dh)
    return out.astype(out_dtype)

def stick_breaking_attention(q, k, v):
    out_dtype = q.dtype
    f32 = jnp.float32
    b, hh, s, dh = q.shape
    qf = q.astype(f32) * (SB_HEAD_DIM ** -0.5)
    kf, vf = k.astype(f32), v.astype(f32)
    nb = s // Q_BLOCK
    r = jnp.arange(Q_BLOCK)
    tri = (r[:, None] >= r[None, :]).astype(f32)
    diag_mask = r[None, :] < r[:, None]
    outs = []
    for i in range(nb):
        q0 = i * Q_BLOCK
        qb = qf[:, :, q0:q0 + Q_BLOCK]
        z_d = jnp.einsum('bhqd,bhkd->bhqk', qb, kf[:, :, q0:q0 + Q_BLOCK])
        l_d = jnp.where(diag_mask, jax.nn.log_sigmoid(-z_d), 0.0)
        c_d = l_d @ tri
        a_d = jnp.where(diag_mask, jnp.exp(z_d + c_d), 0.0)
        o = jnp.einsum('bhqk,bhkd->bhqd', a_d, vf[:, :, q0:q0 + Q_BLOCK])
        if i > 0:
            z_o = jnp.einsum('bhqd,bhkd->bhqk', qb, kf[:, :, :q0]).reshape(b, hh, Q_BLOCK, i, Q_BLOCK)
            c_o = jax.nn.log_sigmoid(-z_o) @ tri
            ci = jnp.arange(i)
            upper = (ci[:, None] > ci[None, :]).astype(f32)
            off = c_o[..., 0] @ upper + c_d[..., 0:1]
            a_o = jnp.exp(z_o + c_o + off[..., None])
            o = o + jnp.einsum('bhqck,bhckd->bhqd', a_o, vf[:, :, :q0].reshape(b, hh, i, Q_BLOCK, dh))
        outs.append(o)
    out = jnp.concatenate(outs, axis=2)
    return out.transpose(0, 2, 1, 3).reshape(b, s, hh * dh).astype(out_dtype)

def split_columns(proj):
    sizes = [NSA_W, KV_W, KV_W, KV_W, KV_W, KV_W, KV_W, 3 * NSA_HEADS, SB_W, SB_W, SB_W, 2 * D_MODEL]
    parts, start = [], 0
    for n in sizes:
        parts.append(proj[..., start:start + n])
        start += n
    return parts

def hybrid_layer(x, positions, norm_g, w_in, cmp_pe, cmp_w1, cmp_w2, w_nsa_o, w_sb_o, w_out, w_ff1, w_ff2):
    b, s, _ = x.shape
    hn = rms_norm(x, norm_g[0])
    (nsa_q, k_c, v_c, k_s, v_s, k_w, v_w, nsa_g, sb_q, sb_k, sb_v, merge_g) = split_columns(hn @ w_in)
    grp = (b, NSA_KV_GROUPS, NSA_HPG, s, HEAD_DIM)
    q_plain = to_heads(nsa_q, NSA_HEADS, HEAD_DIM)
    q_rope = partial_rope(q_plain, positions).reshape(grp)
    q_plain = q_plain.reshape(grp)
    kc = compress_blocks(to_heads(k_c, NSA_KV_GROUPS, HEAD_DIM), cmp_pe[0], cmp_w1[0], cmp_w2[0])
    vc = compress_blocks(to_heads(v_c, NSA_KV_GROUPS, HEAD_DIM), cmp_pe[1], cmp_w1[1], cmp_w2[1])
    ks = partial_rope(to_heads(k_s, NSA_KV_GROUPS, HEAD_DIM), positions)
    kw = partial_rope(to_heads(k_w, NSA_KV_GROUPS, HEAD_DIM), positions)
    gates = jax.nn.sigmoid(nsa_g).reshape(b, s, NSA_HEADS, 3).transpose(0, 2, 1, 3).reshape(grp[:4] + (3,))
    y_nsa = nsa_attention(q_rope, q_plain, kc, vc, ks, to_heads(v_s, NSA_KV_GROUPS, HEAD_DIM),
                          kw, to_heads(v_w, NSA_KV_GROUPS, HEAD_DIM), gates) @ w_nsa_o
    y_sb = stick_breaking_attention(to_heads(sb_q, SB_HEADS, SB_HEAD_DIM), to_heads(sb_k, SB_HEADS, SB_HEAD_DIM),
                                    to_heads(sb_v, SB_HEADS, SB_HEAD_DIM)) @ w_sb_o
    gate = jax.nn.sigmoid(merge_g)
    mixed = (gate[..., :D_MODEL] * y_nsa + gate[..., D_MODEL:] * y_sb) @ w_out
    x = x + rms_norm(mixed, norm_g[1])
    hf = rms_norm(x, norm_g[2])
    ff = jnp.square(jax.nn.relu(hf @ w_ff1)) @ w_ff2
    return x + rms_norm(ff, norm_g[3])

def first_inputs(seed: int = 0) -> dict:
    key = jax.random.key(seed)
    ks = jax.random.split(key, 12)
    f32 = jnp.float32

    def nrm(k, shape, fan_in):
        return jax.random.normal(k, shape, f32) * (fan_in ** -0.5)

    x = jax.random.normal(ks[0], (BATCH, SEQ, D_MODEL), f32)
    positions = jnp.broadcast_to(jnp.arange(SEQ, dtype=jnp.int32)[None, :], (BATCH, SEQ))
    norm_g = 1.0 + 0.05 * jax.random.normal(ks[1], (DEPTH, 4, D_MODEL), f32)
    w_in = nrm(ks[2], (DEPTH, D_MODEL, IN_W), D_MODEL)
    cmp_pe = 0.5 * jax.random.normal(ks[3], (DEPTH, 2, CMP_BLOCK, HEAD_DIM), f32)
    cmp_w1 = nrm(ks[4], (DEPTH, 2, CMP_BLOCK * HEAD_DIM, CMP_HIDDEN), CMP_BLOCK * HEAD_DIM)
    cmp_w2 = nrm(ks[5], (DEPTH, 2, CMP_HIDDEN, HEAD_DIM), CMP_HIDDEN)
    w_nsa_o = nrm(ks[6], (DEPTH, NSA_W, D_MODEL), NSA_W)
    w_sb_o = nrm(ks[7], (DEPTH, SB_W, D_MODEL), SB_W)
    w_out = nrm(ks[8], (DEPTH, D_MODEL, D_MODEL), D_MODEL)
    w_ff1 = nrm(ks[9], (DEPTH, D_MODEL, D_FF), D_MODEL)
    w_ff2 = nrm(ks[10], (DEPTH, D_FF, D_MODEL), D_FF)
    return {'x': x, 'positions': positions, 'norm_g': norm_g, 'w_in': w_in, 'cmp_pe': cmp_pe,
            'cmp_w1': cmp_w1, 'cmp_w2': cmp_w2, 'w_nsa_o': w_nsa_o, 'w_sb_o': w_sb_o,
            'w_out': w_out, 'w_ff1': w_ff1, 'w_ff2': w_ff2}

def first_block(x, positions, norm_g, w_in, cmp_pe, cmp_w1, cmp_w2, w_nsa_o, w_sb_o, w_out, w_ff1, w_ff2):
    for layer in range(DEPTH):
        x = hybrid_layer(x, positions, norm_g[layer], w_in[layer], cmp_pe[layer], cmp_w1[layer],
                         cmp_w2[layer], w_nsa_o[layer], w_sb_o[layer], w_out[layer],
                         w_ff1[layer], w_ff2[layer])
    return x


GRID_W = 64
CTX_LEN = 256

N_MIXERS = 2
D_FF_2 = 4 * D_MODEL
N_MOD = 6
NORM_EPS = 1e-6

MLA_HEADS = 8
MLA_NOPE = 128
MLA_ROPE = 64
MLA_V = 128
MLA_Q_RANK = 384
MLA_KV_RANK = 256
ROPE_BASE = 10000.0

GLA_HEADS = 4
GLA_DK = D_MODEL // 2 // GLA_HEADS
GLA_DV = D_MODEL // GLA_HEADS
GLA_GATE_RANK = 16
GLA_TAU = 16.0
GLA_CHUNK = 64


def rms_norm_2(x, g):
    xf = x.astype(jnp.float32)
    y = xf * lax.rsqrt(jnp.mean(xf * xf, axis=-1, keepdims=True) + NORM_EPS)
    return (y * g.astype(jnp.float32)).astype(x.dtype)

def modulate(h, shift, scale):
    return h * (1.0 + scale) + shift

def sqrelu_mlp(h, w1, w2):
    return jnp.square(jax.nn.relu(h @ w1)) @ w2

def axial_rope_tables(n_tokens):
    rows = n_tokens // GRID_W
    row = jnp.repeat(jnp.arange(rows, dtype=jnp.float32), GRID_W)
    col = jnp.tile(jnp.arange(GRID_W, dtype=jnp.float32), rows)
    half = MLA_ROPE // 2
    inv_freq = ROPE_BASE ** (-jnp.arange(0, half, 2, dtype=jnp.float32) / half)
    ang_r = row[:, None] * inv_freq
    ang_c = col[:, None] * inv_freq
    return (jnp.cos(ang_r), jnp.sin(ang_r), jnp.cos(ang_c), jnp.sin(ang_c))

def _rotate_half(x, cos, sin):
    x1, x2 = jnp.split(x, 2, axis=-1)
    return jnp.concatenate([x1 * cos - x2 * sin, x1 * sin + x2 * cos], axis=-1)

def apply_axial_rope(x, rope):
    cos_r, sin_r, cos_c, sin_c = rope
    if x.ndim == 4:
        cos_r, sin_r, cos_c, sin_c = (t[:, None, :] for t in rope)
    x_r, x_c = jnp.split(x, 2, axis=-1)
    out = jnp.concatenate([_rotate_half(x_r, cos_r, sin_r), _rotate_half(x_c, cos_c, sin_c)], axis=-1)
    return out.astype(x.dtype)

def mla_attend(q_nope, q_rope, k_nope, k_rope, v):
    scale = (MLA_NOPE + MLA_ROPE) ** -0.5
    s = (jnp.einsum('bqhd,bkhd->bhqk', q_nope, k_nope, preferred_element_type=jnp.float32)
         + jnp.einsum('bqhr,bkr->bhqk', q_rope, k_rope, preferred_element_type=jnp.float32))
    p = jax.nn.softmax(s * scale, axis=-1)
    return jnp.einsum('bhqk,bkhd->bqhd', p.astype(v.dtype), v)

def mla_mixer(h_ctx, h_lat, rope, need_ctx, w_dq, g_q, w_uq, w_dkv, g_kv, w_ukv, w_o):
    B, C, _ = h_ctx.shape
    S = h_lat.shape[1]
    T = C + S
    h_all = jnp.concatenate([h_ctx, h_lat], axis=1)
    cq = rms_norm_2(h_all @ w_dq, g_q)
    q = (cq @ w_uq).reshape(B, T, MLA_HEADS, MLA_NOPE + MLA_ROPE)
    ckv = h_all @ w_dkv
    c_kv = rms_norm_2(ckv[..., :MLA_KV_RANK], g_kv)
    kv = (c_kv @ w_ukv).reshape(B, T, MLA_HEADS, MLA_NOPE + MLA_V)
    q_nope, q_rope = q[..., :MLA_NOPE], q[..., MLA_NOPE:]
    k_nope, v = kv[..., :MLA_NOPE], kv[..., MLA_NOPE:]
    k_rope = ckv[..., MLA_KV_RANK:]
    q_rope = jnp.concatenate([q_rope[:, :C], apply_axial_rope(q_rope[:, C:], rope)], axis=1)
    k_rope = jnp.concatenate([k_rope[:, :C], apply_axial_rope(k_rope[:, C:], rope)], axis=1)

    nb = S // Q_BLOCK
    def to_blocks(a):
        return jnp.moveaxis(a.reshape(B, nb, Q_BLOCK, *a.shape[2:]), 1, 0)
    qn_blk = to_blocks(q_nope[:, C:])
    qr_blk = to_blocks(q_rope[:, C:])
    o_lat = lax.map(lambda qb: mla_attend(qb[0], qb[1], k_nope, k_rope, v), (qn_blk, qr_blk))
    o_lat = jnp.moveaxis(o_lat, 0, 1).reshape(B, S, MLA_HEADS * MLA_V)
    y_lat = o_lat @ w_o

    y_ctx = None
    if need_ctx:
        o_ctx = mla_attend(q_nope[:, :C], q_rope[:, :C], k_nope[:, :C], k_rope[:, :C], v[:, :C])
        y_ctx = o_ctx.reshape(B, C, MLA_HEADS * MLA_V) @ w_o
    return y_ctx, y_lat

def gla_log_gate(h, w1, w2, b):
    return jax.nn.log_sigmoid(((h @ w1) @ w2 + b).astype(jnp.float32)) / GLA_TAU

def gla_chunk_scan(q, k, v, g, s0):
    B, T, H, _ = q.shape
    n = T // GLA_CHUNK
    def to_chunks(a):
        return a.reshape(B, n, GLA_CHUNK, H, a.shape[-1]).transpose(1, 0, 3, 2, 4).astype(jnp.float32)
    mask = jnp.tril(jnp.ones((GLA_CHUNK, GLA_CHUNK), dtype=bool))
    def step(s, inp):
        qc, kc, vc, gc = inp
        G = jnp.cumsum(gc, axis=2)
        G_last = G[:, :, -1:, :]
        q_t = qc * jnp.exp(G)
        k_t = kc * jnp.exp(-G)
        a = jnp.where(mask, jnp.einsum('bhid,bhjd->bhij', q_t, k_t), 0.0)
        o = jnp.einsum('bhij,bhjv->bhiv', a, vc) + jnp.einsum('bhid,bhdv->bhiv', q_t, s)
        k_end = kc * jnp.exp(G_last - G)
        s_new = jnp.exp(G_last[:, :, 0, :])[..., None] * s + jnp.einsum('bhjd,bhjv->bhdv', k_end, vc)
        return s_new, o
    s_fin, o = lax.scan(step, s0, (to_chunks(q), to_chunks(k), to_chunks(v), to_chunks(g)))
    o = o.transpose(1, 0, 3, 2, 4).reshape(B, T, H, v.shape[-1])
    return o, s_fin

def gla_mixer(h_ctx, h_lat, need_ctx, w_q, w_k, w_v, w_r, w_gate1, w_gate2, b_gate, g_o, w_o):
    B, C, _ = h_ctx.shape
    S = h_lat.shape[1]
    T = C + S
    h_all = jnp.concatenate([h_ctx, h_lat], axis=1)
    def heads(a, d):
        return a.reshape(B, T, GLA_HEADS, d)
    q = heads(h_all @ w_q, GLA_DK) * (GLA_DK ** -0.5)
    k = heads(h_all @ w_k, GLA_DK)
    v = heads(h_all @ w_v, GLA_DV)
    g_fwd = heads(gla_log_gate(h_all, w_gate1[0], w_gate2[0], b_gate[0]), GLA_DK)
    g_bwd = heads(gla_log_gate(h_all, w_gate1[1], w_gate2[1], b_gate[1]), GLA_DK)
    flip = lambda a: jnp.flip(a, axis=1)
    zeros = jnp.zeros((B, GLA_HEADS, GLA_DK, GLA_DV), jnp.float32)
    qc, kc, vc = q[:, :C], k[:, :C], v[:, :C]
    ql, kl, vl = q[:, C:], k[:, C:], v[:, C:]
    o_cf, s_cf = gla_chunk_scan(qc, kc, vc, g_fwd[:, :C], zeros)
    o_cb, s_cb = gla_chunk_scan(flip(qc), flip(kc), flip(vc), flip(g_bwd[:, :C]), zeros)
    o_lf, _ = gla_chunk_scan(ql, kl, vl, g_fwd[:, C:], s_cf)
    o_lb, _ = gla_chunk_scan(flip(ql), flip(kl), flip(vl), flip(g_bwd[:, C:]), s_cb)
    def out(o, h):
        y = rms_norm_2(o, g_o).astype(h.dtype).reshape(B, -1, GLA_HEADS * GLA_DV)
        return (y * jax.nn.silu(h @ w_r)) @ w_o
    y_lat = out(o_lf + flip(o_lb), h_lat)
    y_ctx = out(o_cf + flip(o_cb), h_ctx) if need_ctx else None
    return y_ctx, y_lat

def second_inputs(seed: int = 0) -> dict:
    key = jax.random.key(seed)
    ks = jax.random.split(key, 32)
    D = D_MODEL
    n_a = (DEPTH + N_MIXERS - 1) // N_MIXERS
    n_b = DEPTH // N_MIXERS
    def nrm(k, shape, scale):
        return jax.random.normal(k, shape, jnp.float32) * scale
    return {
        'x': nrm(ks[0], (BATCH, SEQ, D), 1.0),
        'c': nrm(ks[1], (BATCH, D), 1.0),
        'ctx': nrm(ks[2], (BATCH, CTX_LEN, D), 1.0),
        'c_ctx': nrm(ks[3], (D,), 1.0),
        'ada_w': nrm(ks[4], (DEPTH, D, N_MOD * D), 0.5 * D ** -0.5),
        'ada_b': nrm(ks[5], (DEPTH, N_MOD * D), 0.02),
        'norm_g': 1.0 + nrm(ks[6], (DEPTH, 4, D), 0.02),
        'mlp_w1': nrm(ks[7], (DEPTH, D, D_FF_2), D ** -0.5),
        'mlp_w2': nrm(ks[8], (DEPTH, D_FF_2, D), D_FF_2 ** -0.5),
        'mla_w_dq': nrm(ks[9], (n_a, D, MLA_Q_RANK), D ** -0.5),
        'mla_g_q': 1.0 + nrm(ks[10], (n_a, MLA_Q_RANK), 0.02),
        'mla_w_uq': nrm(ks[11], (n_a, MLA_Q_RANK, MLA_HEADS * (MLA_NOPE + MLA_ROPE)), MLA_Q_RANK ** -0.5),
        'mla_w_dkv': nrm(ks[12], (n_a, D, MLA_KV_RANK + MLA_ROPE), D ** -0.5),
        'mla_g_kv': 1.0 + nrm(ks[13], (n_a, MLA_KV_RANK), 0.02),
        'mla_w_ukv': nrm(ks[14], (n_a, MLA_KV_RANK, MLA_HEADS * (MLA_NOPE + MLA_V)), MLA_KV_RANK ** -0.5),
        'mla_w_o': nrm(ks[15], (n_a, MLA_HEADS * MLA_V, D), (MLA_HEADS * MLA_V) ** -0.5),
        'gla_w_q': nrm(ks[16], (n_b, D, GLA_HEADS * GLA_DK), D ** -0.5),
        'gla_w_k': nrm(ks[17], (n_b, D, GLA_HEADS * GLA_DK), D ** -0.5),
        'gla_w_v': nrm(ks[18], (n_b, D, GLA_HEADS * GLA_DV), D ** -0.5),
        'gla_w_r': nrm(ks[19], (n_b, D, GLA_HEADS * GLA_DV), D ** -0.5),
        'gla_w_gate1': nrm(ks[20], (n_b, 2, D, GLA_GATE_RANK), D ** -0.5),
        'gla_w_gate2': nrm(ks[21], (n_b, 2, GLA_GATE_RANK, GLA_HEADS * GLA_DK), GLA_GATE_RANK ** -0.5),
        'gla_b_gate': nrm(ks[22], (n_b, 2, GLA_HEADS * GLA_DK), 0.1),
        'gla_g_o': 1.0 + nrm(ks[23], (n_b, GLA_DV), 0.02),
        'gla_w_o': nrm(ks[24], (n_b, GLA_HEADS * GLA_DV, D), (GLA_HEADS * GLA_DV) ** -0.5),
    }

def second_block(x, c, ctx, c_ctx, ada_w, ada_b, norm_g, mlp_w1, mlp_w2,
              mla_w_dq, mla_g_q, mla_w_uq, mla_w_dkv, mla_g_kv, mla_w_ukv, mla_w_o,
              gla_w_q, gla_w_k, gla_w_v, gla_w_r, gla_w_gate1, gla_w_gate2, gla_b_gate,
              gla_g_o, gla_w_o):
    B, S, D = x.shape
    rope = axial_rope_tables(S)
    silu_c = jax.nn.silu(c)
    silu_cc = jax.nn.silu(c_ctx)
    x_lat, x_ctx = x, ctx
    for i in range(DEPTH):
        need_ctx = i < DEPTH - 1
        j = i // N_MIXERS
        m_lat = (silu_c @ ada_w[i] + ada_b[i]).reshape(B, N_MOD, 1, D)
        m_ctx = (silu_cc @ ada_w[i] + ada_b[i]).reshape(N_MOD, D)
        h_lat = modulate(rms_norm_2(x_lat, norm_g[i, 0]), m_lat[:, 0], m_lat[:, 1])
        h_ctx = modulate(rms_norm_2(x_ctx, norm_g[i, 0]), m_ctx[0], m_ctx[1])
        if i % N_MIXERS == 0:
            y_ctx, y_lat = mla_mixer(h_ctx, h_lat, rope, need_ctx, mla_w_dq[j], mla_g_q[j], mla_w_uq[j],
                                     mla_w_dkv[j], mla_g_kv[j], mla_w_ukv[j], mla_w_o[j])
        else:
            y_ctx, y_lat = gla_mixer(h_ctx, h_lat, need_ctx, gla_w_q[j], gla_w_k[j], gla_w_v[j], gla_w_r[j],
                                     gla_w_gate1[j], gla_w_gate2[j], gla_b_gate[j], gla_g_o[j], gla_w_o[j])
        x_lat = x_lat + m_lat[:, 2] * rms_norm_2(y_lat, norm_g[i, 1])
        h = modulate(rms_norm_2(x_lat, norm_g[i, 2]), m_lat[:, 3], m_lat[:, 4])
        x_lat = x_lat + m_lat[:, 5] * rms_norm_2(sqrelu_mlp(h, mlp_w1[i], mlp_w2[i]), norm_g[i, 3])
        if need_ctx:
            x_ctx = x_ctx + m_ctx[2] * rms_norm_2(y_ctx, norm_g[i, 1])
            h = modulate(rms_norm_2(x_ctx, norm_g[i, 2]), m_ctx[3], m_ctx[4])
            x_ctx = x_ctx + m_ctx[5] * rms_norm_2(sqrelu_mlp(h, mlp_w1[i], mlp_w2[i]), norm_g[i, 3])
    return x_lat


def setup_inputs(seed=0):
    out = dict(first_inputs(seed))
    for name, value in second_inputs(seed + 1).items():
        if name != "x":
            out[name + "_2"] = value
    return out


def reference(
    x, positions, norm_g, w_in, cmp_pe, cmp_w1, cmp_w2, w_nsa_o, w_sb_o, w_out, w_ff1, w_ff2,
    c_2, ctx_2, c_ctx_2, ada_w_2, ada_b_2, norm_g_2, mlp_w1_2, mlp_w2_2, mla_w_dq_2, mla_g_q_2,
    mla_w_uq_2, mla_w_dkv_2, mla_g_kv_2, mla_w_ukv_2, mla_w_o_2, gla_w_q_2, gla_w_k_2,
    gla_w_v_2, gla_w_r_2, gla_w_gate1_2, gla_w_gate2_2, gla_b_gate_2, gla_g_o_2, gla_w_o_2,
):
    x = first_block(
        x, positions, norm_g, w_in, cmp_pe, cmp_w1, cmp_w2, w_nsa_o, w_sb_o, w_out, w_ff1,
        w_ff2,
    )
    return second_block(
        x, c_2, ctx_2, c_ctx_2, ada_w_2, ada_b_2, norm_g_2, mlp_w1_2, mlp_w2_2, mla_w_dq_2,
        mla_g_q_2, mla_w_uq_2, mla_w_dkv_2, mla_g_kv_2, mla_w_ukv_2, mla_w_o_2, gla_w_q_2,
        gla_w_k_2, gla_w_v_2, gla_w_r_2, gla_w_gate1_2, gla_w_gate2_2, gla_b_gate_2, gla_g_o_2,
        gla_w_o_2,
    )


_drawn_inputs = setup_inputs


def setup_inputs(seed=0):
    import zlib

    import numpy as np

    out = dict(_drawn_inputs(seed))
    spreads = {}
    factors = {'ctx_2': 2.671,
     'norm_g_2': 5.792,
     'mla_g_q_2': 8.0,
     'mla_g_kv_2': 8.0,
     'gla_b_gate_2': 6.349,
     'gla_g_o_2': 8.0}
    for name, (base, spread) in spreads.items():
        noise = np.random.default_rng([zlib.crc32(name.encode()), seed]).standard_normal(out[name].shape)
        drawn = base * np.exp(spread * noise) if base else spread * noise
        out[name] = jnp.asarray(drawn.astype(out[name].dtype))
    for name, factor in factors.items():
        out[name] = (out[name] * factor).astype(out[name].dtype)
    return out
```

```python
from contextlib import ExitStack, contextmanager

import numpy as np
import concourse.bass as bass
from concourse import mybir

F32 = mybir.dt.float32
F32R = mybir.dt.float32r
I32 = mybir.dt.int32
U32 = mybir.dt.uint32
ALU = mybir.AluOpType
ACT = mybir.ActivationFunctionType
AX_X = mybir.AxisListType.X

P = 128
D = 1024
KT = D // P
SEQ = 512
CTX = 256
TOK = SEQ + CTX
DEPTH = 2
UNIT = 2048
EPS = 1e-6
NEG = -1e30

HD = 64
HEADS = 8
SBH = 4
CMP_T, CMP_S = 32, 16
NC = (SEQ - CMP_T) // CMP_S + 1
NCP = 32
QT = SEQ // P
UNITS_QKV = 10
UNITS_CMP = 4
UNITS_MERGE = 12
UNITS_OUT = 4
FF_GROUPS = 8
UNITS_FF = 4 * FF_GROUPS
UNITS_1 = UNITS_QKV + UNITS_CMP + UNITS_MERGE + UNITS_OUT + UNITS_FF

MH = 8
MLA_U = 1280
GH = 4
CH = 64

CONSTS = ["ident", "negtri", "negones", "ones", "sbneg", "sb01", "causal", "cmpneg", "cmpvis",
          "rope_perm", "axial_perm", "gla_f", "gla_b"]


def const_table():
    r = np.arange(P)
    t = {}
    t["ident"] = np.eye(P)
    t["negtri"] = -(r[:, None] >= r[None, :]).astype(float)
    t["negones"] = -np.ones((P, P))
    t["ones"] = np.ones((P, P))
    t["sbneg"] = np.where(r[:, None] < r[None, :], 0.0, NEG)
    t["sb01"] = (r[:, None] < r[None, :]).astype(float)
    t["causal"] = np.where(r[None, :] <= r[:, None], 0.0, NEG)
    c = np.arange(NCP)
    vis = np.stack([(CMP_S * c[None, :] + CMP_T - 1 <= (q * P + r)[:, None]) & (c[None, :] < NC)
                    for q in range(QT)], 1)
    t["cmpvis"] = vis.astype(float).reshape(P, P)
    t["cmpneg"] = np.where(vis, 0.0, NEG).reshape(P, P)
    rp = np.zeros((P, P))
    for b in range(0, P, HD):
        for i in range(8):
            rp[b + i + 8, b + i] = -1.0
            rp[b + i, b + i + 8] = 1.0
    t["rope_perm"] = rp
    ap = np.zeros((P, P))
    for b in range(0, P, 32):
        for i in range(16):
            ap[b + i + 16, b + i] = -1.0
            ap[b + i, b + i + 16] = 1.0
    t["axial_perm"] = ap
    same = (r[:, None] // CH) == (r[None, :] // CH)
    t["gla_f"] = (same & (r[:, None] <= r[None, :])).astype(float)
    t["gla_b"] = (same & (r[:, None] >= r[None, :])).astype(float)
    return np.concatenate([t[n] for n in CONSTS], 1).astype(np.float32)


def axial_table():
    f = np.float32
    inv = (f(10000.0) ** (-np.arange(0, 32, 2, dtype=f) / f(32))).astype(f)
    tok = np.arange(SEQ)
    row, col = (tok // 64).astype(f), (tok % 64).astype(f)
    ang = np.concatenate([row[None] * inv[:, None]] * 2 + [col[None] * inv[:, None]] * 2, 0)
    ang = np.concatenate([ang, ang], 0)
    return np.stack([np.cos(ang), np.sin(ang)], 1).astype(f)


def inv_freq_column():
    inv = np.power(np.float32(500000.0), np.arange(8, dtype=np.float32) * np.float32(-2.0 / 16)).astype(np.float32)
    r = np.arange(P) % HD
    return np.where(r < 16, inv[r % 8], 0).astype(np.float32).reshape(P, 1)


class Bag:
    pass



def load_unit(sp, k, n, src, width=UNIT, it=0, per=0):
    if n >= 2:
        sp.wait_ge(k.w_hi, n - 1 + per * it)
        sp.wait_ge(k.w_lo, n - 1 + per * it)
    sp.dma_start(k.raw[:, n % 2, 0:width], src).then_inc(k.w_loaded[n % 2], 16)


def split_hi(act, k, n, used=None, width=UNIT, it=0, per=0):
    act.wait_ge(k.w_loaded[n % 2], 16 * (n // 2 + 1) + 8 * per * it)
    if used is not None:
        act.wait_ge(*used)
    act.activation(k.whi[:, n % 2, 0:width], k.raw[:, n % 2, 0:width], ACT.Copy).then_inc(k.w_hi, 1)


def split_lo(dve, k, n, width=UNIT, it=0, per=0):
    dve.wait_ge(k.w_hi, n + 1 + per * it)
    dve.tensor_tensor(k.wlo[:, n % 2, 0:width], k.raw[:, n % 2, 0:width],
                      k.whi[:, n % 2, 0:width].bitcast(F32), ALU.subtract).then_inc(k.w_lo, 1)


def unit_ready(pe, k, n, it=0, per=0):
    pe.wait_ge(k.w_lo, n + 1 + per * it)


def mm3(pe, outs, whi, wlo, xs, start, stop):
    for c, (out, (xhi, xlo)) in enumerate(zip(outs, xs)):
        pe.matmul(out, whi, xhi, start=start, stop=False)
        pe.matmul(out, whi, xlo, start=False, stop=False)
    for out, (xhi, xlo) in zip(outs, xs):
        last = pe.matmul(out, wlo, xhi, start=False, stop=stop)
    return last


def chunks(t):
    return [(0, 512)] if t == 512 else [(0, 512), (512, 256)]


def tile_out(k, slot, tok):
    base = slot * 512 * len(chunks(tok))
    return base, [k.ps[:, base + c0:base + c0 + w] for c0, w in chunks(tok)]


def dense_tile(pe, k, outs, w_tiles, x_hi, x_lo, tok, x_wait=None):
    for i, (whi, wlo) in enumerate(w_tiles):
        if x_wait is not None:
            x_wait(i)
        xs = [(x_hi[:, i, c0:c0 + w], x_lo[:, i, c0:c0 + w]) for c0, w in chunks(tok)]
        last = mm3(pe, outs, whi, wlo, xs, i == 0, i == len(w_tiles) - 1)
    return last


def unit_tiles(k, n, off, kt, cols, m):
    out = []
    for i in range(kt):
        a = off + i * cols + m * P
        out.append((k.whi[:, n % 2, a:a + P], k.wlo[:, n % 2, a:a + P]))
    return out



class Norm:

    def __init__(self, k, name, src, kt, tok, bank, it=0, sems=None):
        self.k, self.src, self.kt, self.tok, self.bank, self.it = k, src, kt, tok, bank, it
        self.nt = tok // P
        self.name = name
        self.squared, self.added, self.summed, self.mean, self.root, self.inverse, self.diag, self.spread = sems or [
            k.sem(f"{name}_{s}") for s in ("squared", "added", "summed", "mean", "root", "inverse", "diag", "spread")]
        self.stat = k.ps[:, bank * 512:bank * 512 + self.nt]
        self.rb = k.ps[:, (bank + 1) * 512:(bank + 1) * 512 + tok]

    def at(self, it):
        return Norm(self.k, self.name, self.src, self.kt, self.tok, self.bank, it,
                    [self.squared, self.added, self.summed, self.mean, self.root, self.inverse, self.diag, self.spread])

    def act_squares(self, act, before=None):
        k, tok = self.k, self.tok
        for t in range(self.kt):
            if before is not None:
                before(act, t)
            dst = k.acc[:, 0:tok] if t == 0 else k.sqt[:, t % 2, 0:tok]
            if t >= 3:
                act.wait_ge(self.added, t - 2 + (self.kt - 1) * self.it)
            act.activation(dst, self.src[:, t, 0:tok], ACT.Square).then_inc(self.squared, 1)

    def dve_sum(self, dve):
        k, tok = self.k, self.tok
        for t in range(1, self.kt):
            dve.wait_ge(self.squared, t + 1 + self.kt * self.it)
            if t >= 2:
                dve.wait_ge(self.added, t - 1 + (self.kt - 1) * self.it)
            dve.tensor_tensor(k.acc[:, 0:tok], k.acc[:, 0:tok], k.sqt[:, t % 2, 0:tok],
                              ALU.add).then_inc(self.added, 1)

    def pe_sum(self, pe):
        k = self.k
        pe.wait_ge(self.added, (self.kt - 1) * (self.it + 1))
        for j in range(self.nt):
            last = pe.matmul(self.stat[:, j:j + 1], k.acc[:, j * P:(j + 1) * P], k.c["ones"][:, 0:1],
                             start=True, stop=True)
        last.then_inc(self.summed, 1)

    def dve_mean(self, dve):
        dve.wait_ge(self.summed, 1 + self.it)
        dve.tensor_scalar(self.k.nst[:, 0, 0:self.nt], self.stat, 1.0 / (self.kt * P), EPS,
                          ALU.mult, ALU.add).then_inc(self.mean, 1)

    def act_root(self, act):
        act.wait_ge(self.mean, 1 + self.it)
        act.activation(self.k.nst[:, 1, 0:self.nt], self.k.nst[:, 0, 0:self.nt],
                       ACT.Sqrt).then_inc(self.root, 1)

    def dve_diag(self, dve):
        k = self.k
        dve.wait_ge(self.root, 1 + self.it)
        dve.reciprocal(k.nst[:, 2, 0:self.nt], k.nst[:, 1, 0:self.nt]).then_inc(self.inverse, 1)
        dve.wait_ge(self.inverse, 1 + self.it)
        for j in range(self.nt):
            dve.tensor_scalar(k.diag[:, j * P:(j + 1) * P], k.c["ident"], k.nst[:, 2, j:j + 1], None,
                              ALU.mult).then_inc(self.diag, 1)

    def pe_spread(self, pe):
        k = self.k
        for j in range(self.nt):
            pe.wait_ge(self.diag, j + 1 + self.nt * self.it)
            last = pe.matmul(self.rb[:, j * P:(j + 1) * P], k.c["ones"], k.diag[:, j * P:(j + 1) * P],
                             start=True, stop=True)
        last.then_inc(self.spread, 1)

    def dve_all(self, dve):
        self.dve_sum(dve)
        self.dve_mean(dve)
        self.dve_diag(dve)

    def pe_all(self, pe):
        self.pe_sum(pe)
        self.pe_spread(pe)


class Normed:

    def __init__(self, k, name, norm, hi, lo, parts):
        self.k, self.norm, self.hi, self.lo, self.parts = k, norm, hi, lo, parts
        self.scaled, self.hi_done, self.lo_done = [k.sem(f"{name}_{s}") for s in ("scaled", "hi_done", "lo_done")]

    def dve(self, dve):
        k, n = self.k, self.norm
        kt, it = n.kt, n.it
        np_ = len(self.parts)
        dve.wait_ge(n.spread, 1 + it)

        def lo(t):
            dve.wait_ge(self.hi_done, np_ * (t + 1 + kt * it))
            for c0, w, scale, shift in self.parts:
                src = k.sqt[:, t % 2, c0:c0 + w]
                hi = self.hi[:, t, c0:c0 + w].bitcast(F32)
                dst = self.lo[:, t, c0:c0 + w]
                if shift is None:
                    dve.tensor_tensor(dst, src, hi, ALU.subtract).then_inc(self.lo_done, 1)
                else:
                    dve.scalar_tensor_tensor(dst, src, shift[:, t:t + 1], hi, ALU.add,
                                             ALU.subtract).then_inc(self.lo_done, 1)

        for t in range(kt):
            if t >= 2:
                dve.wait_ge(self.lo_done, np_ * (t - 1 + kt * it))
            for c0, w, scale, shift in self.parts:
                dve.scalar_tensor_tensor(k.sqt[:, t % 2, c0:c0 + w], n.src[:, t, c0:c0 + w],
                                         scale[:, t:t + 1], n.rb[:, c0:c0 + w], ALU.mult,
                                         ALU.mult).then_inc(self.scaled, 1)
            if t >= 1:
                lo(t - 1)
        lo(kt - 1)

    def act(self, act):
        k, n = self.k, self.norm
        np_ = len(self.parts)
        for t in range(n.kt):
            act.wait_ge(self.scaled, np_ * (t + 1 + n.kt * n.it))
            for c0, w, scale, shift in self.parts:
                act.activation(self.hi[:, t, c0:c0 + w], k.sqt[:, t % 2, c0:c0 + w], ACT.Identity,
                               bias=0.0 if shift is None else shift[:, t:t + 1]).then_inc(self.hi_done, 1)

    def pe_wait(self, pe, t):
        pe.wait_ge(self.lo_done, len(self.parts) * (t + 1 + self.norm.kt * self.norm.it))


class Residual:

    def __init__(self, k, name, norm, x, parts):
        self.k, self.norm, self.x, self.parts = k, norm, x, parts
        self.scaled, self.updated = k.sem(f"{name}_scaled"), k.sem(f"{name}_updated")

    def dve(self, dve):
        k, n = self.k, self.norm
        dve.wait_ge(n.spread, 1)
        for t in range(n.kt):
            if t >= 2:
                dve.wait_ge(self.updated, t - 1)
            for c0, w, scale in self.parts:
                dve.scalar_tensor_tensor(k.sqt[:, t % 2, c0:c0 + w], n.src[:, t, c0:c0 + w],
                                         scale[:, t:t + 1], n.rb[:, c0:c0 + w], ALU.mult,
                                         ALU.mult).then_inc(self.scaled, 1)

    def pool(self, pool):
        k, n = self.k, self.norm
        for t in range(n.kt):
            pool.wait_ge(self.scaled, len(self.parts) * (t + 1))
            pool.tensor_tensor(self.x[:, t, 0:n.tok], self.x[:, t, 0:n.tok], k.sqt[:, t % 2, 0:n.tok],
                               ALU.add).then_inc(self.updated, 1)



def stage_qkv(nc, k, b, stream, first_unit):
    norm = Norm(k, "n1", k.x, KT, SEQ, 5)
    normed = Normed(k, "h1", norm, k.hhi, k.hlo, [(0, SEQ, b.g[:, 0, :], None)])
    ready, taken = k.sem("qkv_ready"), k.sem("qkv_taken")
    ring, tiles = 4, 2 * UNITS_QKV - 4 + 2 * QT
    n0 = first_unit

    with nc.Block() as block:
        @block.sync
        def _(sp):
            for n in range(n0, n0 + UNITS_QKV + 2):
                load_unit(sp, k, n, stream(n))

        @block.tensor
        def _(pe):
            norm.pe_all(pe)
            j = 0
            for u in range(UNITS_QKV):
                n = n0 + u
                unit_ready(pe, k, n)
                if u < UNITS_QKV - 2:
                    for m in range(2):
                        if j >= ring:
                            pe.wait_ge(taken, j - ring + 1)
                        _, outs = tile_out(k, j % ring, SEQ)
                        last = dense_tile(pe, k, outs, unit_tiles(k, n, 0, KT, 256, m), k.hhi, k.hlo, SEQ,
                                          (lambda i: normed.pe_wait(pe, i)) if j == 0 else None)
                        last.then_inc(ready, 1)
                        j += 1
                else:
                    for t in range(QT):
                        pe.wait_ge(taken, j - ring + 1)
                        out = k.ps[:, (j % ring) * 512:(j % ring) * 512 + 256]
                        for i in range(KT):
                            w = (k.whi[:, n % 2, i * 256:(i + 1) * 256], k.wlo[:, n % 2, i * 256:(i + 1) * 256])
                            last = mm3(pe, [out], k.hhi[:, i, t * P:(t + 1) * P], k.hlo[:, i, t * P:(t + 1) * P],
                                       [w], i == 0, i == KT - 1)
                        last.then_inc(ready, 1)
                        j += 1

        @block.vector
        def _(dve):
            norm.dve_all(dve)
            split_lo(dve, k, n0)
            normed.dve(dve)
            split_lo(dve, k, n0 + 1)
            for u in range(2, UNITS_QKV):
                split_lo(dve, k, n0 + u)

        @block.scalar
        def _(act):
            norm.act_squares(act)
            norm.act_root(act)
            split_hi(act, k, n0)
            normed.act(act)
            split_hi(act, k, n0 + 1)
            j = 0

            def out(pairs, scale=1.0):
                nonlocal j
                act.wait_ge(ready, j + 1)
                for i, (dst, rows, cols) in enumerate(pairs):
                    last = act.activation(dst, k.ps[rows, (j % ring) * 512 + cols.start:(j % ring) * 512 + cols.stop],
                                          ACT.Copy, scale=scale)
                last.then_inc(taken, 1)
                j += 1

            every, lower, upper, full = slice(0, P), slice(0, 64), slice(64, P), slice(0, SEQ)
            for u in range(UNITS_QKV):
                for m in range(2 if u < 8 else QT):
                    if u < 2:
                        out([(b.q[:, 2 * u + m, :], every, full)])
                    elif u == 2 and m == 0:
                        out([(b.kv_cmp[0:64, 0, :], lower, full), (b.kv_cmp[64:P, 0, 0:SEQ - 1], lower, slice(1, SEQ)),
                             (b.kv_cmp[0:64, 1, :], upper, full), (b.kv_cmp[64:P, 1, 0:SEQ - 1], upper, slice(1, SEQ))])
                    elif u == 2:
                        out([(b.kk[0:64, 0, :], lower, full), (b.kk[64:P, 0, :], lower, full), (b.vv[0:64, :], upper, full)])
                    elif u == 3 and m == 0:
                        out([(b.kk[0:64, 1, :], lower, full), (b.kk[64:P, 1, :], lower, full), (b.vv[64:P, :], upper, full)])
                    elif u == 3:
                        out([(b.gate_t[0:24, :], slice(0, 24), full)])
                    elif u < 6:
                        out([(b.sbq[:, 2 * (u - 4) + m, :], every, full)], scale=float(np.float32(128.0 ** -0.5)))
                    elif u < 8:
                        out([(b.sbk[:, 2 * (u - 6) + m, :], every, full)])
                    else:
                        out([(b.sbv[:, m, 256 * (u - 8):256 * (u - 7)], every, slice(0, 256))])
                if u + 2 < UNITS_QKV:
                    split_hi(act, k, n0 + u + 2, (ready, j))
    assert tiles == 24
    return n0 + UNITS_QKV


def stage_rope(nc, k, b):
    turned, half1, half2, rotated = k.sem("rope_turned"), k.sem("rope_cos"), k.sem("rope_sin"), k.sem("rope_done")
    gated, flipped = k.sem("gate_sigmoid"), k.sem("value_flipped")
    srcs = [b.q[:, i, :] for i in range(4)] + [b.kk[:, i, :] for i in range(2)]
    dsts = [b.qr[:, i, :] for i in range(4)] + [b.kr[:, i, :] for i in range(2)]
    with nc.Block() as block:
        @block.tensor
        def _(pe):
            for i, src in enumerate(srcs):
                pe.matmul(k.ps[:, i * 512:(i + 1) * 512], k.c["rope_perm"], src, start=True, stop=True).then_inc(turned, 1)
            for t in range(QT):
                pe.transpose(k.ps[:, 3072 + t * P:3072 + (t + 1) * P], b.vv[:, t * P:(t + 1) * P], k.c["ident"]).then_inc(flipped, 1)
            pe.wait_ge(gated, 1)
            for t in range(QT):
                pe.transpose(k.ps[:, 3584 + t * 24:3584 + (t + 1) * 24], b.gate_t[0:24, t * P:(t + 1) * P],
                             k.c["ident"][0:24, 0:24]).then_inc(flipped, 1)

        @block.gpsimd
        def _(pool):
            for i, src in enumerate(srcs):
                if i >= 2:
                    pool.wait_ge(rotated, i - 1)
                pool.tensor_tensor(k.sqt[:, i % 2, 0:SEQ], src, b.cos, ALU.mult).then_inc(half1, 1)

        @block.vector
        def _(dve):
            for i, dst in enumerate(dsts):
                dve.wait_ge(turned, i + 1)
                if i:
                    dve.wait_ge(rotated, i)
                dve.tensor_tensor(k.acc[:, 0:SEQ], k.ps[:, i * 512:(i + 1) * 512], b.sin, ALU.mult).then_inc(half2, 1)
                dve.wait_ge(half2, i + 1)
                dve.wait_ge(half1, i + 1)
                dve.tensor_tensor(dst, k.acc[:, 0:SEQ], k.sqt[:, i % 2, 0:SEQ], ALU.add).then_inc(rotated, 1)

        @block.scalar
        def _(act):
            act.activation(b.gate_t[0:24, :], b.gate_t[0:24, :], ACT.Sigmoid).then_inc(gated, 1)
            act.wait_ge(flipped, QT)
            act.activation(b.v[:, :, :].rearrange("p a b -> p (a b)"), k.ps[:, 3072:3584], ACT.Copy)
            act.wait_ge(flipped, 2 * QT)
            act.activation(b.gate[:, :, :].rearrange("p a b -> p (a b)"), k.ps[:, 3584:3584 + 96], ACT.Copy)


def stage_compress(nc, k, b, stream, n0):
    added, made_hi, made_lo, zeroed = k.sem("cmp_pe_added"), k.sem("cmp_hi"), k.sem("cmp_lo"), k.sem("cmp_zeroed")
    hidden, gelu, outs_ready = k.sem("cmp_hidden"), k.sem("cmp_gelu"), k.sem("cmp_out")
    small = k.sem("cmp_small")
    half = CMP_T // 4
    with nc.Block() as block:
        @block.sync
        def _(sp):
            for c in range(2):
                for r in range(2 if c == 0 else 1):
                    sp.dma_start(b.w2[:, c, :, 64 * r:64 * r + 64],
                                 b.w2_src[c].rearrange("(h p) n -> p h n", p=P)).then_inc(small, 16)
                sp.dma_start(b.pe[:, c, :], b.pe_src[c]).then_inc(small, 16)
            for n in range(n0 + 2, n0 + UNITS_CMP + 2):
                load_unit(sp, k, n, stream(n))

        @block.vector
        def _(dve):
            dve.memset(b.blk[:, :, :, NC:NCP], 0.0).then_inc(zeroed, 1)
            split_lo(dve, k, n0)
            split_lo(dve, k, n0 + 1)
            dve.wait_ge(small, 80)
            for c in range(2):
                view = b.kv_cmp[:, c, :].rearrange("p (c r) -> p r c", r=CMP_S)
                for h in range(2):
                    dve.tensor_tensor(b.blk[:, c, h * half:(h + 1) * half, 0:NC],
                                      view[:, 0:CMP_S:2, h:h + NC],
                                      b.pe[:, c, h * half:(h + 1) * half].unsqueeze(2).to_broadcast([P, half, NC]),
                                      ALU.add).then_inc(added, 1)
            for c in range(2):
                dve.wait_ge(made_hi, c + 1)
                dve.tensor_tensor(b.blk_lo[:, c], b.blk[:, c], b.blk_hi[:, c].bitcast(F32),
                                  ALU.subtract).then_inc(made_lo, 1)
            for n in range(n0 + 2, n0 + UNITS_CMP):
                split_lo(dve, k, n)

        @block.scalar
        def _(act):
            split_hi(act, k, n0)
            split_hi(act, k, n0 + 1)
            act.wait_ge(zeroed, 1)
            for c in range(2):
                act.wait_ge(added, 2 * c + 2)
                act.activation(b.blk_hi[:, c], b.blk[:, c], ACT.Copy).then_inc(made_hi, 1)
            split_hi(act, k, n0 + 2, (hidden, 1))
            split_hi(act, k, n0 + 3, (hidden, 2))
            for c in range(2):
                act.wait_ge(hidden, 2 * c + 2)
                for h in range(2):
                    a = (2 * c + h) * 512
                    act.activation(b.hid[:, c, h, :], k.ps[:, a:a + NCP], ACT.Gelu_apprx_tanh).then_inc(gelu, 1)
            act.wait_ge(outs_ready, 1)
            act.activation(b.kc[:, 0:NC], k.ps[:, 2048:2048 + NC], ACT.Copy)
            act.wait_ge(outs_ready, 2)
            act.activation(b.vc[0:NC, :], k.ps[0:NC, 2560:2560 + 64], ACT.Copy)

        @block.tensor
        def _(pe):
            for c in range(2):
                pe.wait_ge(made_lo, c + 1)
                for u in range(2):
                    n = n0 + 2 * c + u
                    unit_ready(pe, k, n)
                    for i in range(8):
                        for h in range(2):
                            a = (2 * c + h) * 512
                            w = i * 256 + h * P
                            last = mm3(pe, [k.ps[:, a:a + NCP]], k.whi[:, n % 2, w:w + P], k.wlo[:, n % 2, w:w + P],
                                       [(b.blk_hi[:, c, 8 * u + i, :], b.blk_lo[:, c, 8 * u + i, :])],
                                       u == 0 and i == 0, u == 1 and i == 7)
                    last.then_inc(hidden, 1)
            pe.wait_ge(small, 80)
            pe.wait_ge(gelu, 2)
            for h in range(2):
                last = pe.matmul(k.ps[:, 2048:2048 + NC], b.w2[:, 0, h, :], b.hid[:, 0, h, 0:NC], start=h == 0, stop=h == 1)
            last.then_inc(outs_ready, 1)
            pe.wait_ge(gelu, 4)
            for h in range(2):
                last = pe.matmul(k.ps[0:NC, 2560:2560 + 64], b.hid[:, 1, h, 0:NC], b.w2[:, 1, h, 0:64], start=h == 0, stop=h == 1)
            last.then_inc(outs_ready, 1)
    return n0 + UNITS_CMP


def stage_cmp_attention(nc, k, b):
    scored, masked, expd, probs, flipped, copied, chain = (
        k.sem(f"ca_{s}") for s in ("scored", "masked", "exp", "probs", "flipped", "copied", "chain"))
    with nc.Block() as block:
        @block.tensor
        def _(pe):
            for t in range(QT):
                for h in range(HEADS):
                    r = slice(64 * (h % 2), 64 * (h % 2) + 64)
                    a = t * 512 + 2048 * (h % 2) + h // 2 * NCP
                    last = pe.matmul(k.ps[:, a:a + NC], b.q[r, h // 2, t * P:(t + 1) * P], b.kc[r, 0:NC],
                                     start=True, stop=True)
                last.then_inc(scored, 1)
            for h in range(HEADS):
                if h == 0:
                    pe.wait_ge(probs, QT)
                if h >= 4:
                    pe.wait_ge(copied, h - 3)
                for t in range(QT):
                    a = 2048 + (h % 4) * 512 + t * P
                    last = pe.transpose(k.ps[0:NC, a:a + P], b.pc[:, t, h, 0:NC], k.c["ident"])
                last.then_inc(flipped, 1)

        @block.vector
        def _(dve):
            n = 0

            def link(ins):
                nonlocal n
                n += 1
                ins.then_inc(chain, 1)
                dve.wait_ge(chain, n)

            for t in range(QT):
                s = b.pc[:, t, :, 0:NC]
                neg = k.c["cmpneg"][:, t * NCP:t * NCP + NC].unsqueeze(1).to_broadcast([P, HEADS // 2, NC])
                vis = k.c["cmpvis"][:, t * NCP:t * NCP + NC].unsqueeze(1).to_broadcast([P, HEADS, NC])
                dve.wait_ge(scored, t + 1)
                for odd in range(2):
                    a = t * 512 + 2048 * odd
                    ps = k.ps[:, a:a + HEADS // 2 * NCP].rearrange("p (h c) -> p h c", c=NCP)[:, :, 0:NC]
                    ins = dve.tensor_tensor(b.pc[:, t, odd:HEADS:2, 0:NC], ps, neg, ALU.add)
                    link(ins)
                link(dve.tensor_reduce(b.cst[:, 0, :], s, AX_X, ALU.max))
                dve.tensor_tensor(s, s, b.cst[:, 0, :].unsqueeze(2).to_broadcast([P, HEADS, NC]),
                                  ALU.subtract).then_inc(masked, 1)
                dve.wait_ge(expd, t + 1)
                link(dve.tensor_reduce(b.cst[:, 1, :], s, AX_X, ALU.add))
                link(dve.reciprocal(b.cst[:, 2, :], b.cst[:, 1, :]))
                gate = b.gate[:, t, :].rearrange("p (h c) -> p h c", c=3)[:, :, 0]
                link(dve.tensor_tensor(b.cst[:, 3, :], b.cst[:, 2, :], gate, ALU.mult))
                link(dve.tensor_tensor(s, s, b.cst[:, 3, :].unsqueeze(2).to_broadcast([P, HEADS, NC]), ALU.mult))
                dve.tensor_tensor(s, s, vis, ALU.mult).then_inc(probs, 1)

        @block.scalar
        def _(act):
            for t in range(QT):
                act.wait_ge(masked, t + 1)
                s = b.pc[:, t, :, 0:NC]
                act.activation(s, s, ACT.Exp, scale=HD ** -0.5).then_inc(expd, 1)
            for h in range(HEADS):
                act.wait_ge(flipped, h + 1)
                a = 2048 + (h % 4) * 512
                act.activation(b.pct[0:NC, h, :], k.ps[0:NC, a:a + 512], ACT.Copy).then_inc(copied, 1)


def stage_causal_attention(nc, k, b):
    names = ("staged", "scored", "maxed", "expd", "scaled", "flipped", "copied_a", "copied_v", "summed", "hi_done",
             "lo_done", "chain")
    s = {n: k.sem(f"sa_{n}") for n in names}
    U = 2 * QT
    LINKS = 4 * U
    vcols = lambda br: slice(64 * br, 64 * br + 64)
    with nc.Block() as block:
        @block.tensor
        def _(pe):
            with pe.Fori(0, HEADS // 2) as it:
                def scores(u):
                    h, t = u // QT, u % QT
                    w = (t + 1) * P
                    r = slice(64 * h, 64 * h + 64)
                    if u == 0:
                        pe.wait_ge(s["staged"], 2 * it + 1)
                    pe.wait_ge(s["expd"], U * it + max(u - 1, 0))
                    for br in range(2):
                        a = (u % 2) * 1024 + br * 512
                        last = pe.matmul(k.ps[:, a:a + w], b.qst[r, t * P:(t + 1) * P], b.kr[r, br, 0:w],
                                         start=True, stop=True)
                    last.then_inc(s["scored"], 1)

                def flips(u):
                    t = u % QT
                    pe.wait_ge(s["scaled"], U * it + u + 1)
                    pe.wait_ge(s["copied_a"], U * it + u)
                    pe.wait_ge(s["copied_v"], U * it + u)
                    for br in range(2):
                        for j in range(t + 1):
                            a = 2048 + br * 512 + j * P
                            last = pe.transpose(k.ps[:, a:a + P], b.p[:, u % 2, br, j * P:(j + 1) * P], k.c["ident"])
                    last.then_inc(s["flipped"], 1)

                def values(u):
                    h, t = u // QT, u % QT
                    rows = slice(64 * h, 64 * h + 64)
                    out = k.ps[rows, 3072 + t * P:3072 + (t + 1) * P]
                    if u == 0:
                        pe.wait_ge(s["lo_done"], it)
                        pe.wait_ge(s["staged"], 2 * it + 2)
                    pe.matmul(out, b.vc[0:NC, :], b.pcst[:, h, t * P:(t + 1) * P], start=True, stop=False)
                    pe.wait_ge(s["copied_a"], U * it + u + 1)
                    pe.wait_ge(s["copied_v"], U * it + u + 1)
                    for br in range(2):
                        for j in range(t + 1):
                            last = pe.matmul(out, b.v[:, j, vcols(br)], b.pt[:, u % 2, br, j * P:(j + 1) * P],
                                             start=False, stop=br == 1 and j == t)
                    last.then_inc(s["summed"], 1)

                scores(0)
                scores(1)
                flips(0)
                for u in range(U):
                    if u + 2 < U:
                        scores(u + 2)
                    if u + 1 < U:
                        flips(u + 1)
                    values(u)

        @block.vector
        def _(dve):
            with dve.Fori(0, HEADS // 2) as it:
                n = 0

                def link(ins):
                    nonlocal n
                    n += 1
                    ins.then_inc(s["chain"], 1)
                    dve.wait_ge(s["chain"], LINKS * it + n)

                def top(u):
                    t = u % QT
                    w = (t + 1) * P
                    dve.wait_ge(s["scored"], U * it + u + 1)
                    a = (u % 2) * 1024
                    both = k.ps[:, a:a + 1024].rearrange("p (b w) -> p b w", b=2)
                    diag = both[:, :, t * P:w]
                    link(dve.tensor_tensor(diag, diag, k.c["causal"].unsqueeze(1).to_broadcast([P, 2, P]), ALU.add))
                    link(dve.tensor_reduce(b.sst[:, u % 2, 0, :], both[:, :, 0:w], AX_X, ALU.max))
                    dve.tensor_scalar(b.sst[:, u % 2, 1, :], b.sst[:, u % 2, 0, :], -(HD ** -0.5), None,
                                      ALU.mult).then_inc(s["maxed"], 1)

                def scale(u):
                    h, t = u // QT, u % QT
                    w = (t + 1) * P
                    dve.wait_ge(s["expd"], U * it + u + 1)
                    link(dve.reciprocal(b.sst[:, u % 2, 3, :], b.sst[:, u % 2, 2, :]))
                    gate = b.gate[:, t, bass.ds(6 * it + 3 * h + 1, 2)]
                    link(dve.tensor_tensor(b.sst[:, u % 2, 4, :], b.sst[:, u % 2, 3, :], gate, ALU.mult))
                    for br in range(2):
                        last = dve.tensor_scalar(b.p[:, u % 2, br, 0:w], b.p[:, u % 2, br, 0:w],
                                                 b.sst[:, u % 2, 4, br:br + 1], None, ALU.mult)
                    last.then_inc(s["scaled"], 1)

                def copy(u):
                    w = (u % QT + 1) * P
                    dve.wait_ge(s["flipped"], U * it + u + 1)
                    if u >= 2:
                        dve.wait_ge(s["summed"], U * it + u - 1)
                    dve.tensor_copy(b.pt[:, u % 2, 1, 0:w], k.ps[:, 2560:2560 + w]).then_inc(s["copied_v"], 1)

                top(0)
                top(1)
                scale(0)
                for u in range(U):
                    copy(u)
                    if u + 2 < U:
                        top(u + 2)
                    if u + 1 < U:
                        scale(u + 1)
                dve.wait_ge(s["hi_done"], it + 1)
                dve.tensor_tensor(b.onlo[:, it, :], k.ps[:, 3072:3584], b.onhi[:, it, :].bitcast(F32),
                                  ALU.subtract).then_inc(s["lo_done"], 1)
                assert n == LINKS

        @block.scalar
        def _(act):
            with act.Fori(0, HEADS // 2) as it:
                def exps(u):
                    w = (u % QT + 1) * P
                    act.wait_ge(s["maxed"], U * it + u + 1)
                    if u >= 2:
                        act.wait_ge(s["flipped"], U * it + u - 1)
                    for br in range(2):
                        a = (u % 2) * 1024 + br * 512
                        last = act.activation(b.p[:, u % 2, br, 0:w], k.ps[:, a:a + w], ACT.Exp,
                                              bias=b.sst[:, u % 2, 1, br:br + 1], scale=HD ** -0.5,
                                              accum_out=b.sst[:, u % 2, 2, br:br + 1])
                    last.then_inc(s["expd"], 1)

                def copy(u):
                    w = (u % QT + 1) * P
                    act.wait_ge(s["flipped"], U * it + u + 1)
                    if u >= 2:
                        act.wait_ge(s["summed"], U * it + u - 1)
                    act.activation(b.pt[:, u % 2, 0, 0:w], k.ps[:, 2048:2048 + w], ACT.Copy).then_inc(s["copied_a"], 1)

                act.wait_ge(s["scored"], U * it)
                act.activation(b.qst, b.qr[:, it, :], ACT.Copy).then_inc(s["staged"], 1)
                act.wait_ge(s["summed"], U * it)
                act.activation(b.pcst, b.pct[0:NC, bass.ds(2 * it, 2), :], ACT.Copy).then_inc(s["staged"], 1)
                exps(0)
                exps(1)
                for u in range(U):
                    copy(u)
                    if u + 2 < U:
                        exps(u + 2)
                act.wait_ge(s["summed"], U * (it + 1))
                act.activation(b.onhi[:, it, :], k.ps[:, 3072:3584], ACT.Copy).then_inc(s["hi_done"], 1)


def stage_stick_breaking(nc, k, b):
    names = ("zeroed", "staged", "scored", "absd", "expd", "logd", "soft", "totals", "weighed", "weights", "summed", "hi_done",
             "lo_done", "chain")
    s = {n: k.sem(f"sb_{n}") for n in names}
    order = list(range(QT))[::-1]
    TOTALS = QT - 1
    LINKS = QT
    with nc.Block() as block:
        @block.gpsimd
        def _(pool):
            pool.memset(b.tot, 0.0).then_inc(s["zeroed"], 1)
            pool.wait_ge(s["zeroed"], 1)
            with pool.Fori(0, SBH) as it:
                for i, j in enumerate(order[:-1]):
                    pool.wait_ge(s["soft"], QT * it + i + 1)
                    if i:
                        pool.wait_ge(s["totals"], TOTALS * it + i)
                    pool.tensor_tensor(b.tot[:, j, j * P:SEQ], b.sp[:, j, j * P:SEQ], b.tot[:, j + 1, j * P:SEQ],
                                       ALU.add).then_inc(s["totals"], 1)

        @block.tensor
        def _(pe):
            with pe.Fori(0, SBH) as it:
                pe.wait_ge(s["staged"], 2 * it + 2)
                for j in order:
                    pe.matmul(k.ps[:, j * 512:j * 512 + SEQ - j * P], b.kst[:, j * P:(j + 1) * P],
                              b.sbq[:, it, j * P:SEQ], start=True, stop=True).then_inc(s["scored"], 1)
                for i, j in enumerate(order):
                    w = SEQ - j * P
                    pe.wait_ge(s["soft"], QT * it + i + 1)
                    pe.matmul(k.ps[:, j * 512:j * 512 + w], k.c["negtri"], b.sp[:, j, j * P:SEQ],
                              start=False, stop=False, skip_group_check=True)
                    last = pe.matmul(k.ps[:, j * 512:j * 512 + P], k.c["ident"], k.c["sbneg"],
                                     start=False, stop=True, skip_group_check=True)
                    if i:
                        pe.wait_ge(s["totals"], TOTALS * it + i)
                        last = pe.matmul(k.ps[:, j * 512 + P:j * 512 + w], k.c["negones"], b.tot[:, j + 1, (j + 1) * P:SEQ],
                                         start=False, stop=True, skip_group_check=True)
                    last.then_inc(s["weighed"], 1)
                pe.wait_ge(s["weights"], QT * (it + 1))
                pe.wait_ge(s["lo_done"], it)
                for j in range(QT):
                    last = pe.matmul(k.ps[:, 2048 + j * P:2560], b.vst[:, j, :], b.a[:, j, j * P:SEQ],
                                     start=j == 0, stop=j == QT - 1)
                last.then_inc(s["summed"], 1)

        @block.vector
        def _(dve):
            with dve.Fori(0, SBH) as it:
                n = 0

                def link(ins):
                    nonlocal n
                    n += 1
                    ins.then_inc(s["chain"], 1)
                    dve.wait_ge(s["chain"], LINKS * it + n)

                for i, j in enumerate(order):
                    dve.wait_ge(s["logd"], QT * it + i + 1)
                    sp = b.sp[:, j, j * P:SEQ]
                    link(dve.scalar_tensor_tensor(sp, k.ps[:, j * 512:j * 512 + SEQ - j * P], 0.0, sp, ALU.max, ALU.add))
                    ins = dve.tensor_tensor(b.sp[:, j, j * P:(j + 1) * P], b.sp[:, j, j * P:(j + 1) * P], k.c["sb01"], ALU.mult)
                    ins.then_inc(s["soft"], 1)
                dve.wait_ge(s["hi_done"], it + 1)
                dve.tensor_tensor(b.oslo[:, it, :], k.ps[:, 2048:2560], b.oshi[:, it, :].bitcast(F32),
                                  ALU.subtract).then_inc(s["lo_done"], 1)

        @block.scalar
        def _(act):
            with act.Fori(0, SBH) as it:
                act.wait_ge(s["summed"], it)
                act.wait_ge(s["totals"], TOTALS * it)
                act.activation(b.kst, b.sbk[:, it, :], ACT.Copy).then_inc(s["staged"], 1)
                act.activation(b.vst, b.sbv[:, :, bass.ds(it * P, P)], ACT.Copy).then_inc(s["staged"], 1)
                for i, j in enumerate(order):
                    act.wait_ge(s["scored"], QT * it + i + 1)
                    act.activation(b.sp[:, j, j * P:SEQ], k.ps[:, j * 512:j * 512 + SEQ - j * P], ACT.Abs).then_inc(s["absd"], 1)
                for i, j in enumerate(order):
                    sp = b.sp[:, j, j * P:SEQ]
                    act.wait_ge(s["absd"], QT * it + i + 1)
                    act.activation(sp, sp, ACT.Exp, scale=-1.0).then_inc(s["expd"], 1)
                for i, j in enumerate(order):
                    sp = b.sp[:, j, j * P:SEQ]
                    act.wait_ge(s["expd"], QT * it + i + 1)
                    act.activation(sp, sp, ACT.Ln, bias=1.0).then_inc(s["logd"], 1)
                for i, j in enumerate(order):
                    act.wait_ge(s["weighed"], QT * it + i + 1)
                    act.activation(b.a[:, j, j * P:SEQ], k.ps[:, j * 512:j * 512 + SEQ - j * P],
                                   ACT.Exp).then_inc(s["weights"], 1)
                act.wait_ge(s["summed"], it + 1)
                act.activation(b.oshi[:, it, :], k.ps[:, 2048:2560], ACT.Copy).then_inc(s["hi_done"], 1)


def stage_merge(nc, k, b, stream, n0):
    names = ("ready", "taken_a", "taken_v", "gates", "part", "mixed", "hi_done", "lo_done")
    s = {n: k.sem(f"mg_{n}") for n in names}
    TURNS, PAIRS = 2, 2
    per = UNITS_MERGE // TURNS

    with nc.Block() as block:
        @block.sync
        def _(sp):
            with sp.Fori(0, TURNS) as it:
                for u in range(per):
                    load_unit(sp, k, n0 + u + 2, stream(n0 + u + 2 + per * it), it=it, per=per)

        @block.tensor
        def _(pe):
            with pe.Fori(0, TURNS) as it:
                for pr in range(PAIRS):
                    for u in range(3):
                        n = n0 + 3 * pr + u
                        unit_ready(pe, k, n, it, per)
                        for g in range(2 if u == 2 else 1):
                            for m in range(2):
                                slot = 2 * u + 2 * g + m
                                done = PAIRS * it + pr
                                if u < 2:
                                    pe.wait_ge(s["taken_a"], 4 * done)
                                else:
                                    pe.wait_ge(s["taken_v"], 4 * done)
                                _, outs = tile_out(k, slot, SEQ)
                                if u < 2:
                                    w, xh, xl = unit_tiles(k, n, 0, KT, 256, m), k.hhi, k.hlo
                                elif g == 0:
                                    w, xh, xl = unit_tiles(k, n, 0, 4, 256, m), b.onhi, b.onlo
                                else:
                                    w, xh, xl = unit_tiles(k, n, 1024, 4, 256, m), b.oshi, b.oslo
                                last = dense_tile(pe, k, outs, w, xh, xl, SEQ)
                                last.then_inc(s["ready"], 1)

        @block.scalar
        def _(act):
            split_hi(act, k, n0)
            split_hi(act, k, n0 + 1)

            def turn(it, last_turn):
                for pr in range(PAIRS):
                    base = PAIRS * it + pr
                    for u in range(3):
                        if u < 2:
                            for m in range(2):
                                i = 2 * u + m
                                act.wait_ge(s["ready"], 8 * base + i + 1)
                                if i == 0:
                                    act.wait_ge(s["taken_v"], 4 * base)
                                act.activation(b.gt[:, i, :], k.ps[:, i * 512:(i + 1) * 512],
                                               ACT.Sigmoid).then_inc(s["taken_a"], 1)
                        else:
                            for m in range(2):
                                act.wait_ge(s["mixed"], 2 * base + m + 1)
                                act.activation(b.mhi[:, 4 * it + 2 * pr + m, :], b.mt[:, m, :],
                                               ACT.Copy).then_inc(s["hi_done"], 1)
                        if not (last_turn and 3 * pr + u + 2 >= per):
                            split_hi(act, k, n0 + 3 * pr + u + 2, (s["ready"], 8 * base + (2, 4, 8)[u]), it=it, per=per)

            with act.Fori(0, TURNS - 1) as it:
                turn(it, False)
            turn(TURNS - 1, True)

        @block.vector
        def _(dve):
            split_lo(dve, k, n0)
            split_lo(dve, k, n0 + 1)

            def turn(it, last_turn):
                for pr in range(PAIRS):
                    base = PAIRS * it + pr
                    for u in range(3):
                        if u == 2:
                            for m in range(2):
                                dve.wait_ge(s["ready"], 8 * base + 5 + m)
                                dve.wait_ge(s["taken_a"], 4 * base + 4)
                                dve.tensor_tensor(b.gt[:, m, :], k.ps[:, (4 + m) * 512:(5 + m) * 512], b.gt[:, m, :],
                                                  ALU.mult).then_inc(s["taken_v"], 1)
                            for m in range(2):
                                dve.wait_ge(s["ready"], 8 * base + 7 + m)
                                dve.wait_ge(s["taken_v"], 4 * base + 2)
                                dve.tensor_tensor(b.mt[:, m, :], k.ps[:, (6 + m) * 512:(7 + m) * 512], b.gt[:, 2 + m, :],
                                                  ALU.mult).then_inc(s["part"], 1)
                            for m in range(2):
                                dve.wait_ge(s["part"], 2 * base + m + 1)
                                dve.tensor_tensor(b.mt[:, m, :], b.mt[:, m, :], b.gt[:, m, :],
                                                  ALU.add).then_inc(s["mixed"], 1)
                            for m in range(2):
                                dve.wait_ge(s["hi_done"], 2 * base + m + 1)
                                i = 4 * it + 2 * pr + m
                                dve.tensor_tensor(b.mlo[:, i, :], b.mt[:, m, :], b.mhi[:, i, :].bitcast(F32),
                                                  ALU.subtract).then_inc(s["lo_done"], 1)
                            dve.wait_ge(s["lo_done"], 2 * base + 2)
                            dve.sem_inc(s["taken_v"], 2)
                        if not (last_turn and 3 * pr + u + 2 >= per):
                            split_lo(dve, k, n0 + 3 * pr + u + 2, it=it, per=per)

            with dve.Fori(0, TURNS - 1) as it:
                turn(it, False)
            turn(TURNS - 1, True)
    return n0 + UNITS_MERGE


def stage_project(nc, k, name, stream, n0, xhi, xlo, y, tok, last_unit):
    ready, taken = k.sem(f"{name}_ready"), k.sem(f"{name}_taken")
    ring = 4
    with nc.Block() as block:
        @block.sync
        def _(sp):
            for n in range(n0 + 2, min(n0 + 4 + 2, last_unit)):
                load_unit(sp, k, n, stream(n))

        @block.tensor
        def _(pe):
            for j in range(KT):
                if j % 2 == 0:
                    unit_ready(pe, k, n0 + j // 2)
                if j >= ring:
                    pe.wait_ge(taken, j - ring + 1)
                _, outs = tile_out(k, j % ring, tok)
                last = dense_tile(pe, k, outs, unit_tiles(k, n0 + j // 2, 0, KT, 256, j % 2), xhi, xlo, tok)
                last.then_inc(ready, 1)

        @block.vector
        def _(dve):
            for u in range(4):
                split_lo(dve, k, n0 + u)

        @block.scalar
        def _(act):
            split_hi(act, k, n0)
            split_hi(act, k, n0 + 1)
            for j in range(KT):
                act.wait_ge(ready, j + 1)
                base, _ = tile_out(k, j % ring, tok)
                act.activation(y[:, j, 0:tok], k.ps[:, base:base + tok], ACT.Copy).then_inc(taken, 1)
                if j % 2 and j // 2 + 2 < 4:
                    split_hi(act, k, n0 + j // 2 + 2, (ready, j + 1))
    return n0 + 4


def stage_mlp(nc, k, name, stream, n0, y, hid_hi, hid_lo, tok, post, pre, last_unit):
    names = ("ready", "relu", "squared", "hid_hi", "hid_lo", "added")
    s = {n: k.sem(f"{name}_{n}") for n in names}
    n_post = Norm(k, f"{name}_p", y, KT, tok, 5)
    res = Residual(k, f"{name}_r", n_post, k.x, post)
    n_pre = Norm(k, f"{name}_q", k.x, KT, tok, 5)
    normed = Normed(k, f"{name}_h", n_pre, k.hhi, k.hlo, pre)
    ring = 4
    T1, T2 = 4, KT
    last_u = n0 + UNITS_FF

    with nc.Block() as block:
        @block.sync
        def _(sp):
            with sp.Fori(0, FF_GROUPS - 1) as it:
                for u in range(4):
                    load_unit(sp, k, n0 + u + 2, stream(n0 + u + 2 + 4 * it), it=it, per=4)
            for n in range(last_u - 2, min(last_u + 2, last_unit)):
                load_unit(sp, k, n, stream(n))

        @block.gpsimd
        def _(pool):
            res.pool(pool)

        @block.tensor
        def _(pe):
            n_post.pe_all(pe)
            n_pre.pe_all(pe)
            for i in range(KT):
                normed.pe_wait(pe, i)

            def group(it, first):
                for j in range(T1 + T2):
                    u = j // 2 if j < T1 else 2 + (j - T1) // 4
                    n = n0 + u
                    if j in (0, 2, 4, 8):
                        unit_ready(pe, k, n, it, 4)
                    if j < T1:
                        if not first:
                            pe.wait_ge(s["added"], T2 * it - (T1 - 1 - j))
                    elif j < 2 * T1:
                        pe.wait_ge(s["relu"], T1 * it + (j - T1) + 1)
                    else:
                        pe.wait_ge(s["added"], T2 * it + j - 2 * T1 + 1)
                    _, outs = tile_out(k, j % ring, tok)
                    if j < T1:
                        last = dense_tile(pe, k, outs, unit_tiles(k, n, 0, KT, 256, j % 2), k.hhi, k.hlo, tok)
                    else:
                        last = dense_tile(pe, k, outs, unit_tiles(k, n, 0, 4, 512, (j - T1) % 4), hid_hi, hid_lo, tok,
                                          (lambda i: pe.wait_ge(s["hid_lo"], T1 * it + i + 1)) if j == T1 else None)
                    last.then_inc(s["ready"], 1)

            group(0, True)
            with pe.Fori(1, FF_GROUPS) as it:
                group(it, False)

        @block.scalar
        def _(act):
            n_post.act_squares(act)
            n_post.act_root(act)
            n_pre.act_squares(act, lambda e, t: e.wait_ge(res.updated, KT) if t == 0 else None)
            n_pre.act_root(act)
            split_hi(act, k, n0)
            split_hi(act, k, n0 + 1)
            normed.act(act)

            def group(it, last_group):
                def hidden_hi(j):
                    act.wait_ge(s["squared"], T1 * it + j + 1)
                    act.activation(hid_hi[:, j, 0:tok], k.sqt[:, j % 2, 0:tok], ACT.Copy).then_inc(s["hid_hi"], 1)

                for j in range(T1):
                    act.wait_ge(s["ready"], (T1 + T2) * it + j + 1)
                    base, _ = tile_out(k, j % ring, tok)
                    if j >= 2:
                        act.wait_ge(s["hid_lo"], T1 * it + j - 1)
                    act.activation(k.sqt[:, j % 2, 0:tok], k.ps[:, base:base + tok], ACT.Relu).then_inc(s["relu"], 1)
                    hidden_hi(j)
                    if j % 2:
                        split_hi(act, k, n0 + j // 2 + 2, (s["ready"], (T1 + T2) * it + j + 1), it=it, per=4)
                if not last_group:
                    split_hi(act, k, n0 + 4, (s["ready"], (T1 + T2) * it + 8), it=it, per=4)
                    split_hi(act, k, n0 + 5, (s["ready"], (T1 + T2) * it + 12), it=it, per=4)

            with act.Fori(0, FF_GROUPS - 1) as it:
                group(it, False)
            group(FF_GROUPS - 1, True)

        @block.vector
        def _(dve):
            n_post.dve_all(dve)
            res.dve(dve)
            n_pre.dve_all(dve)
            split_lo(dve, k, n0)
            split_lo(dve, k, n0 + 1)
            normed.dve(dve)

            def group(it, first, last_group):
                for j in range(T1):
                    dve.wait_ge(s["relu"], T1 * it + j + 1)
                    sq = k.sqt[:, j % 2, 0:tok]
                    dve.tensor_tensor(sq, sq, sq, ALU.mult).then_inc(s["squared"], 1)
                    dve.wait_ge(s["hid_hi"], T1 * it + j + 1)
                    dve.tensor_tensor(hid_lo[:, j, 0:tok], sq, hid_hi[:, j, 0:tok].bitcast(F32),
                                      ALU.subtract).then_inc(s["hid_lo"], 1)
                    if j % 2:
                        split_lo(dve, k, n0 + j // 2 + 2, it=it, per=4)
                for j in range(T2):
                    dve.wait_ge(s["ready"], (T1 + T2) * it + T1 + j + 1)
                    base, _ = tile_out(k, (T1 + j) % ring, tok)
                    src = k.ps[:, base:base + tok]
                    if first:
                        dve.tensor_copy(y[:, j, 0:tok], src).then_inc(s["added"], 1)
                    else:
                        dve.tensor_tensor(y[:, j, 0:tok], src, y[:, j, 0:tok], ALU.add).then_inc(s["added"], 1)
                    if j % 4 == 3 and not last_group:
                        split_lo(dve, k, n0 + 4 + j // 4, it=it, per=4)

            group(0, True, False)
            with dve.Fori(1, FF_GROUPS - 1) as it:
                group(it, False, False)
            group(FF_GROUPS - 1, False, True)
    return last_u


def stage_residual(nc, k, name, y, tok, post):
    norm = Norm(k, f"{name}_p", y, KT, tok, 5)
    res = Residual(k, f"{name}_r", norm, k.x, post)
    with nc.Block() as block:
        @block.tensor
        def _(pe):
            norm.pe_all(pe)

        @block.scalar
        def _(act):
            norm.act_squares(act)
            norm.act_root(act)

        @block.vector
        def _(dve):
            norm.dve_all(dve)
            res.dve(dve)

        @block.gpsimd
        def _(pool):
            res.pool(pool)


def stage_rope_tables(nc, k, b, positions, inv_freq):
    loaded, chain, sined = k.sem("rt_loaded"), k.sem("rt_chain"), k.sem("rt_sin")
    two_pi = 2 * np.pi
    c1 = float(np.float32(6.28125))
    c2 = float(np.round((two_pi - c1) * 2 ** 21) / 2 ** 21)
    c3 = float(np.float32(two_pi - c1 - c2))
    with nc.Block() as block:
        @block.sync
        def _(sp):
            sp.dma_start(b.pos_i, positions.partition_broadcast(P)).then_inc(loaded, 16)
            sp.dma_start(b.inv, inv_freq).then_inc(loaded, 16)

        @block.vector
        def _(dve):
            n = 0

            def link(ins):
                nonlocal n
                n += 1
                ins.then_inc(chain, 1)
                dve.wait_ge(chain, n)

            ang, turns = k.sqt[:, 0, 0:SEQ], k.sqt[:, 1, 0:SEQ]
            dve.wait_ge(loaded, 32)
            link(dve.tensor_copy(turns, b.pos_i))
            link(dve.tensor_scalar(ang, turns, b.inv, None, ALU.mult))
            for i, (dst, shift) in enumerate(((b.sin, 0.0), (b.cos, float(np.pi / 2)))):
                link(dve.tensor_scalar(turns, ang, 1.0 / two_pi, shift / two_pi, ALU.mult, ALU.add))
                link(dve.tensor_copy(b.pos_i, turns))
                link(dve.tensor_copy(turns, b.pos_i))
                link(dve.scalar_tensor_tensor(dst, turns, -c1, ang, ALU.mult, ALU.add))
                link(dve.scalar_tensor_tensor(dst, turns, -c2, dst, ALU.mult, ALU.add))
                link(dve.scalar_tensor_tensor(dst, turns, -c3, dst, ALU.mult, ALU.add))
                link(dve.tensor_scalar(dst, dst, shift, None, ALU.add))
                link(dve.tensor_scalar(dst, dst, float(np.float32(np.pi)) , -float(np.float32(np.pi)), ALU.min, ALU.max))
            dve.sem_inc(sined, 1)

        @block.scalar
        def _(act):
            act.wait_ge(sined, 1)
            act.activation(b.sin, b.sin, ACT.Sin)
            act.activation(b.cos, b.cos, ACT.Sin)



ADA_TURNS = 6 * DEPTH
U_ADA = 4 * ADA_TURNS
U_DOWN, U_GATE = 3, 1
U_GLA = 4
UNITS_2 = U_ADA + U_DOWN + MH + 4 + UNITS_FF + U_GATE + U_GLA * GH + UNITS_FF
MLA_SCALE = float(192 ** -0.5)


def stage_modulation(nc, k, b, a, stream, n0):
    names = ("loaded", "silu", "c_hi", "c_lo", "ready", "taken", "scales")
    s = {n: k.sem(f"ada_{n}") for n in names}
    with nc.Block() as block:
        @block.sync
        def _(sp):
            load_unit(sp, k, n0, stream(n0))
            load_unit(sp, k, n0 + 1, stream(n0 + 1))
            sp.dma_start(b.cv, a["cvec"]).then_inc(s["loaded"], 16)
            sp.dma_start(b.ada_b, a["ada_b"]).then_inc(s["loaded"], 16)
            sp.dma_start(b.g, a["norm_g2"]).then_inc(s["loaded"], 16)
            with sp.Fori(0, ADA_TURNS) as it:
                for u in range(4):
                    load_unit(sp, k, n0 + u + 2, stream(n0 + u + 2 + 4 * it), it=it, per=4)

        @block.scalar
        def _(act):
            act.wait_ge(s["loaded"], 48)
            act.activation(b.cv, b.cv, ACT.Silu).then_inc(s["silu"], 1)
            act.wait_ge(s["silu"], 1)
            act.activation(b.cv_hi, b.cv, ACT.Copy).then_inc(s["c_hi"], 1)
            split_hi(act, k, n0)
            split_hi(act, k, n0 + 1)

            def turn(it, last):
                for u in range(2 if last else 4):
                    split_hi(act, k, n0 + 2 + u, (s["ready"], 4 * it + u + 1), it=it, per=4)
            with act.Fori(0, ADA_TURNS - 1) as it:
                turn(it, False)
            turn(ADA_TURNS - 1, True)

        @block.tensor
        def _(pe):
            pe.wait_ge(s["c_lo"], 1)
            with pe.Fori(0, ADA_TURNS) as it:
                for u in range(4):
                    n = n0 + u
                    unit_ready(pe, k, n, it, 4)
                    if u == 0:
                        pe.wait_ge(s["taken"], it)
                    for m in range(2):
                        j = 2 * u + m
                        for i, (whi, wlo) in enumerate(unit_tiles(k, n, 0, KT, 256, m)):
                            last = mm3(pe, [k.ps[:, 2 * j:2 * j + 2]], whi, wlo, [(b.cv_hi[:, i, :], b.cv_lo[:, i, :])],
                                       i == 0, i == KT - 1)
                    last.then_inc(s["ready"], 1)

        @block.vector
        def _(dve):
            dve.wait_ge(s["c_hi"], 1)
            dve.tensor_tensor(b.cv_lo, b.cv, b.cv_hi.bitcast(F32), ALU.subtract).then_inc(s["c_lo"], 1)
            split_lo(dve, k, n0)
            split_lo(dve, k, n0 + 1)

            def turn(it, last):
                for u in range(4):
                    if u < 2 or not last:
                        split_lo(dve, k, n0 + 2 + u, it=it, per=4)
                dve.wait_ge(s["ready"], 4 * it + 4)
                ps = k.ps[:, 0:16].rearrange("p (t v) -> p t v", v=2)
                dve.tensor_tensor(b.mod[:, it, :, :], ps, b.ada_b[:, it, :].unsqueeze(2).to_broadcast([P, KT, 2]),
                                  ALU.add).then_inc(s["taken"], 1)
            with dve.Fori(0, ADA_TURNS - 1) as it:
                turn(it, False)
            turn(ADA_TURNS - 1, True)
            dve.wait_ge(s["taken"], ADA_TURNS)
            for l in range(DEPTH):
                for j, (m, plus) in enumerate(((1, 1.0), (2, 0.0), (4, 1.0), (5, 0.0))):
                    g = b.g[:, l, j, :].unsqueeze(2).to_broadcast([P, KT, 2])
                    dve.scalar_tensor_tensor(b.sc[:, 4 * l + j, :, :], b.mod[:, 6 * l + m, :, :], plus, g, ALU.add,
                                             ALU.mult).then_inc(s["scales"], 1)
            dve.wait_ge(s["scales"], 4 * DEPTH)
    return n0 + U_ADA


def parts_of(b, layer, norm, tok, shift=None):
    out = []
    for v, (c0, w) in enumerate(((0, SEQ), (SEQ, CTX))):
        if c0 < tok:
            part = (c0, w, b.sc[:, 4 * layer + norm, :, v])
            out.append(part if shift is None else part + (b.mod[:, 6 * layer + shift, :, v],))
    return out


def stage_norm_dense(nc, k, name, stream, n0, n_units, width, cols, out, tok, parts):
    norm = Norm(k, f"{name}_n", k.x, KT, tok, 5)
    normed = Normed(k, f"{name}_h", norm, k.hhi, k.hlo, parts)
    ready, taken = k.sem(f"{name}_ready"), k.sem(f"{name}_taken")
    ring, per = 4, cols // P
    with nc.Block() as block:
        @block.sync
        def _(sp):
            for n in range(n0 + 2, n0 + n_units + 2):
                load_unit(sp, k, n, stream(n))

        @block.tensor
        def _(pe):
            norm.pe_all(pe)
            for j in range(n_units * per):
                if j % per == 0:
                    unit_ready(pe, k, n0 + j // per)
                if j >= ring:
                    pe.wait_ge(taken, j - ring + 1)
                _, outs = tile_out(k, j % ring, tok)
                last = dense_tile(pe, k, outs, unit_tiles(k, n0 + j // per, 0, KT, cols, j % per), k.hhi, k.hlo, tok,
                                  (lambda i: normed.pe_wait(pe, i)) if j == 0 else None)
                last.then_inc(ready, 1)

        @block.vector
        def _(dve):
            norm.dve_all(dve)
            split_lo(dve, k, n0, width)
            normed.dve(dve)
            for u in range(1, n_units):
                split_lo(dve, k, n0 + u, width)

        @block.scalar
        def _(act):
            norm.act_squares(act)
            norm.act_root(act)
            split_hi(act, k, n0, width=width)
            normed.act(act)
            if n_units > 1:
                split_hi(act, k, n0 + 1, width=width)
            for j in range(n_units * per):
                act.wait_ge(ready, j + 1)
                base, _ = tile_out(k, j % ring, tok)
                act.activation(out[:, j, 0:tok], k.ps[:, base:base + tok], ACT.Copy).then_inc(taken, 1)
                if j % per == per - 1 and j // per + 2 < n_units:
                    split_hi(act, k, n0 + j // per + 2, (ready, j + 1), width)
    return n0 + n_units


def stage_norm(nc, k, name, src, kt, hi, lo, scale):
    norm = Norm(k, f"{name}_n", src, kt, TOK, 5)
    normed = Normed(k, f"{name}_h", norm, hi, lo, [(0, TOK, scale, None)])
    with nc.Block() as block:
        @block.tensor
        def _(pe):
            norm.pe_all(pe)

        @block.vector
        def _(dve):
            norm.dve_all(dve)
            normed.dve(dve)

        @block.scalar
        def _(act):
            norm.act_squares(act)
            norm.act_root(act)
            normed.act(act)


def stage_key_rope(nc, k, b, src):
    turned, half1, half2 = k.sem("kr_turned"), k.sem("kr_cos"), k.sem("kr_sin")
    with nc.Block() as block:
        @block.tensor
        def _(pe):
            pe.matmul(k.ps[:, 0:SEQ], k.c["axial_perm"], src[:, 0:SEQ], start=True, stop=True).then_inc(turned, 1)

        @block.gpsimd
        def _(pool):
            pool.tensor_tensor(k.sqt[:, 0, 0:SEQ], src[:, 0:SEQ], b.axial[:, 0, :], ALU.mult).then_inc(half1, 1)

        @block.scalar
        def _(act):
            act.activation(b.krope[:, SEQ:TOK], src[:, SEQ:TOK], ACT.Copy)

        @block.vector
        def _(dve):
            dve.wait_ge(turned, 1)
            dve.tensor_tensor(k.acc[:, 0:SEQ], k.ps[:, 0:SEQ], b.axial[:, 1, :], ALU.mult).then_inc(half2, 1)
            dve.wait_ge(half2, 1)
            dve.wait_ge(half1, 1)
            dve.tensor_tensor(b.krope[:, 0:SEQ], k.acc[:, 0:SEQ], k.sqt[:, 0, 0:SEQ], ALU.add)


def stage_latent_attention(nc, k, b, stream, n0):
    names = ("projected", "taken_a", "taken_v", "raw", "turned", "half1", "half2", "rotated", "scored", "maxed",
             "expd", "scaled", "flipped", "copied_a", "copied_v", "summed", "hi_done", "lo_done", "chain")
    s = {n: k.sem(f"la_{n}") for n in names}
    U = TOK // P
    LINKS = 2 * U
    W_QN, W_QR, W_K, W_V = 0, 384, 768, 1024

    def keys(u):
        return (0, TOK) if u < QT else (SEQ, CTX)

    def pieces(w):
        return [(0, 512), (512, w - 512)] if w > 512 else [(0, w)]

    with nc.Block() as block:
        @block.sync
        def _(sp):
            with sp.Fori(0, MH // 2) as it:
                for hd in range(2):
                    load_unit(sp, k, n0 + hd + 2, stream(n0 + hd + 2 + 2 * it), it=it, per=2)

        def head(pe, hd, H, it):
            n = n0 + hd
            tiles = lambda off, kt: [(k.whi[:, n % 2, off + i * P:off + (i + 1) * P], k.wlo[:, n % 2, off + i * P:off + (i + 1) * P])
                                     for i in range(kt)]
            unit_ready(pe, k, n, it, 2)
            pe.wait_ge(s["expd"], U * H)
            dense_tile(pe, k, tile_out(k, 0, TOK)[1], tiles(W_QN, 3), b.cq_hi, b.cq_lo, TOK).then_inc(s["projected"], 1)
            dense_tile(pe, k, tile_out(k, 1, TOK)[1], tiles(W_QR, 3), b.cq_hi, b.cq_lo, TOK).then_inc(s["projected"], 1)
            pe.wait_ge(s["copied_a"], U * H)
            pe.wait_ge(s["copied_v"], QT * H)
            dense_tile(pe, k, tile_out(k, 2, TOK)[1], tiles(W_K, 2), b.ckv_hi, b.ckv_lo, TOK).then_inc(s["projected"], 1)
            pe.wait_ge(s["lo_done"], H)
            for t in range(U):
                c = slice(t * P, (t + 1) * P)
                for i, w in enumerate(tiles(W_V, 2)):
                    last = mm3(pe, [k.ps[:, 3072 + t * P:3072 + (t + 1) * P]], b.ckv_hi[:, i, c], b.ckv_lo[:, i, c],
                               [w], i == 0, i == 1)
            last.then_inc(s["projected"], 1)
            pe.wait_ge(s["taken_a"], 3 * H + 2)
            pe.matmul(k.ps[:, 1024:1536], k.c["axial_perm"], b.qraw, start=True, stop=True).then_inc(s["turned"], 1)

            def scores(u):
                k0, w = keys(u)
                c = slice(u * P, (u + 1) * P)
                if u == 0:
                    pe.wait_ge(s["taken_a"], 3 * H + 3)
                    pe.wait_ge(s["rotated"], H + 1)
                else:
                    pe.wait_ge(s["expd"], U * H + max(u - 1, 0))
                base = (u % 2) * 1024
                for p0, pw in pieces(w):
                    out = k.ps[:, base + p0:base + p0 + pw]
                    pe.matmul(out, b.qn[:, c], b.kn[:, k0 + p0:k0 + p0 + pw], start=True, stop=False)
                    last = pe.matmul(out, b.qr[0:64, c], b.krope[0:64, k0 + p0:k0 + p0 + pw], start=False, stop=True)
                last.then_inc(s["scored"], 1)

            def flips(u):
                _, w = keys(u)
                pe.wait_ge(s["scaled"], U * H + u + 1)
                pe.wait_ge(s["copied_a"], U * H + u)
                pe.wait_ge(s["copied_v"], QT * H + min(u, QT))
                for j in range(w // P):
                    last = pe.transpose(k.ps[:, 2048 + j * P:2048 + (j + 1) * P], b.p[:, u % 2, j * P:(j + 1) * P], k.c["ident"])
                last.then_inc(s["flipped"], 1)

            def values(u):
                k0, w = keys(u)
                if u == 0:
                    pe.wait_ge(s["taken_v"], H + 1)
                pe.wait_ge(s["copied_a"], U * H + u + 1)
                pe.wait_ge(s["copied_v"], QT * H + min(u + 1, QT))
                for j in range(w // P):
                    last = pe.matmul(k.ps[:, 3072 + u * P:3072 + (u + 1) * P], b.v[:, k0 // P + j, :],
                                     b.pt[:, u % 2, j * P:(j + 1) * P], start=j == 0, stop=j == w // P - 1)
                last.then_inc(s["summed"], 1)

            scores(0)
            scores(1)
            flips(0)
            for u in range(U):
                if u + 2 < U:
                    scores(u + 2)
                if u + 1 < U:
                    flips(u + 1)
                values(u)

        @block.tensor
        def _(pe):
            with pe.Fori(0, MH // 2) as it:
                for hd in range(2):
                    head(pe, hd, 2 * it + hd, it)

        @block.gpsimd
        def _(pool):
            with pool.Fori(0, MH) as H:
                pool.wait_ge(s["raw"], H + 1)
                pool.tensor_tensor(b.qcos, b.qraw, b.axial[:, 0, :], ALU.mult).then_inc(s["half1"], 1)

        def head_v(dve, hd, H, it, last_head):
            n = 0

            def link(ins):
                nonlocal n
                n += 1
                ins.then_inc(s["chain"], 1)
                dve.wait_ge(s["chain"], LINKS * H + n)

            dve.wait_ge(s["projected"], 4 * H + 4)
            dve.tensor_copy(b.v[:, :, :].rearrange("p a b -> p (a b)"), k.ps[:, 3072:3072 + TOK]).then_inc(s["taken_v"], 1)
            dve.wait_ge(s["turned"], H + 1)
            dve.tensor_tensor(k.acc[:, 0:SEQ], k.ps[:, 1024:1536], b.axial[:, 1, :], ALU.mult).then_inc(s["half2"], 1)
            dve.wait_ge(s["half1"], H + 1)
            dve.wait_ge(s["half2"], H + 1)
            dve.tensor_tensor(b.qr[:, 0:SEQ], k.acc[:, 0:SEQ], b.qcos, ALU.add).then_inc(s["rotated"], 1)
            if not last_head:
                split_lo(dve, k, n0 + hd + 1, MLA_U, it=it, per=2)

            def top(u):
                _, w = keys(u)
                dve.wait_ge(s["scored"], U * H + u + 1)
                base = (u % 2) * 1024
                link(dve.tensor_reduce(b.st[:, u % 2, 0:1], k.ps[:, base:base + w], AX_X, ALU.max))
                dve.tensor_scalar(b.st[:, u % 2, 1:2], b.st[:, u % 2, 0:1], -MLA_SCALE, None, ALU.mult).then_inc(s["maxed"], 1)

            def scale(u):
                _, w = keys(u)
                dve.wait_ge(s["expd"], U * H + u + 1)
                link(dve.reciprocal(b.st[:, u % 2, 3:4], b.st[:, u % 2, 2:3]))
                dve.tensor_scalar(b.p[:, u % 2, 0:w], b.p[:, u % 2, 0:w], b.st[:, u % 2, 3:4], None,
                                  ALU.mult).then_inc(s["scaled"], 1)

            def copy(u):
                if u < QT:
                    dve.wait_ge(s["flipped"], U * H + u + 1)
                    if u >= 2:
                        dve.wait_ge(s["summed"], U * H + u - 1)
                    dve.tensor_copy(b.pt[:, u % 2, 512:TOK], k.ps[:, 2560:2560 + TOK - 512]).then_inc(s["copied_v"], 1)

            top(0)
            top(1)
            scale(0)
            for u in range(U):
                copy(u)
                if u + 2 < U:
                    top(u + 2)
                if u + 1 < U:
                    scale(u + 1)
            dve.wait_ge(s["hi_done"], H + 1)
            dve.tensor_tensor(k.hlo[:, H, :], k.ps[:, 3072:3072 + TOK], k.hhi[:, H, :].bitcast(F32),
                              ALU.subtract).then_inc(s["lo_done"], 1)
            assert n == LINKS

        @block.vector
        def _(dve):
            split_lo(dve, k, n0, MLA_U)
            with dve.Fori(0, MH // 2 - 1) as it:
                for hd in range(2):
                    head_v(dve, hd, 2 * it + hd, it, False)
            for hd in range(2):
                head_v(dve, hd, MH - 2 + hd, MH // 2 - 1, hd == 1)

        def head_a(act, hd, H, it, last_head):
            act.wait_ge(s["projected"], 4 * H + 1)
            act.activation(b.qn, k.ps[:, 0:TOK], ACT.Copy).then_inc(s["taken_a"], 1)
            act.wait_ge(s["projected"], 4 * H + 2)
            act.wait_ge(s["rotated"], H)
            act.activation(b.qraw, k.ps[:, 1024:1536], ACT.Copy).then_inc(s["raw"], 1)
            act.activation(b.qr[:, SEQ:TOK], k.ps[:, 1536:1536 + CTX], ACT.Copy).then_inc(s["taken_a"], 1)
            act.wait_ge(s["projected"], 4 * H + 3)
            act.activation(b.kn, k.ps[:, 2048:2048 + TOK], ACT.Copy).then_inc(s["taken_a"], 1)
            if not last_head:
                split_hi(act, k, n0 + hd + 1, (s["projected"], 4 * H + 3), MLA_U, it, 2)

            def exps(u):
                _, w = keys(u)
                act.wait_ge(s["maxed"], U * H + u + 1)
                if u >= 2:
                    act.wait_ge(s["flipped"], U * H + u - 1)
                base = (u % 2) * 1024
                act.activation(b.p[:, u % 2, 0:w], k.ps[:, base:base + w], ACT.Exp, bias=b.st[:, u % 2, 1:2],
                               scale=MLA_SCALE, accum_out=b.st[:, u % 2, 2:3]).then_inc(s["expd"], 1)

            def copy(u):
                _, w = keys(u)
                w = min(w, 512)
                act.wait_ge(s["flipped"], U * H + u + 1)
                if u >= 2:
                    act.wait_ge(s["summed"], U * H + u - 1)
                act.activation(b.pt[:, u % 2, 0:w], k.ps[:, 2048:2048 + w], ACT.Copy).then_inc(s["copied_a"], 1)

            exps(0)
            exps(1)
            for u in range(U):
                copy(u)
                if u + 2 < U:
                    exps(u + 2)
            act.wait_ge(s["summed"], U * (H + 1))
            act.activation(k.hhi[:, H, :], k.ps[:, 3072:3072 + TOK], ACT.Copy).then_inc(s["hi_done"], 1)

        @block.scalar
        def _(act):
            split_hi(act, k, n0, width=MLA_U)
            with act.Fori(0, MH // 2 - 1) as it:
                for hd in range(2):
                    head_a(act, hd, 2 * it + hd, it, False)
            for hd in range(2):
                head_a(act, hd, MH - 2 + hd, MH // 2 - 1, hd == 1)

    return n0 + MH


def stage_gla_heads(nc, k, b, a, stream, n0):
    names = ("small", "zeroed", "projected", "taken_q", "taken_k", "taken_v", "taken_r", "gated", "biased", "absd",
             "exp1", "logd", "ends", "decays", "tilted", "tilted_p", "attended", "masked", "flipped", "turned",
             "state_f", "state_b", "updated_f", "updated_b", "summed", "o_out", "normed", "value", "hi_done",
             "lo_done", "ready", "added", "chain")
    s = {n: k.sem(f"gla_{n}") for n in names}
    NCH = TOK // CH
    LAT = SEQ // CH
    seqs = ([8, 9, 10, 11, 0, 1, 2, 3, 4, 5, 6, 7], [11, 10, 9, 8, 7, 6, 5, 4, 3, 2, 1, 0])
    upd = (s["updated_f"], s["updated_b"])
    sta = (s["state_f"], s["state_b"])
    STEPS = NCH - 1
    inv_tau = 1.0 / 16.0
    g, cum, tail = (k.acc, k.diag), (k.sqt[:, 0, :], k.sqt[:, 1, :]), (b.ke[:, 0, :], b.ke[:, 1, :])
    att = (k.acc[:, 0:SEQ], k.diag[:, 0:SEQ])
    chunked = lambda t: t.rearrange("p (c i) -> p c i", i=CH)
    TILES = 7
    V_AT = [512, 768, 0, 256, 1024, 1280]
    R_AT = [1536, 512]
    PS_A, PS_S, PS_O, PS_T = (0, 1024), (512, 1536), (2048, 2560), (2048, 3072)
    BIG = 3e38

    with nc.Block() as block:
        @block.sync
        def _(sp):
            with sp.Fori(0, GH) as it:
                sp.wait_ge(s["biased"], 2 * it)
                sp.dma_start(b.w2s, a["gla_w2"][it]).then_inc(s["small"], 16)
                sp.dma_start(b.bias, a["gla_b"][it]).then_inc(s["small"], 16)
                for u in range(4):
                    load_unit(sp, k, n0 + u + 2, stream(n0 + u + 2 + 4 * it), it=it, per=4)

        @block.tensor
        def _(pe):
            with pe.Fori(0, GH) as it:
                norm = b.o_norm.at(it)
                unit_ready(pe, k, n0, it, 4)
                pe.wait_ge(s["added"], KT * it)
                dense_tile(pe, k, [k.ps[:, 0:512]], unit_tiles(k, n0, 0, KT, P, 0), k.hhi, k.hlo, SEQ).then_inc(s["projected"], 1)
                dense_tile(pe, k, tile_out(k, 1, TOK)[1], unit_tiles(k, n0, 1024, KT, P, 0), k.hhi, k.hlo, TOK).then_inc(s["projected"], 1)
                pe.wait_ge(s["small"], 32 * (it + 1))
                pe.wait_ge(s["lo_done"], 2 * it)
                for d in range(2):
                    for c0, w in chunks(TOK):
                        last = pe.matmul(k.ps[:, 2048 + 1024 * d + c0:2048 + 1024 * d + c0 + w], b.w2s[32 * d:32 * d + 16, :],
                                         b.lr[32 * d:32 * d + 16, c0:c0 + w], start=True, stop=True)
                    last.then_inc(s["gated"], 1)
                unit_ready(pe, k, n0 + 1, it, 4)
                for t in range(6):
                    if t == 2:
                        pe.wait_ge(s["taken_q"], it + 1)
                    if t == 4:
                        pe.wait_ge(s["taken_k"], it + 1)
                    n = n0 + 1
                    for i in range(KT):
                        w = (k.whi[:, n % 2, i * 256:(i + 1) * 256], k.wlo[:, n % 2, i * 256:(i + 1) * 256])
                        last = mm3(pe, [k.ps[:, V_AT[t]:V_AT[t] + 256]], k.hhi[:, i, t * P:(t + 1) * P],
                                   k.hlo[:, i, t * P:(t + 1) * P], [w], i == 0, i == KT - 1)
                    if t % 2:
                        last.then_inc(s["projected"], 1)
                unit_ready(pe, k, n0 + 2, it, 4)
                for m in range(2):
                    if m == 1:
                        pe.wait_ge(s["taken_v"], 3 * it + 1)
                    dense_tile(pe, k, [k.ps[:, R_AT[m]:R_AT[m] + 512]], unit_tiles(k, n0 + 2, 0, KT, 256, m),
                               k.hhi, k.hlo, SEQ).then_inc(s["projected"], 1)
                pe.wait_ge(s["tilted"], 4 * it + 4)
                pe.wait_ge(s["taken_v"], 3 * it + 3)
                for d in range(2):
                    for t in range(QT):
                        c = slice(t * P, (t + 1) * P)
                        last = pe.matmul(k.ps[:, PS_A[d] + t * P:PS_A[d] + (t + 1) * P], b.kt[:, d, c], b.qt[:, d, c],
                                         start=True, stop=True)
                    last.then_inc(s["attended"], 1)
                for d in range(2):
                    pe.wait_ge(s["tilted_p"], 2 * it + d + 1)
                    for t in range(6):
                        last = pe.transpose(k.ps[:, PS_T[d] + t * P:PS_T[d] + (t + 1) * P], b.ke[:, d, t * P:(t + 1) * P], k.c["ident"])
                    last.then_inc(s["flipped"], 1)
                pe.wait_ge(s["turned"], 2 * it + 2)
                pe.wait_ge(s["taken_r"], 2 * it + 2)

                def update(i):
                    for d in range(2):
                        c = seqs[d][i]
                        r = slice(CH * (c % 2), CH * (c % 2) + CH)
                        if i:
                            pe.wait_ge(upd[d], STEPS * it + i)
                        pe.matmul(k.ps[:, PS_S[d]:PS_S[d] + 256], b.ket[r, d, c // 2, :], b.v[r, c // 2, :],
                                  start=True, stop=True).then_inc(sta[d], 1)

                def inter(i):
                    for d in range(2):
                        c = seqs[d][i]
                        pe.wait_ge(upd[d], STEPS * it + i)
                        for vt in range(2):
                            last = pe.matmul(k.ps[:, PS_O[vt] + c * CH:PS_O[vt] + (c + 1) * CH],
                                             b.state[:, d, i % 2, vt * P:(vt + 1) * P], b.qt[:, d, c * CH:(c + 1) * CH],
                                             start=False, stop=d == 1 and i == NCH - 1, skip_group_check=True)
                    return last

                for i in range(NCH):
                    if i == NCH - LAT:
                        pe.wait_ge(s["masked"], it + 1)
                        for vt in range(2):
                            for t in range(QT):
                                pe.matmul(k.ps[:, PS_O[vt] + t * P:PS_O[vt] + (t + 1) * P], b.v[:, t, vt * P:(vt + 1) * P],
                                          att[0][:, t * P:(t + 1) * P], start=t == 0, stop=False, skip_group_check=True)
                    if i < STEPS:
                        update(i)
                    if i >= NCH - LAT:
                        last = inter(i)
                last.then_inc(s["summed"], 1)
                norm.pe_all(pe)
                unit_ready(pe, k, n0 + 3, it, 4)
                for m in range(KT):
                    if m >= 4:
                        pe.wait_ge(s["added"], KT * it + m - 3)
                    last = dense_tile(pe, k, [k.ps[:, (m % 4) * 512:(m % 4) * 512 + 512]],
                                      unit_tiles(k, n0 + 3, 0, 2, 1024, m), b.o_hi, b.o_lo, SEQ,
                                      (lambda i: pe.wait_ge(s["lo_done"], 2 * it + i + 1)) if m == 0 else None)
                    last.then_inc(s["ready"], 1)

        @block.gpsimd
        def _(pool):
            pool.memset(b.y, 0.0).then_inc(s["zeroed"], 1)
            with pool.Fori(0, GH) as it:
                for d in range(2):
                    pool.wait_ge(s["decays"], 2 * it + d + 1)
                    pool.wait_ge(s["taken_k"], it + 1)
                    pool.tensor_tensor(tail[d], tail[d], b.k, ALU.mult).then_inc(s["tilted_p"], 1)

        def turn_v(dve, it, last_turn):
            norm = b.o_norm.at(it)
            n = 0

            def link(ins):
                nonlocal n
                n += 1
                ins.then_inc(s["chain"], 1)
                dve.wait_ge(s["chain"], CHAIN * it + n)

            CHAIN = 9
            for d in range(2):
                dve.wait_ge(s["gated"], 2 * it + d + 1)
                dve.tensor_scalar(g[d], k.ps[:, 2048 + 1024 * d:2048 + 1024 * d + TOK], b.bias[:, d:d + 1], None,
                                  ALU.add).then_inc(s["biased"], 1)
            for d in range(2):
                dve.wait_ge(s["logd"], 2 * it + d + 1)
                link(dve.scalar_tensor_tensor(g[d], g[d], 0.0, tail[d], ALU.min, ALU.subtract))
                link(dve.tensor_tensor_scan(cum[d], b.reset, g[d], 0.0, ALU.mult, ALU.add))
                total = chunked(cum[d])[:, :, CH - 1:CH]
                if d == 0:
                    dve.tensor_tensor(chunked(tail[0]), total.to_broadcast([P, NCH, CH]), chunked(cum[0]),
                                      ALU.subtract).then_inc(s["ends"], 1)
                else:
                    link(dve.tensor_tensor(tail[1], cum[1], g[1], ALU.subtract))
                    dve.tensor_tensor(chunked(b.kt[:, 1, :]), total[:, 0:LAT].to_broadcast([P, LAT, CH]),
                                      chunked(tail[1][:, 0:SEQ]), ALU.subtract).then_inc(s["ends"], 1)
            split_lo(dve, k, n0 + 2, it=it, per=4)
            for d in range(2):
                dve.wait_ge(s["decays"], 2 * it + d + 1)
                dve.wait_ge(s["taken_q"], it + 1)
                dve.wait_ge(s["taken_k"], it + 1)
                dve.tensor_tensor(b.qt[:, d, :], b.qt[:, d, :], b.q, ALU.mult).then_inc(s["tilted"], 1)
                dve.tensor_tensor(b.kt[:, d, :], b.kt[:, d, :], b.k[:, 0:SEQ], ALU.mult).then_inc(s["tilted"], 1)
            for d, mask in enumerate((k.c["gla_f"], k.c["gla_b"])):
                dve.wait_ge(s["attended"], 2 * it + d + 1)
                link(dve.tensor_scalar(att[d], k.ps[:, PS_A[d]:PS_A[d] + SEQ], BIG, -BIG, ALU.min, ALU.max))
                tiles = att[d].rearrange("p (t q) -> p t q", q=P)
                link(dve.tensor_tensor(tiles, tiles, mask.unsqueeze(1).to_broadcast([P, QT, P]), ALU.mult))
            dve.tensor_tensor(att[0], att[0], att[1], ALU.add).then_inc(s["masked"], 1)
            split_lo(dve, k, n0 + 3, it=it, per=4)
            for i in range(STEPS):
                for d in range(2):
                    c = seqs[d][i]
                    dve.wait_ge(sta[d], STEPS * it + i + 1)
                    new = b.state[:, d, (i + 1) % 2, :]
                    src = k.ps[:, PS_S[d]:PS_S[d] + 256]
                    if i == 0:
                        dve.tensor_copy(new, src).then_inc(upd[d], 1)
                    else:
                        dve.wait_ge(upd[d], STEPS * it + i)
                        dve.scalar_tensor_tensor(new, b.state[:, d, i % 2, :], b.decay[:, d, c:c + 1], src, ALU.mult,
                                                 ALU.add).then_inc(upd[d], 1)
            norm.dve_all(dve)
            dve.wait_ge(norm.spread, it + 1)
            for t in range(2):
                dve.scalar_tensor_tensor(b.of[:, t, :], b.of[:, t, :], b.g_o[:, t:t + 1], norm.rb, ALU.mult,
                                         ALU.mult).then_inc(s["normed"], 1)
            for t in range(2):
                dve.wait_ge(s["normed"], 2 * it + t + 1)
                dve.tensor_tensor(b.of[:, t, :], b.of[:, t, :], b.sr[:, t, :], ALU.mult).then_inc(s["value"], 1)
            for t in range(2):
                dve.wait_ge(s["hi_done"], 2 * it + t + 1)
                dve.tensor_tensor(b.o_lo[:, t, :], b.of[:, t, :], b.o_hi[:, t, :].bitcast(F32),
                                  ALU.subtract).then_inc(s["lo_done"], 1)
            if not last_turn:
                split_lo(dve, k, n0 + 4, it=it, per=4)
            dve.wait_ge(s["zeroed"], 1)
            for m in range(KT):
                dve.wait_ge(s["ready"], KT * it + m + 1)
                dve.tensor_tensor(b.y[:, m, :], k.ps[:, (m % 4) * 512:(m % 4) * 512 + 512], b.y[:, m, :],
                                  ALU.add).then_inc(s["added"], 1)
            if not last_turn:
                split_lo(dve, k, n0 + 5, it=it, per=4)
            assert n == CHAIN

        @block.vector
        def _(dve):
            split_lo(dve, k, n0)
            split_lo(dve, k, n0 + 1)
            with dve.Fori(0, GH - 1) as it:
                turn_v(dve, it, False)
            turn_v(dve, GH - 1, True)

        def v_pair(act, pair, P0):
            a = V_AT[2 * pair]
            act.wait_ge(s["projected"], P0 + 3 + pair)
            act.activation(b.v[:, 2 * pair:2 * pair + 2, :].rearrange("p a b -> p (a b)"), k.ps[:, a:a + 512],
                           ACT.Copy).then_inc(s["taken_v"], 1)

        def turn_a(act, it, last_turn):
            norm = b.o_norm.at(it)
            P0 = TILES * it
            act.wait_ge(s["projected"], P0 + 1)
            act.activation(b.q, k.ps[:, 0:512], ACT.Copy, scale=float(P ** -0.5)).then_inc(s["taken_q"], 1)
            act.wait_ge(s["projected"], P0 + 2)
            act.activation(b.k, k.ps[:, 1024:1024 + TOK], ACT.Copy).then_inc(s["taken_k"], 1)
            split_hi(act, k, n0 + 2, (s["projected"], P0 + 2), it=it, per=4)
            for d in range(2):
                act.wait_ge(s["biased"], 2 * it + d + 1)
                act.activation(tail[d], g[d], ACT.Abs).then_inc(s["absd"], 1)
            for d in range(2):
                act.wait_ge(s["absd"], 2 * it + d + 1)
                act.activation(tail[d], tail[d], ACT.Exp, scale=-1.0).then_inc(s["exp1"], 1)
            for d in range(2):
                act.wait_ge(s["exp1"], 2 * it + d + 1)
                act.activation(tail[d], tail[d], ACT.Ln, bias=1.0).then_inc(s["logd"], 1)
            v_pair(act, 0, P0)
            for d in range(2):
                act.wait_ge(s["ends"], 2 * it + d + 1)
                cols = chunked(cum[d])[:, :, CH - 1]
                act.activation(b.decay[:, d, :], cols, ACT.Exp, scale=inv_tau)
                src = cum[0][:, 0:SEQ] if d == 0 else b.kt[:, 1, :]
                act.activation(b.qt[:, d, :], src, ACT.Exp, scale=inv_tau)
                act.activation(tail[d], tail[d], ACT.Exp, scale=inv_tau)
                act.activation(b.kt[:, d, :], src, ACT.Exp, scale=-inv_tau).then_inc(s["decays"], 1)
            v_pair(act, 1, P0)
            v_pair(act, 2, P0)
            split_hi(act, k, n0 + 3, (s["projected"], P0 + 5), it=it, per=4)
            for m in range(2):
                act.wait_ge(s["projected"], P0 + 6 + m)
                act.activation(b.sr[:, m, :], k.ps[:, R_AT[m]:R_AT[m] + 512], ACT.Silu).then_inc(s["taken_r"], 1)
            for d in range(2):
                act.wait_ge(s["flipped"], 2 * it + d + 1)
                act.activation(b.ket[:, d, :, :].rearrange("p a b -> p (a b)"), k.ps[:, PS_T[d]:PS_T[d] + TOK],
                               ACT.Copy).then_inc(s["turned"], 1)
            if not last_turn:
                split_hi(act, k, n0 + 4, (s["projected"], P0 + 7), it=it, per=4)
            act.wait_ge(s["summed"], it + 1)
            act.activation(b.of[:, 0, :], k.ps[:, PS_O[0]:PS_O[0] + 512], ACT.Copy).then_inc(s["o_out"], 1)
            act.activation(b.of[:, 1, :], k.ps[:, PS_O[1]:PS_O[1] + 512], ACT.Copy).then_inc(s["o_out"], 1)
            norm.act_squares(act, lambda e, t: e.wait_ge(s["o_out"], 2 * it + t + 1))
            norm.act_root(act)
            for t in range(2):
                act.wait_ge(s["value"], 2 * it + t + 1)
                act.activation(b.o_hi[:, t, :], b.of[:, t, :], ACT.Copy).then_inc(s["hi_done"], 1)
            if not last_turn:
                split_hi(act, k, n0 + 5, (s["ready"], KT * it + KT), it=it, per=4)

        @block.scalar
        def _(act):
            split_hi(act, k, n0)
            split_hi(act, k, n0 + 1)
            with act.Fori(0, GH - 1) as it:
                turn_a(act, it, False)
            turn_a(act, GH - 1, True)

    return n0 + U_GLA * GH


def second_block(nc, k, a):
    at = k.at
    b = Bag()
    stream = lambda n: a["stream2"][n]
    k.hhi, k.hlo = at("h_hi_2", [P, KT, TOK], F32R, 60), at("h_lo_2", [P, KT, TOK], F32R, 84)
    b.axial = at("axial", [P, 2, SEQ], F32, 108)
    b.mod, b.sc = at("mod", [P, ADA_TURNS, KT, 2], F32, 112), at("norm_scales", [P, 4 * DEPTH, KT, 2], F32, 112.75)
    b.g_q, b.g_kv, b.g_o = at("g_q", [P, 3], F32, 113.25), at("g_kv", [P, 2], F32, 113.3125), at("g_o", [P, 2], F32, 113.375)
    b.st, b.spare = at("mla_stat", [P, 2, 4], F32, 113.5), at("spare", [P, 1], F32, 113.5625)
    b.cv, b.cv_hi, b.cv_lo = at("cvec", [P, KT, 2], F32, 114), at("cvec_hi", [P, KT, 2], F32R, 115), at("cvec_lo", [P, KT, 2], F32R, 116)
    b.ada_b, b.g = at("ada_b", [P, ADA_TURNS, KT], F32, 117), at("norm_g2", [P, DEPTH, 4, KT], F32, 118)
    y = at("y2", [P, KT, TOK], F32, 151)
    down = at("mla_down", [P, 6, TOK], F32, 151)
    b.cq_hi, b.cq_lo = at("cq_hi", [P, 3, TOK], F32R, 114), at("cq_lo", [P, 3, TOK], F32R, 123)
    b.ckv_hi, b.ckv_lo = at("ckv_hi", [P, 2, TOK], F32R, 132), at("ckv_lo", [P, 2, TOK], F32R, 138)
    b.krope = at("k_rope", [P, TOK], F32, 144)
    b.qn, b.qr, b.kn = at("q_nope", [P, TOK], F32, 147), at("q_rope", [P, TOK], F32, 150), at("k_nope", [P, TOK], F32, 153)
    b.v, b.qraw, b.qcos = at("mla_v", [P, TOK // P, P], F32, 156), at("q_raw", [P, SEQ], F32, 159), at("q_cos", [P, SEQ], F32, 161)
    b.p, b.pt = k.sqt, at("mla_pt", [P, 2, TOK], F32, 163)
    hid_hi, hid_lo = at("hid_hi2", [P, 4, TOK], F32R, 127), at("hid_lo2", [P, 4, TOK], F32R, 139)

    loaded = k.sem("second_loaded")
    with nc.Block() as block:
        @block.sync
        def _(sp):
            for dst, src in ((b.axial, a["axial"]), (b.g_q, a["g_q"]), (b.g_kv, a["g_kv"]), (b.g_o, a["g_o"])):
                sp.dma_start(dst, src).then_inc(loaded, 16)
            sp.wait_ge(loaded, 64)

    rings(k, "second", 175)
    n = stage_modulation(nc, k, b, a, stream, 0)
    with k.sem_scope():
        n = stage_norm_dense(nc, k, "down", stream, n, U_DOWN, UNIT, 256, down, TOK, parts_of(b, 0, 0, TOK, 0))
        stage_norm(nc, k, "cq", down[:, 0:3, :], 3, b.cq_hi, b.cq_lo, b.g_q)
        stage_norm(nc, k, "ckv", down[:, 3:5, :], 2, b.ckv_hi, b.ckv_lo, b.g_kv)
        stage_key_rope(nc, k, b, down[:, 5, :])
        n = stage_latent_attention(nc, k, b, stream, n)
        n = stage_project(nc, k, "mla_o", stream, n, k.hhi, k.hlo, y, TOK, UNITS_2)
    with k.sem_scope():
        n = stage_mlp(nc, k, "mlp0", stream, n, y, hid_hi, hid_lo, TOK, parts_of(b, 0, 1, TOK), parts_of(b, 0, 2, TOK, 3), UNITS_2)
        stage_residual(nc, k, "mlp0r", y, TOK, parts_of(b, 0, 3, TOK))
    c = Bag()
    c.g_o = b.g_o
    low = at("gate_low", [P, 1, TOK], F32, 114)
    c.lr = low[:, 0, :]
    c.q, c.k, c.v = at("gla_q", [P, SEQ], F32, 117), at("gla_k", [P, TOK], F32, 119), at("gla_v", [P, 6, 256], F32, 122)
    c.sr, c.ke, c.of = at("silu_r", [P, 2, SEQ], F32, 128), at("k_end", [P, 2, TOK], F32, 132), at("gla_o", [P, 2, SEQ], F32, 132)
    c.qt, c.kt = at("q_tilt", [P, 2, SEQ], F32, 138), at("k_tilt", [P, 2, SEQ], F32, 142)
    c.o_hi, c.o_lo = at("gla_o_hi", [P, 2, SEQ], F32R, 138), at("gla_o_lo", [P, 2, SEQ], F32R, 142)
    c.ket, c.state = at("k_end_t", [P, 2, 6, P], F32, 146), at("state", [P, 2, 2, 256], F32, 152)
    c.reset, c.y = at("chunk_reset", [P, TOK], F32, 156), at("y3", [P, KT, SEQ], F32, 159)
    c.w2s, c.bias, c.decay = at("gate2", [64, P], F32, 59.25), at("gate_bias", [P, 2], F32, 59.8125), at("decay", [P, 2, 12], F32, 59.875)
    n = stage_norm_dense(nc, k, "gate1", stream, n, U_GATE, 1024, P, low, TOK,
                         parts_of(b, 1, 0, TOK, 0))
    c.o_norm = Norm(k, "o_norm", c.of, 2, SEQ, 6)
    r_set = k.sem("reset_set")
    with nc.Block() as block:
        @block.vector
        def _(dve):
            dve.memset(c.reset, 1.0).then_inc(r_set, 1)
            dve.wait_ge(r_set, 1)
            dve.memset(c.reset.rearrange("p (c i) -> p c i", i=CH)[:, :, 0:1], 0.0)
    n = stage_gla_heads(nc, k, c, a, stream, n)
    hid_hi, hid_lo = at("hid_hi3", [P, 4, SEQ], F32R, 114), at("hid_lo3", [P, 4, SEQ], F32R, 122)
    n = stage_mlp(nc, k, "mlp1", stream, n, c.y, hid_hi, hid_lo, SEQ, parts_of(b, 1, 1, SEQ), parts_of(b, 1, 2, SEQ, 3), UNITS_2)
    stage_residual(nc, k, "mlp1r", c.y, SEQ, parts_of(b, 1, 3, SEQ))
    assert n == UNITS_2


def second_arrays(g, a):
    col = lambda v: np.ascontiguousarray(v.reshape(-1, P).T)
    a["axial"] = axial_table()
    a["cvec"] = np.stack([col(g["c_2"][0]), col(g["c_ctx_2"])], 2)
    a["ada_b"] = np.ascontiguousarray(g["ada_b_2"].reshape(ADA_TURNS, KT, P).transpose(2, 0, 1))
    a["norm_g2"] = np.ascontiguousarray(g["norm_g_2"].reshape(DEPTH, 4, KT, P).transpose(3, 0, 1, 2))
    a["g_q"], a["g_kv"], a["g_o"] = col(g["mla_g_q_2"][0]), col(g["mla_g_kv_2"][0]), col(g["gla_g_o_2"][0])
    out = [units(g["ada_w_2"][l], KT, 256, 24) for l in range(DEPTH)]
    dkv = g["mla_w_dkv_2"][0]
    out.append(units(np.concatenate([g["mla_w_dq_2"][0], dkv, dkv[:, 256:]], 1), KT, 256, U_DOWN))
    uq, ukv = g["mla_w_uq_2"][0], g["mla_w_ukv_2"][0]
    for h in range(MH):
        q, kv = uq[:, 192 * h:192 * (h + 1)], ukv[:, 256 * h:256 * (h + 1)]
        row = np.concatenate([units(q[:, :P], 3, P, 1), units(np.concatenate([q[:, P:], q[:, P:]], 1), 3, P, 1),
                              units(kv[:, :P], 2, P, 1), units(kv[:, P:], 2, P, 1)], 2)
        out.append(np.concatenate([row, np.zeros((1, P, UNIT - MLA_U), row.dtype)], 2))
    out.append(units(g["mla_w_o_2"][0], KT, 256, 4))
    out.append(mlp_units(g["mlp_w1_2"][0], g["mlp_w2_2"][0]))
    w1 = g["gla_w_gate1_2"][0]
    z = np.zeros((D, 16), w1.dtype)
    gate = units(np.concatenate([w1[0], z, w1[1], z], 1), KT, P, 1)
    out.append(np.concatenate([gate, np.zeros_like(gate)], 2))
    wq, wk, wv, wr, wo = (g[f"gla_w_{c}_2"][0] for c in "qkvro")
    for h in range(GH):
        out.append(np.concatenate([units(w[:, P * h:P * (h + 1)], KT, P, 1) for w in (wq, wk)], 2))
        out.append(units(wv[:, 256 * h:256 * (h + 1)], KT, 256, 1))
        out.append(units(wr[:, 256 * h:256 * (h + 1)], KT, 256, 1))
        out.append(units(wo[256 * h:256 * (h + 1)], 2, 1024, 1))
    out.append(mlp_units(g["mlp_w1_2"][1], g["mlp_w2_2"][1]))
    a["stream2"] = np.concatenate(out)
    assert a["stream2"].shape == (UNITS_2, P, UNIT)
    w2 = g["gla_w_gate2_2"][0]
    low = np.zeros((GH, 64, P), w2.dtype)
    for d in range(2):
        low[:, 32 * d:32 * d + 16] = w2[d].reshape(16, GH, P).transpose(1, 0, 2)
    a["gla_w2"] = low
    a["gla_b"] = np.ascontiguousarray(g["gla_b_gate_2"][0].reshape(2, GH, P).transpose(1, 2, 0))



def rings(k, sec, kb):
    k.whi = k.at(f"w_hi_{sec}", [P, 2, UNIT], F32R, kb)
    k.wlo = k.at(f"w_lo_{sec}", [P, 2, UNIT], F32R, kb + 16)


def first_block(nc, k, a):
    at = k.at
    b = Bag()
    k.hhi, k.hlo = at("h_hi_1", [P, KT, SEQ], F32R, 60), at("h_lo_1", [P, KT, SEQ], F32R, 76)
    b.cos, b.sin = at("rope_cos", [P, SEQ], F32, 92), at("rope_sin", [P, SEQ], F32, 94)
    b.g, b.inv = at("norm_g1", [P, 4, KT], F32, 96), at("rope_inv", [P, 1], F32, 96.25)
    b.pos_i = at("positions_i", [P, SEQ], I32, 97)
    stage_rope_tables(nc, k, b, a["positions"], a["inv_freq"])

    b.sbq, b.sbk, b.sbv = at("sbq", [P, 4, SEQ], F32, 97), at("sbk", [P, 4, SEQ], F32, 105), at("sbv", [P, QT, 512], F32, 113)
    b.q, b.kk, b.vv = at("q", [P, 4, SEQ], F32, 121), at("kk", [P, 2, SEQ], F32, 129), at("vv", [P, SEQ], F32, 133)
    b.kv_cmp, b.gate_t = at("kv_cmp", [P, 2, SEQ], F32, 135), at("gate_t", [24, SEQ], F32, 139)
    b.qr, b.kr = at("qr", [P, 4, SEQ], F32, 141), at("kr", [P, 2, SEQ], F32, 149)
    b.v, b.gate = at("v", [P, QT, P], F32, 153), at("gate", [P, QT, 24], F32, 155)
    b.kc, b.vc = at("kc", [P, NCP], F32, 155.5), at("vc", [NCP, 64], F32, 155.75)
    half = CMP_T // 2
    b.w2, b.pe = at("w2", [P, 2, 2, P], F32, 156), at("pe", [P, 2, half], F32, 158)
    b.blk = at("blk", [P, 2, half, NCP], F32, 159)
    b.blk_hi, b.blk_lo = at("blk_hi", [P, 2, half, NCP], F32R, 163), at("blk_lo", [P, 2, half, NCP], F32R, 167)
    b.hid = at("cmp_hid", [P, 2, 2, NCP], F32, 171)
    b.pct = at("pct", [NCP, HEADS, SEQ], F32, 157)
    b.cst, b.sst = at("cst", [P, 4, HEADS], F32, 173), at("sst", [P, 2, 5, 2], F32, 173.5)
    b.pc = at("pc", [P, QT, HEADS, NCP], F32, 175)
    b.p, b.pt = at("p", [P, 2, 2, SEQ], F32, 175), at("pt", [P, 2, 2, SEQ], F32, 183)
    b.qst, b.pcst = k.diag[:, 0:SEQ], at("pcst", [NC, 2, SEQ], F32, 47)
    b.onhi, b.onlo = at("on_hi", [P, 4, SEQ], F32R, 191), at("on_lo", [P, 4, SEQ], F32R, 199)
    b.sp, b.tot, b.a = at("sp", [P, QT, SEQ], F32, 121), at("tot", [P, QT + 1, SEQ], F32, 129), at("sba", [P, QT, SEQ], F32, 139)
    b.kst, b.vst = at("kst", [P, SEQ], F32, 147), at("vst", [P, QT, P], F32, 149)
    b.oshi, b.oslo = at("os_hi", [P, 4, SEQ], F32R, 175), at("os_lo", [P, 4, SEQ], F32R, 183)
    b.mhi, b.mlo = at("m_hi", [P, KT, SEQ], F32R, 129), at("m_lo", [P, KT, SEQ], F32R, 145)
    b.gt, b.mt = at("gt", [P, 4, SEQ], F32, 161), at("mt", [P, 2, SEQ], F32, 169)
    y = at("y1", [P, KT, SEQ], F32, 161)
    hid_hi, hid_lo = at("hid_hi1", [P, 4, SEQ], F32R, 129), at("hid_lo1", [P, 4, SEQ], F32R, 137)

    with nc.Fori(0, DEPTH) as layer, k.sem_scope(*k.w_loaded, k.w_hi, k.w_lo):
        stream = lambda n: a["stream1"][layer, n]
        g_loaded = k.sem("g_loaded")
        with nc.Block() as block:
            @block.sync
            def _(sp):
                sp.dma_start(b.g, a["norm_g"][layer]).then_inc(g_loaded, 16)
                sp.wait_ge(g_loaded, 16)
        b.w2_src = [a["cmp_w2"][layer, c] for c in range(2)]
        b.pe_src = [a["cmp_pe"][layer, c] for c in range(2)]
        rings(k, "qkv", 175)
        n = stage_qkv(nc, k, b, stream, 0)
        stage_rope(nc, k, b)
        n = stage_compress(nc, k, b, stream, n)
        stage_cmp_attention(nc, k, b)
        stage_causal_attention(nc, k, b)
        stage_stick_breaking(nc, k, b)
        rings(k, "mix", 97)
        n = stage_merge(nc, k, b, stream, n)
        n = stage_project(nc, k, "wo", stream, n, b.mhi, b.mlo, y, SEQ, UNITS_1)
        n = stage_mlp(nc, k, "ff", stream, n, y, hid_hi, hid_lo, SEQ,
                      [(0, SEQ, b.g[:, 1, :])], [(0, SEQ, b.g[:, 2, :], None)], UNITS_1)
        assert n == UNITS_1
        stage_residual(nc, k, "ffr", y, SEQ, [(0, SEQ, b.g[:, 3, :])])


def build(nc, a):
    with ExitStack() as es:
        k = Bag()
        k.scope = (es, [])

        def sem(name):
            stack, sems = k.scope
            sems.append(stack.enter_context(nc.semaphore(name)))
            return sems[-1]

        @contextmanager
        def sem_scope(*more):
            outer = k.scope
            with ExitStack() as stack:
                k.scope = (stack, [])
                yield
                with nc.Block() as block:
                    @block.sync
                    def _(sp):
                        for s in [*k.scope[1], *more]:
                            sp.sem_clear(s)
                k.scope = outer

        k.sem, k.sem_scope = sem, sem_scope
        k.w_loaded = [sem(f"w_loaded{i}") for i in range(2)]
        k.w_hi, k.w_lo = sem("w_hi"), sem("w_lo")
        k.ps = es.enter_context(nc.psum_tensor("ps", [P, 4096], F32))[:]
        origin = -(-nc.sbuf_base // 32) * 32

        def at(name, shape, dt, kb):
            return nc.alloc_sbuf_tensor_at(name, shape, dt, offset=origin + int(kb * 1024))[:]

        k.at = at
        consts = at("consts", [P, len(CONSTS) * P], F32, 0)
        k.c = {n: consts[:, i * P:(i + 1) * P] for i, n in enumerate(CONSTS)}
        k.x = at("x", [P, KT, TOK], F32, 7)
        k.raw = at("w_raw", [P, 2, UNIT], F32, 31)
        k.sqt, k.acc, k.diag = at("sq", [P, 2, TOK], F32, 47), at("acc", [P, TOK], F32, 53), at("diag", [P, TOK], F32, 56)
        k.nst = at("norm_stat", [P, 3, 8], F32, 59)

        start = sem("inputs_loaded")
        with nc.Block() as block:
            @block.sync
            def _(sp):
                sp.dma_start(k.x[:, :, 0:SEQ], a["x"]).then_inc(start, 16)
                sp.dma_start(k.x[:, :, SEQ:TOK], a["ctx"]).then_inc(start, 16)
                sp.dma_start(consts, a["consts"]).then_inc(start, 16)
                sp.wait_ge(start, 48)

        if FIRST:
            first_block(nc, k, a)
        if SECOND:
            second_block(nc, k, a)

        stored = sem("stored")
        with nc.Block() as block:
            @block.sync
            def _(sp):
                sp.dma_start(a["out"], k.x[:, :, 0:SEQ]).then_inc(stored, 16)
                sp.wait_ge(stored, 16)


FIRST, SECOND = True, True


def feature_major(t):
    n, d = t.shape
    return np.ascontiguousarray(t.T.reshape(d // P, P, n).transpose(1, 0, 2))


def units(w, kt, cols, n):
    w = np.concatenate([w, np.zeros((w.shape[0], n * cols - w.shape[1]), w.dtype)], 1) if w.shape[1] < n * cols else w
    return w.reshape(kt, P, n, cols).transpose(2, 1, 0, 3).reshape(n, P, kt * cols)


def mlp_units(w1, w2):
    out = []
    for g in range(FF_GROUPS):
        out.append(units(w1[:, 512 * g:512 * (g + 1)], KT, 256, 2))
        out.append(units(w2[512 * g:512 * (g + 1)], 4, 512, 2))
    return np.concatenate(out)


def stream_1(w_in, cmp_w1, w_nsa_o, w_sb_o, w_out, w_ff1, w_ff2):
    pad = np.zeros((D, 104), w_in.dtype)
    qkv = np.concatenate([w_in[:, :920], pad, w_in[:, 920:2456]], 1)
    out = [units(qkv, KT, 256, UNITS_QKV)]
    for c in range(2):
        w = cmp_w1[c].reshape(16, P, 256)
        out.append(w.reshape(2, 8, P, 256).transpose(0, 2, 1, 3).reshape(2, P, UNIT))
    gates = units(w_in[:, 2456:], KT, 256, 8)
    no, so = units(w_nsa_o, 4, 256, 4), units(w_sb_o, 4, 256, 4)
    for pr in range(4):
        out.append(np.stack([gates[pr], gates[4 + pr], np.concatenate([no[pr], so[pr]], 1)]))
    out.append(units(w_out, KT, 256, 4))
    out.append(mlp_units(w_ff1, w_ff2))
    out = np.concatenate(out)
    assert out.shape == (UNITS_1, P, UNIT)
    return out


def host_arrays(i):
    g = {n: np.asarray(v) for n, v in i.items()}
    a = {}
    a["x"] = feature_major(g["x"][0])
    a["ctx"] = feature_major(g["ctx_2"][0])
    a["positions"] = np.ascontiguousarray(g["positions"][0])
    a["consts"] = const_table()
    a["inv_freq"] = inv_freq_column()
    a["norm_g"] = np.ascontiguousarray(g["norm_g"].reshape(DEPTH, 4, KT, P).transpose(0, 3, 1, 2))
    a["cmp_pe"] = np.ascontiguousarray(g["cmp_pe"].reshape(DEPTH, 2, 16, P).transpose(0, 1, 3, 2))
    a["cmp_w2"] = g["cmp_w2"]
    a["stream1"] = np.stack([stream_1(*(g[n][l] for n in ("w_in", "cmp_w1", "w_nsa_o", "w_sb_o", "w_out", "w_ff1", "w_ff2")))
                             for l in range(DEPTH)])
    if SECOND:
        second_arrays(g, a)
    return a


def kernel(**inputs):
    import concourse.bacc as _bacc
    from concourse.bass_utils import run_bass_kernel_spmd as _run

    nc = _bacc.Bacc("TRN2", target_bir_lowering=False, num_devices=1)
    arrays = {f"in_{n}": np.ascontiguousarray(v) for n, v in host_arrays(inputs).items()}
    a = {n[3:]: nc.dram_tensor(n, v.shape, mybir.dt.from_np(v.dtype), kind="ExternalInput").ap() for n, v in arrays.items()}
    a["out"] = nc.dram_tensor("out", (P, KT, SEQ), F32, kind="ExternalOutput").ap()
    build(nc, a)
    r = _run(nc, [arrays], core_ids=[0])
    got = r.results[0]["out"]
    return np.ascontiguousarray(got.transpose(1, 0, 2).reshape(D, SEQ).T).reshape(1, SEQ, D)
```

```python
from contextlib import ExitStack, contextmanager

import numpy as np
import concourse.bass as bass
from concourse import mybir

F32 = mybir.dt.float32
F32R = mybir.dt.float32r
I32 = mybir.dt.int32
U32 = mybir.dt.uint32
ALU = mybir.AluOpType
ACT = mybir.ActivationFunctionType
AX_X = mybir.AxisListType.X

P = 128
D = 1024
KT = D // P
SEQ = 512
CTX = 256
TOK = SEQ + CTX
DEPTH = 2
UNIT = 2048
EPS = 1e-6
NEG = -1e30

HD = 64
HEADS = 8
SBH = 4
CMP_T, CMP_S = 32, 16
NC = (SEQ - CMP_T) // CMP_S + 1
NCP = 32
QT = SEQ // P
UNITS_QKV = 10
UNITS_CMP = 4
UNITS_MERGE = 12
UNITS_OUT = 4
FF_GROUPS = 8
UNITS_FF = 4 * FF_GROUPS
UNITS_1 = UNITS_QKV + UNITS_MERGE + UNITS_OUT + UNITS_FF

ADA_TURNS = 6 * DEPTH
U_ADA = 24
ADA_PER = U_ADA // FF_GROUPS
MH = 8
MLA_U = 1024
GH = 4
CH = 64

CONSTS = ["ident", "negtri", "negones", "ones", "sbneg", "sb01", "causal", "cmpneg", "cmpvis",
          "rope_perm", "axial_perm", "gla_f", "gla_b", "small"]


def const_table():
    r = np.arange(P)
    t = {}
    t["ident"] = np.eye(P)
    t["negtri"] = -(r[:, None] >= r[None, :]).astype(float)
    t["negones"] = -np.ones((P, P))
    t["ones"] = np.ones((P, P))
    t["sbneg"] = np.where(r[:, None] < r[None, :], 0.0, NEG)
    t["sb01"] = (r[:, None] < r[None, :]).astype(float)
    t["causal"] = np.where(r[None, :] <= r[:, None], 0.0, NEG)
    c = np.arange(NCP)
    vis = np.stack([(CMP_S * c[None, :] + CMP_T - 1 <= (q * P + r)[:, None]) & (c[None, :] < NC)
                    for q in range(QT)], 1)
    t["cmpvis"] = vis.astype(float).reshape(P, P)
    t["cmpneg"] = np.where(vis, 0.0, NEG).reshape(P, P)
    rp = np.zeros((P, P))
    for b in range(0, P, HD):
        for i in range(8):
            rp[b + i + 8, b + i] = -1.0
            rp[b + i, b + i + 8] = 1.0
    t["rope_perm"] = rp
    ap = np.zeros((P, P))
    for b in range(0, P, 32):
        for i in range(16):
            ap[b + i + 16, b + i] = -1.0
            ap[b + i, b + i + 16] = 1.0
    t["axial_perm"] = ap
    same = (r[:, None] // CH) == (r[None, :] // CH)
    t["gla_f"] = (same & (r[:, None] <= r[None, :])).astype(float)
    t["small"] = np.zeros((P, P))
    t["small"][:, 0] = EPS
    t["small"][:, 1:3] = r[:, None] % 2 == r[None, 0:2]
    t["gla_b"] = (same & (r[:, None] >= r[None, :])).astype(float)
    return np.concatenate([t[n] for n in CONSTS], 1).astype(np.float32)


def axial_table():
    f = np.float32
    inv = (f(10000.0) ** (-np.arange(0, 32, 2, dtype=f) / f(32))).astype(f)
    tok = np.arange(SEQ)
    row, col = (tok // 64).astype(f), (tok % 64).astype(f)
    ang = np.concatenate([row[None] * inv[:, None]] * 2 + [col[None] * inv[:, None]] * 2, 0)
    ang = np.concatenate([ang, ang], 0)
    return np.stack([np.cos(ang), np.sin(ang)], 1).astype(f)


def inv_freq_column():
    inv = np.power(np.float32(500000.0), np.arange(8, dtype=np.float32) * np.float32(-2.0 / 16)).astype(np.float32)
    r = np.arange(P) % HD
    return np.where(r < 16, inv[r % 8], 0).astype(np.float32).reshape(P, 1)


class Bag:
    pass



def load_unit(sp, k, n, src, width=UNIT, it=0, per=0):
    if n >= 2:
        sp.wait_ge(k.w_hi, n - 1 + per * it)
        sp.wait_ge(k.w_lo, n - 1 + per * it)
    sp.dma_start(k.raw[:, n % 2, 0:width], src).then_inc(k.w_loaded[n % 2], 16)


def split_hi(act, k, n, used=None, width=UNIT, it=0, per=0):
    act.wait_ge(k.w_loaded[n % 2], 16 * (n // 2 + 1) + 8 * per * it)
    if used is not None:
        act.wait_ge(*used)
    act.activation(k.whi[:, n % 2, 0:width], k.raw[:, n % 2, 0:width], ACT.Copy).then_inc(k.w_hi, 1)


def split_lo(dve, k, n, width=UNIT, it=0, per=0):
    dve.wait_ge(k.w_hi, n + 1 + per * it)
    dve.tensor_tensor(k.wlo[:, n % 2, 0:width], k.raw[:, n % 2, 0:width],
                      k.whi[:, n % 2, 0:width].bitcast(F32), ALU.subtract).then_inc(k.w_lo, 1)


def unit_ready(pe, k, n, it=0, per=0):
    pe.wait_ge(k.w_lo, n + 1 + per * it)


def mm3(pe, outs, whi, wlo, xs, start, stop):
    for c, (out, (xhi, xlo)) in enumerate(zip(outs, xs)):
        pe.matmul(out, whi, xhi, start=start, stop=False)
        pe.matmul(out, whi, xlo, start=False, stop=False)
    for out, (xhi, xlo) in zip(outs, xs):
        last = pe.matmul(out, wlo, xhi, start=False, stop=stop)
    return last


def chunks(t):
    return [(0, 512)] if t == 512 else [(0, 512), (512, 256)]


def tile_out(k, slot, tok):
    base = slot * 512 * len(chunks(tok))
    return base, [k.ps[:, base + c0:base + c0 + w] for c0, w in chunks(tok)]


def dense_tile(pe, k, outs, w_tiles, x_hi, x_lo, tok, x_wait=None):
    for i, (whi, wlo) in enumerate(w_tiles):
        if x_wait is not None:
            x_wait(i)
        xs = [(x_hi[:, i, c0:c0 + w], x_lo[:, i, c0:c0 + w]) for c0, w in chunks(tok)]
        last = mm3(pe, outs, whi, wlo, xs, i == 0, i == len(w_tiles) - 1)
    return last


def unit_tiles(k, n, off, kt, cols, m):
    out = []
    for i in range(kt):
        a = off + i * cols + m * P
        out.append((k.whi[:, n % 2, a:a + P], k.wlo[:, n % 2, a:a + P]))
    return out



class Norm:

    NAMES = ("squared", "summed", "root", "column", "inverse", "diag", "spread")

    def __init__(self, k, name, src, kt, tok, bank, it=0, sems=None):
        self.k, self.src, self.kt, self.tok, self.bank, self.it = k, src, kt, tok, bank, it
        self.nt = tok // P
        self.name = name
        self.sems = sems or [k.sem(f"{name}_{s}") for s in self.NAMES]
        self.squared, self.summed, self.root, self.column, self.inverse, self.diag, self.spread = self.sems
        self.sums = self.rb = k.ps[:, bank * 512:bank * 512 + tok]
        self.stat = k.ps[:, 3584:3584 + self.nt]

    def at(self, it):
        return Norm(self.k, self.name, self.src, self.kt, self.tok, self.bank, it, self.sems)

    def act_square(self, act, t):
        k, tok = self.k, self.tok
        if t >= 2:
            act.wait_ge(self.summed, t - 1 + self.kt * self.it)
        act.activation(k.sqt[:, t % 2, 0:tok], self.src[:, t, 0:tok], ACT.Square,
                       scale=float((self.kt * P) ** -0.5)).then_inc(self.squared, 1)

    def act_table(self, act):
        act.activation(self.k.tiny, self.k.c["ones"][:, 0:1], ACT.Sqrt)

    def act_root(self, act):
        act.wait_ge(self.summed, self.kt * (self.it + 1))
        act.activation(self.k.root[:, 0:self.tok], self.sums[0:1, :], ACT.Sqrt,
                       bias=self.k.c["eps"][0:1, 0:1]).then_inc(self.root, 1)

    def act_all(self, act, before=None):
        for t in range(self.kt):
            if before is not None:
                before(act, t)
            self.act_square(act, t)
            if t == 0:
                self.act_table(act)
        self.act_root(act)

    def pe_add(self, pe, t):
        k = self.k
        pe.wait_ge(self.squared, t + 1 + self.kt * self.it)
        for c0, w in chunks(self.tok):
            last = pe.matmul(self.sums[:, c0:c0 + w], k.c["ones"], k.sqt[:, t % 2, c0:c0 + w],
                             start=t == 0, stop=t == self.kt - 1)
        last.then_inc(self.summed, 1)

    def pe_all(self, pe):
        for t in range(self.kt):
            self.pe_add(pe, t)
        self.pe_spread(pe)

    def pe_spread(self, pe):
        pe.wait_ge(self.root, 1 + self.it)
        for j in range(self.nt):
            last = pe.matmul(self.stat[:, j:j + 1], self.k.root[:, j * P:(j + 1) * P], self.k.c["ones"][0:1, 0:1],
                             start=True, stop=True)
        last.then_inc(self.column, 1)
        for j in range(self.nt):
            pe.wait_ge(self.diag, j + 1 + self.nt * self.it)
            last = pe.matmul(self.rb[:, j * P:(j + 1) * P], self.k.c["ones"], self.k.diag[:, j * P:(j + 1) * P],
                             start=True, stop=True)
        last.then_inc(self.spread, 1)

    def dve_all(self, dve):
        k = self.k
        dve.wait_ge(self.column, 1 + self.it)
        dve.reciprocal(k.nst[:, 0:self.nt], self.stat).then_inc(self.inverse, 1)
        dve.wait_ge(self.inverse, 1 + self.it)
        for j in range(self.nt):
            dve.tensor_scalar(k.diag[:, j * P:(j + 1) * P], k.c["ident"], k.nst[:, j:j + 1], None,
                              ALU.mult).then_inc(self.diag, 1)
        dve.wait_ge(self.spread, 1 + self.it)


class Normed:

    def __init__(self, k, name, norm, hi, lo, parts):
        self.k, self.norm, self.hi, self.lo, self.parts = k, norm, hi, lo, parts
        self.scaled, self.hi_done, self.lo_done = [k.sem(f"{name}_{s}") for s in ("scaled", "hi_done", "lo_done")]

    def dve(self, dve):
        k, n = self.k, self.norm
        kt = n.kt
        np_ = len(self.parts)

        def lo(t):
            dve.wait_ge(self.hi_done, np_ * (t + 1))
            for c0, w, scale, shift in self.parts:
                src = k.sqt[:, t % 2, c0:c0 + w]
                hi = self.hi[:, t, c0:c0 + w].bitcast(F32)
                dst = self.lo[:, t, c0:c0 + w]
                if shift is None:
                    dve.tensor_tensor(dst, src, hi, ALU.subtract).then_inc(self.lo_done, 1)
                else:
                    dve.scalar_tensor_tensor(dst, src, shift[:, t:t + 1], hi, ALU.add,
                                             ALU.subtract).then_inc(self.lo_done, 1)

        for t in range(kt):
            if t >= 2:
                dve.wait_ge(self.lo_done, np_ * (t - 1))
            for c0, w, scale, shift in self.parts:
                dve.scalar_tensor_tensor(k.sqt[:, t % 2, c0:c0 + w], n.src[:, t, c0:c0 + w],
                                         scale[:, t:t + 1], n.rb[:, c0:c0 + w], ALU.mult,
                                         ALU.mult).then_inc(self.scaled, 1)
            if t >= 1:
                lo(t - 1)
        lo(kt - 1)

    def act(self, act):
        k, n = self.k, self.norm
        np_ = len(self.parts)
        for t in range(n.kt):
            act.wait_ge(self.scaled, np_ * (t + 1))
            for c0, w, scale, shift in self.parts:
                act.activation(self.hi[:, t, c0:c0 + w], k.sqt[:, t % 2, c0:c0 + w], ACT.Identity,
                               bias=0.0 if shift is None else shift[:, t:t + 1]).then_inc(self.hi_done, 1)

    def pe_wait(self, pe, t):
        pe.wait_ge(self.lo_done, len(self.parts) * (t + 1))


class Residual:

    def __init__(self, k, name, norm, x, parts):
        self.k, self.norm, self.x, self.parts = k, norm, x, parts
        self.scaled, self.even, self.odd = [k.sem(f"{name}_{s}") for s in ("scaled", "even", "odd")]

    def add(self, e, t, sem):
        n = self.norm
        e.wait_ge(self.scaled, len(self.parts) * (t + 1))
        e.tensor_tensor(self.x[:, t, 0:n.tok], self.x[:, t, 0:n.tok], n.src[:, t, 0:n.tok], ALU.add).then_inc(sem, 1)

    def dve(self, dve):
        n = self.norm
        for t in range(n.kt):
            for c0, w, scale in self.parts:
                dve.scalar_tensor_tensor(n.src[:, t, c0:c0 + w], n.src[:, t, c0:c0 + w], scale[:, t:t + 1],
                                         n.rb[:, c0:c0 + w], ALU.mult, ALU.mult).then_inc(self.scaled, 1)
            if t % 2:
                self.add(dve, t - 1, self.even)

    def pool(self, pool):
        for t in range(1, self.norm.kt, 2):
            self.add(pool, t, self.odd)

    def wait(self, e, t):
        e.wait_ge(self.odd if t % 2 else self.even, t // 2 + 1)


def split_first(dve, k, n, count=2, width=UNIT):
    for m in range(n, n + count):
        dve.wait_ge(k.w_loaded[m % 2], 16 * (m // 2 + 1))
        dve.tensor_copy(k.whi[:, m % 2, 0:width], k.raw[:, m % 2, 0:width]).then_inc(k.w_hi, 1)
    for m in range(n, n + count):
        split_lo(dve, k, m, width)


def first_tiles(pe, k, n, cols, count, tok, x_wait, ready):
    outs = [tile_out(k, j, tok)[1] for j in range(count)]
    w = [unit_tiles(k, n, 0, KT, cols, j) for j in range(count)]
    for i in range(KT):
        x_wait(i)
        xs = [(k.hhi[:, i, c0:c0 + cw], k.hlo[:, i, c0:c0 + cw]) for c0, cw in chunks(tok)]
        for j in range(count):
            last = mm3(pe, outs[j], *w[j][i], xs, i == 0, i == KT - 1)
            if i == KT - 1:
                last.then_inc(ready, 1)



def stage_qkv(nc, k, b, stream, first_unit):
    norm = Norm(k, "n1", k.x, KT, SEQ, 5)
    normed = Normed(k, "h1", norm, k.hhi, k.hlo, [(0, SEQ, b.g[:, 0, :], None)])
    ready, taken = k.sem("qkv_ready"), k.sem("qkv_taken")
    ring, tiles = 4, 2 * UNITS_QKV - 4 + 2 * QT
    n0 = first_unit
    g_loaded = k.sem("g_loaded")

    with nc.Block() as block:
        @block.sync
        def _(sp):
            sp.dma_start(b.g, b.g_src).then_inc(g_loaded, 16)
            for n in range(n0, n0 + UNITS_QKV + 2):
                load_unit(sp, k, n, stream(n))

        @block.tensor
        def _(pe):
            norm.pe_all(pe)
            unit_ready(pe, k, n0)
            first_tiles(pe, k, n0, 256, 2, SEQ, lambda i: normed.pe_wait(pe, i), ready)
            j = 2
            for u in range(1, UNITS_QKV):
                n = n0 + u
                unit_ready(pe, k, n)
                if u < UNITS_QKV - 2:
                    for m in range(2):
                        if j >= ring:
                            pe.wait_ge(taken, j - ring + 1)
                        _, outs = tile_out(k, j % ring, SEQ)
                        last = dense_tile(pe, k, outs, unit_tiles(k, n, 0, KT, 256, m), k.hhi, k.hlo, SEQ)
                        last.then_inc(ready, 1)
                        j += 1
                else:
                    for t in range(QT):
                        pe.wait_ge(taken, j - ring + 1)
                        out = k.ps[:, (j % ring) * 512:(j % ring) * 512 + 256]
                        for i in range(KT):
                            w = (k.whi[:, n % 2, i * 256:(i + 1) * 256], k.wlo[:, n % 2, i * 256:(i + 1) * 256])
                            last = mm3(pe, [out], k.hhi[:, i, t * P:(t + 1) * P], k.hlo[:, i, t * P:(t + 1) * P],
                                       [w], i == 0, i == KT - 1)
                        last.then_inc(ready, 1)
                        j += 1

        @block.vector
        def _(dve):
            split_first(dve, k, n0)
            norm.dve_all(dve)
            dve.wait_ge(g_loaded, 16)
            normed.dve(dve)
            for u in range(2, UNITS_QKV):
                split_lo(dve, k, n0 + u)

        @block.scalar
        def _(act):
            norm.act_all(act)
            normed.act(act)
            j = 0

            def out(pairs, scale=1.0):
                nonlocal j
                act.wait_ge(ready, j + 1)
                for i, (dst, rows, cols) in enumerate(pairs):
                    last = act.activation(dst, k.ps[rows, (j % ring) * 512 + cols.start:(j % ring) * 512 + cols.stop],
                                          ACT.Copy, scale=scale)
                last.then_inc(taken, 1)
                j += 1

            every, lower, upper, full = slice(0, P), slice(0, 64), slice(64, P), slice(0, SEQ)
            for u in range(UNITS_QKV):
                for m in range(2 if u < 8 else QT):
                    if u < 2:
                        out([(b.q[:, 2 * u + m, :], every, full)])
                    elif u == 2 and m == 0:
                        out([(b.kv_cmp[0:64, 0, :], lower, full), (b.kv_cmp[64:P, 0, 0:SEQ - 1], lower, slice(1, SEQ)),
                             (b.kv_cmp[0:64, 1, :], upper, full), (b.kv_cmp[64:P, 1, 0:SEQ - 1], upper, slice(1, SEQ))])
                    elif u == 2:
                        out([(b.kk[0:64, 0, :], lower, full), (b.kk[64:P, 0, :], lower, full), (b.vv[0:64, :], upper, full)])
                    elif u == 3 and m == 0:
                        out([(b.kk[0:64, 1, :], lower, full), (b.kk[64:P, 1, :], lower, full), (b.vv[64:P, :], upper, full)])
                    elif u == 3:
                        out([(b.gate_t[0:24, :], slice(0, 24), full)])
                    elif u < 6:
                        out([(b.sbq[:, 2 * (u - 4) + m, :], every, full)], scale=float(np.float32(128.0 ** -0.5)))
                    elif u < 8:
                        out([(b.sbk[:, 2 * (u - 6) + m, :], every, full)])
                    else:
                        out([(b.sbv[:, m, 256 * (u - 8):256 * (u - 7)], every, slice(0, 256))])
                if u + 2 < UNITS_QKV:
                    split_hi(act, k, n0 + u + 2, (ready, j))
    assert tiles == 24
    return n0 + UNITS_QKV


def stage_rope(nc, k, b):
    turned, half1, half2, rotated = k.sem("rope_turned"), k.sem("rope_cos"), k.sem("rope_sin"), k.sem("rope_done")
    gated, flipped = k.sem("gate_sigmoid"), k.sem("value_flipped")
    srcs = [b.q[:, i, :] for i in range(4)] + [b.kk[:, i, :] for i in range(2)]
    dsts = [b.qr[:, i, :] for i in range(4)] + [b.kr[:, i, :] for i in range(2)]
    b.cw_loaded, b.small_loaded = [k.sem(f"cmp_w_loaded{u}") for u in range(4)], k.sem("cmp_small_loaded")
    with nc.Block() as block:
        @block.sync
        def _(sp):
            for u in range(2):
                sp.dma_start(b.cw[:, u, :], b.cw_src[u]).then_inc(b.cw_loaded[u], 16)
            for c in range(2):
                for r in range(2 if c == 0 else 1):
                    sp.dma_start(b.w2[:, c, :, 64 * r:64 * r + 64],
                                 b.w2_src[c].rearrange("(h p) n -> p h n", p=P)).then_inc(b.small_loaded, 16)
                sp.dma_start(b.pe[:, c, :], b.pe_src[c]).then_inc(b.small_loaded, 16)
            for u in range(2, 4):
                sp.dma_start(b.cw[:, u, :], b.cw_src[u]).then_inc(b.cw_loaded[u], 16)

        @block.tensor
        def _(pe):
            for i, src in enumerate(srcs):
                pe.matmul(k.ps[:, i * 512:(i + 1) * 512], k.c["rope_perm"], src, start=True, stop=True).then_inc(turned, 1)
            for t in range(QT):
                pe.transpose(k.ps[:, 3072 + t * P:3072 + (t + 1) * P], b.vv[:, t * P:(t + 1) * P], k.c["ident"]).then_inc(flipped, 1)
            pe.wait_ge(gated, 1)
            for t in range(QT):
                pe.transpose(k.ps[:, 3584 + t * 24:3584 + (t + 1) * 24], b.gate_t[0:24, t * P:(t + 1) * P],
                             k.c["ident"][0:24, 0:24]).then_inc(flipped, 1)

        @block.gpsimd
        def _(pool):
            for i, src in enumerate(srcs):
                if i >= 2:
                    pool.wait_ge(rotated, i - 1)
                pool.tensor_tensor(k.sqt[:, i % 2, 0:SEQ], src, b.cos, ALU.mult).then_inc(half1, 1)

        @block.vector
        def _(dve):
            for i, dst in enumerate(dsts):
                dve.wait_ge(turned, i + 1)
                if i:
                    dve.wait_ge(rotated, i)
                dve.tensor_tensor(k.acc[:, 0:SEQ], k.ps[:, i * 512:(i + 1) * 512], b.sin, ALU.mult).then_inc(half2, 1)
                dve.wait_ge(half2, i + 1)
                dve.wait_ge(half1, i + 1)
                dve.tensor_tensor(dst, k.acc[:, 0:SEQ], k.sqt[:, i % 2, 0:SEQ], ALU.add).then_inc(rotated, 1)

        @block.scalar
        def _(act):
            act.activation(b.gate_t[0:24, :], b.gate_t[0:24, :], ACT.Sigmoid).then_inc(gated, 1)
            act.wait_ge(flipped, QT)
            act.activation(b.v[:, :, :].rearrange("p a b -> p (a b)"), k.ps[:, 3072:3584], ACT.Copy)
            act.wait_ge(flipped, 2 * QT)
            act.activation(b.gate[:, :, :].rearrange("p a b -> p (a b)"), k.ps[:, 3584:3584 + 96], ACT.Copy)


def stage_compress(nc, k, b):
    added, hidden, gelu, turned, copied, outs_ready = (
        k.sem(f"cmp_{s}") for s in ("pe_added", "hidden", "gelu", "turned", "copied", "out"))
    half = CMP_T // 4
    with nc.Block() as block:
        @block.vector
        def _(dve):
            dve.wait_ge(b.small_loaded, 80)
            for c in range(2):
                view = b.kv_cmp[:, c, :].rearrange("p (c r) -> p r c", r=CMP_S)
                for h in range(2):
                    dve.tensor_tensor(b.blk[:, c, h * half:(h + 1) * half, 0:NC],
                                      view[:, 0:CMP_S:2, h:h + NC],
                                      b.pe[:, c, h * half:(h + 1) * half].unsqueeze(2).to_broadcast([P, half, NC]),
                                      ALU.add).then_inc(added, 1)

        @block.tensor
        def _(pe):
            def first_layer(c):
                for u in range(2):
                    pe.wait_ge(added, 2 * c + u + 1)
                    pe.wait_ge(b.cw_loaded[2 * c + u], 16)
                    for i in range(8):
                        last = pe.matmul(k.ps[0:NC, c * 512:c * 512 + 256], b.blk[:, c, 8 * u + i, 0:NC],
                                         b.cw[:, 2 * c + u, i * 256:(i + 1) * 256],
                                         start=u == 0 and i == 0, stop=u == 1 and i == 7)
                last.then_inc(hidden, 1)

            def turn(c):
                pe.wait_ge(gelu, c + 1)
                for h in range(2):
                    last = pe.transpose(k.ps[:, 1024 + 512 * c + h * NCP:1024 + 512 * c + h * NCP + NC],
                                        b.hid_row[:, c, h * P:(h + 1) * P], k.c["ident"][0:NC, 0:NC])
                last.then_inc(turned, 1)

            first_layer(0)
            first_layer(1)
            turn(0)
            turn(1)
            pe.wait_ge(copied, 1)
            for h in range(2):
                last = pe.matmul(k.ps[:, 2048:2048 + NC], b.w2[:, 0, h, :], b.hid[:, 0, h, 0:NC], start=h == 0, stop=h == 1)
            last.then_inc(outs_ready, 1)
            pe.wait_ge(copied, 2)
            for h in range(2):
                last = pe.matmul(k.ps[0:NC, 2560:2560 + 64], b.hid[:, 1, h, 0:NC], b.w2[:, 1, h, 0:64], start=h == 0, stop=h == 1)
            last.then_inc(outs_ready, 1)

        @block.scalar
        def _(act):
            for c in range(2):
                act.wait_ge(hidden, c + 1)
                act.activation(b.hid_row[:, c, :], k.ps[0:NC, c * 512:c * 512 + 256], ACT.Gelu_apprx_tanh).then_inc(gelu, 1)
            for c in range(2):
                act.wait_ge(turned, c + 1)
                src = k.ps[:, 1024 + 512 * c:1024 + 512 * c + 2 * NCP].rearrange("p (h c) -> p h c", c=NCP)
                act.activation(b.hid[:, c, :, 0:NC], src[:, :, 0:NC], ACT.Copy).then_inc(copied, 1)
            act.wait_ge(outs_ready, 1)
            act.activation(b.kc[:, 0:NC], k.ps[:, 2048:2048 + NC], ACT.Copy)
            act.wait_ge(outs_ready, 2)
            act.activation(b.vc[0:NC, :], k.ps[0:NC, 2560:2560 + 64], ACT.Copy)


def stage_cmp_attention(nc, k, b):
    scored, masked, expd, probs, flipped, chain = (
        k.sem(f"ca_{s}") for s in ("scored", "masked", "exp", "probs", "flipped", "chain"))
    with nc.Block() as block:
        @block.tensor
        def _(pe):
            for t in range(QT):
                for h in range(HEADS):
                    r = slice(64 * (h % 2), 64 * (h % 2) + 64)
                    a = t * 512 + 2048 * (h % 2) + h // 2 * NCP
                    last = pe.matmul(k.ps[:, a:a + NC], b.q[r, h // 2, t * P:(t + 1) * P], b.kc[r, 0:NC],
                                     start=True, stop=True)
                last.then_inc(scored, 1)
            for t in range(QT):
                pe.wait_ge(probs, t + 1)
                for h in range(HEADS):
                    a = t * 512 + 2048 * (h // 4) + h % 4 * P
                    last = pe.transpose(k.ps[0:NC, a:a + P], b.pc[:, t, h, 0:NC], k.c["ident"])
                last.then_inc(flipped, 1)

        @block.vector
        def _(dve):
            n = 0

            def link(ins):
                nonlocal n
                n += 1
                ins.then_inc(chain, 1)
                dve.wait_ge(chain, n)

            for t in range(QT):
                s = b.pc[:, t, :, 0:NC]
                neg = k.c["cmpneg"][:, t * NCP:t * NCP + NC].unsqueeze(1).to_broadcast([P, HEADS // 2, NC])
                vis = k.c["cmpvis"][:, t * NCP:t * NCP + NC].unsqueeze(1).to_broadcast([P, HEADS, NC])
                dve.wait_ge(scored, t + 1)
                for odd in range(2):
                    a = t * 512 + 2048 * odd
                    ps = k.ps[:, a:a + HEADS // 2 * NCP].rearrange("p (h c) -> p h c", c=NCP)[:, :, 0:NC]
                    ins = dve.tensor_tensor(b.pc[:, t, odd:HEADS:2, 0:NC], ps, neg, ALU.add)
                    link(ins)
                link(dve.tensor_reduce(b.cst[:, 0, :], s, AX_X, ALU.max))
                dve.tensor_tensor(s, s, b.cst[:, 0, :].unsqueeze(2).to_broadcast([P, HEADS, NC]),
                                  ALU.subtract).then_inc(masked, 1)
                dve.wait_ge(expd, t + 1)
                link(dve.tensor_reduce(b.cst[:, 1, :], s, AX_X, ALU.add))
                link(dve.reciprocal(b.cst[:, 2, :], b.cst[:, 1, :]))
                gate = b.gate[:, t, :].rearrange("p (h c) -> p h c", c=3)[:, :, 0]
                link(dve.tensor_tensor(b.cst[:, 3, :], b.cst[:, 2, :], gate, ALU.mult))
                link(dve.tensor_tensor(s, s, b.cst[:, 3, :].unsqueeze(2).to_broadcast([P, HEADS, NC]), ALU.mult))
                dve.tensor_tensor(s, s, vis, ALU.mult).then_inc(probs, 1)

        @block.scalar
        def _(act):
            def copy(t):
                act.wait_ge(flipped, t + 1)
                for g in range(2):
                    a = t * 512 + 2048 * g
                    act.activation(b.pct[0:NC, 4 * g:4 * g + 4, t * P:(t + 1) * P],
                                   k.ps[0:NC, a:a + 512].rearrange("p (h q) -> p h q", q=P), ACT.Copy)

            for t in range(QT):
                act.wait_ge(masked, t + 1)
                s = b.pc[:, t, :, 0:NC]
                act.activation(s, s, ACT.Exp, scale=HD ** -0.5).then_inc(expd, 1)
                if t:
                    copy(t - 1)
            copy(QT - 1)


def stage_causal_attention(nc, k, b):
    names = ("staged", "scored", "maxed", "expd", "scaled", "flipped", "copied_a", "copied_v", "summed", "hi_done",
             "lo_done", "chain")
    s = {n: k.sem(f"sa_{n}") for n in names}
    U = 2 * QT
    T = [*range(QT), *range(QT)[::-1]]
    LINKS = 4 * U
    vcols = lambda br: slice(64 * br, 64 * br + 64)
    with nc.Block() as block:
        @block.tensor
        def _(pe):
            with pe.Fori(0, HEADS // 2) as it:
                def scores(u):
                    h, t = u // QT, T[u]
                    w = (t + 1) * P
                    r = slice(64 * h, 64 * h + 64)
                    if u == 0:
                        pe.wait_ge(s["staged"], 2 * it + 1)
                    pe.wait_ge(s["expd"], U * it + max(u - 1, 0))
                    for br in range(2):
                        a = (u % 2) * 1024 + br * 512
                        last = pe.matmul(k.ps[:, a:a + w], b.qst[r, t * P:(t + 1) * P], b.kr[r, br, 0:w],
                                         start=True, stop=True)
                    last.then_inc(s["scored"], 1)

                def flips(u):
                    t = T[u]
                    pe.wait_ge(s["scaled"], U * it + u + 1)
                    pe.wait_ge(s["copied_a"], U * it + u)
                    pe.wait_ge(s["copied_v"], U * it + u)
                    for br in range(2):
                        for j in range(t + 1):
                            a = 2048 + br * 512 + j * P
                            last = pe.transpose(k.ps[:, a:a + P], b.p[:, u % 2, br, j * P:(j + 1) * P], k.c["ident"])
                    last.then_inc(s["flipped"], 1)

                def values(u):
                    h, t = u // QT, T[u]
                    rows = slice(64 * h, 64 * h + 64)
                    out = k.ps[rows, 3072 + t * P:3072 + (t + 1) * P]
                    if u == 0:
                        pe.wait_ge(s["lo_done"], it)
                        pe.wait_ge(s["staged"], 2 * it + 2)
                    pe.matmul(out, b.vc[0:NC, :], b.pcst[:, h, t * P:(t + 1) * P], start=True, stop=False)
                    pe.wait_ge(s["copied_a"], U * it + u + 1)
                    pe.wait_ge(s["copied_v"], U * it + u + 1)
                    for br in range(2):
                        for j in range(t + 1):
                            last = pe.matmul(out, b.v[:, j, vcols(br)], b.pt[:, u % 2, br, j * P:(j + 1) * P],
                                             start=False, stop=br == 1 and j == t)
                    last.then_inc(s["summed"], 1)

                scores(0)
                scores(1)
                flips(0)
                for u in range(U):
                    if u + 2 < U:
                        scores(u + 2)
                    values(u)
                    if u + 1 < U:
                        flips(u + 1)

        @block.vector
        def _(dve):
            with dve.Fori(0, HEADS // 2) as it:
                n = 0

                def link(ins):
                    nonlocal n
                    n += 1
                    ins.then_inc(s["chain"], 1)
                    dve.wait_ge(s["chain"], LINKS * it + n)

                def top(u):
                    t = T[u]
                    w = (t + 1) * P
                    dve.wait_ge(s["scored"], U * it + u + 1)
                    a = (u % 2) * 1024
                    both = k.ps[:, a:a + 1024].rearrange("p (b w) -> p b w", b=2)
                    diag = both[:, :, t * P:w]
                    link(dve.tensor_tensor(diag, diag, k.c["causal"].unsqueeze(1).to_broadcast([P, 2, P]), ALU.add))
                    link(dve.tensor_reduce(b.sst[:, u % 2, 0, :], both[:, :, 0:w], AX_X, ALU.max))
                    dve.tensor_scalar(b.sst[:, u % 2, 1, :], b.sst[:, u % 2, 0, :], -(HD ** -0.5), None,
                                      ALU.mult).then_inc(s["maxed"], 1)

                def scale(u):
                    h, t = u // QT, T[u]
                    w = (t + 1) * P
                    dve.wait_ge(s["expd"], U * it + u + 1)
                    link(dve.reciprocal(b.sst[:, u % 2, 3, :], b.sst[:, u % 2, 2, :]))
                    gate = b.gate[:, t, bass.ds(6 * it + 3 * h + 1, 2)]
                    link(dve.tensor_tensor(b.sst[:, u % 2, 4, :], b.sst[:, u % 2, 3, :], gate, ALU.mult))
                    for br in range(2):
                        last = dve.tensor_scalar(b.p[:, u % 2, br, 0:w], b.p[:, u % 2, br, 0:w],
                                                 b.sst[:, u % 2, 4, br:br + 1], None, ALU.mult)
                    last.then_inc(s["scaled"], 1)

                def copy(u):
                    w = (T[u] + 1) * P
                    dve.wait_ge(s["flipped"], U * it + u + 1)
                    if u >= 2:
                        dve.wait_ge(s["summed"], U * it + u - 1)
                    dve.tensor_copy(b.pt[:, u % 2, 1, 0:w], k.ps[:, 2560:2560 + w]).then_inc(s["copied_v"], 1)

                top(0)
                top(1)
                scale(0)
                for u in range(U):
                    copy(u)
                    if u + 1 < U:
                        scale(u + 1)
                    if u + 2 < U:
                        top(u + 2)
                dve.wait_ge(s["hi_done"], it + 1)
                dve.tensor_tensor(b.onlo[:, it, :], k.ps[:, 3072:3584], b.onhi[:, it, :].bitcast(F32),
                                  ALU.subtract).then_inc(s["lo_done"], 1)
                assert n == LINKS

        @block.scalar
        def _(act):
            with act.Fori(0, HEADS // 2) as it:
                def exps(u):
                    w = (T[u] + 1) * P
                    act.wait_ge(s["maxed"], U * it + u + 1)
                    if u >= 2:
                        act.wait_ge(s["flipped"], U * it + u - 1)
                    for br in range(2):
                        a = (u % 2) * 1024 + br * 512
                        last = act.activation(b.p[:, u % 2, br, 0:w], k.ps[:, a:a + w], ACT.Exp,
                                              bias=b.sst[:, u % 2, 1, br:br + 1], scale=HD ** -0.5,
                                              accum_out=b.sst[:, u % 2, 2, br:br + 1])
                    last.then_inc(s["expd"], 1)

                def copy(u):
                    w = (T[u] + 1) * P
                    act.wait_ge(s["flipped"], U * it + u + 1)
                    if u >= 2:
                        act.wait_ge(s["summed"], U * it + u - 1)
                    act.activation(b.pt[:, u % 2, 0, 0:w], k.ps[:, 2048:2048 + w], ACT.Copy).then_inc(s["copied_a"], 1)

                act.wait_ge(s["scored"], U * it)
                act.activation(b.qst, b.qr[:, it, :], ACT.Copy).then_inc(s["staged"], 1)
                act.wait_ge(s["summed"], U * it)
                act.activation(b.pcst, b.pct[0:NC, bass.ds(2 * it, 2), :], ACT.Copy).then_inc(s["staged"], 1)
                exps(0)
                exps(1)
                for u in range(U):
                    copy(u)
                    if u + 2 < U:
                        exps(u + 2)
                act.wait_ge(s["summed"], U * (it + 1))
                act.activation(b.onhi[:, it, :], k.ps[:, 3072:3584], ACT.Copy).then_inc(s["hi_done"], 1)


def stage_stick_breaking(nc, k, b):
    names = ("zeroed", "staged", "scored", "absd", "expd", "logd", "soft", "totals", "weighed", "weights", "values", "summed", "hi_done",
             "lo_done", "chain")
    s = {n: k.sem(f"sb_{n}") for n in names}
    order = list(range(QT))[::-1]
    TOTALS = QT - 1
    LINKS = QT
    with nc.Block() as block:
        @block.gpsimd
        def _(pool):
            pool.memset(b.tot, 0.0).then_inc(s["zeroed"], 1)
            pool.wait_ge(s["zeroed"], 1)
            with pool.Fori(0, SBH) as it:
                for i, j in enumerate(order[:-1]):
                    pool.wait_ge(s["soft"], QT * it + i + 1)
                    if i:
                        pool.wait_ge(s["totals"], TOTALS * it + i)
                    pool.tensor_tensor(b.tot[:, j, j * P:SEQ], b.sp[:, j, j * P:SEQ], b.tot[:, j + 1, j * P:SEQ],
                                       ALU.add).then_inc(s["totals"], 1)

        def scores(pe, H, i):
            j = order[i]
            if i == 0:
                pe.wait_ge(s["staged"], H + 1)
            pe.wait_ge(s["weights"], QT * (H - 1) + i + 1)
            pe.matmul(k.ps[:, j * 512:j * 512 + SEQ - j * P], b.kst[:, j * P:(j + 1) * P],
                      b.sbq[:, H, j * P:SEQ], start=True, stop=True).then_inc(s["scored"], 1)

        def head(pe, it, last_head):
            for i, j in enumerate(order):
                w = SEQ - j * P
                pe.wait_ge(s["soft"], QT * it + i + 1)
                pe.matmul(k.ps[:, j * 512:j * 512 + w], k.c["negtri"], b.sp[:, j, j * P:SEQ],
                          start=False, stop=False, skip_group_check=True)
                last = pe.matmul(k.ps[:, j * 512:j * 512 + P], k.c["ident"], k.c["sbneg"],
                                 start=False, stop=True, skip_group_check=True)
                if i:
                    pe.wait_ge(s["totals"], TOTALS * it + i)
                    last = pe.matmul(k.ps[:, j * 512 + P:j * 512 + w], k.c["negones"], b.tot[:, j + 1, (j + 1) * P:SEQ],
                                     start=False, stop=True, skip_group_check=True)
                last.then_inc(s["weighed"], 1)
            if not last_head:
                for i in range(QT):
                    scores(pe, it + 1, i)
            pe.wait_ge(s["weights"], QT * (it + 1))
            pe.wait_ge(s["values"], it + 1)
            for j in range(QT):
                last = pe.matmul(k.ps[:, 2048 + j * P:2560], b.vst[:, j, :], b.a[:, j, j * P:SEQ],
                                 start=j == 0, stop=j == QT - 1)
            last.then_inc(s["summed"], 1)

        @block.tensor
        def _(pe):
            pe.wait_ge(s["staged"], 1)
            for j in order:
                pe.matmul(k.ps[:, j * 512:j * 512 + SEQ - j * P], b.kst[:, j * P:(j + 1) * P],
                          b.sbq[:, 0, j * P:SEQ], start=True, stop=True).then_inc(s["scored"], 1)
            with pe.Fori(0, SBH - 1) as it:
                head(pe, it, False)
            head(pe, SBH - 1, True)

        @block.vector
        def _(dve):
            with dve.Fori(0, SBH) as it:
                n = 0

                def link(ins):
                    nonlocal n
                    n += 1
                    ins.then_inc(s["chain"], 1)
                    dve.wait_ge(s["chain"], LINKS * it + n)

                dve.tensor_copy(b.vst, b.sbv[:, :, bass.ds(it * P, P)]).then_inc(s["values"], 1)
                for i, j in enumerate(order):
                    dve.wait_ge(s["logd"], QT * it + i + 1)
                    sp = b.sp[:, j, j * P:SEQ]
                    link(dve.scalar_tensor_tensor(sp, k.ps[:, j * 512:j * 512 + SEQ - j * P], 0.0, sp, ALU.max, ALU.add))
                    ins = dve.tensor_tensor(b.sp[:, j, j * P:(j + 1) * P], b.sp[:, j, j * P:(j + 1) * P], k.c["sb01"], ALU.mult)
                    ins.then_inc(s["soft"], 1)
                dve.wait_ge(s["summed"], it + 1)
                dve.tensor_copy(b.oshi[:, it, :], k.ps[:, 2048:2560]).then_inc(s["hi_done"], 1)
                dve.wait_ge(s["hi_done"], it + 1)
                dve.tensor_tensor(b.oslo[:, it, :], k.ps[:, 2048:2560], b.oshi[:, it, :].bitcast(F32),
                                  ALU.subtract).then_inc(s["lo_done"], 1)

        def stage_keys(act, H):
            act.activation(b.kst, b.sbk[:, H, :], ACT.Copy).then_inc(s["staged"], 1)

        def head_a(act, it, last_head):
            for i, j in enumerate(order):
                act.wait_ge(s["scored"], QT * it + i + 1)
                if i == 0:
                    act.wait_ge(s["totals"], TOTALS * it)
                act.activation(b.sp[:, j, j * P:SEQ], k.ps[:, j * 512:j * 512 + SEQ - j * P], ACT.Abs).then_inc(s["absd"], 1)
            for i, j in enumerate(order):
                sp = b.sp[:, j, j * P:SEQ]
                act.wait_ge(s["absd"], QT * it + i + 1)
                act.activation(sp, sp, ACT.Exp, scale=-1.0).then_inc(s["expd"], 1)
            for i, j in enumerate(order):
                sp = b.sp[:, j, j * P:SEQ]
                act.wait_ge(s["expd"], QT * it + i + 1)
                act.activation(sp, sp, ACT.Ln, bias=1.0).then_inc(s["logd"], 1)
            if not last_head:
                stage_keys(act, it + 1)
            act.wait_ge(s["summed"], it)
            for i, j in enumerate(order):
                act.wait_ge(s["weighed"], QT * it + i + 1)
                act.activation(b.a[:, j, j * P:SEQ], k.ps[:, j * 512:j * 512 + SEQ - j * P],
                               ACT.Exp).then_inc(s["weights"], 1)

        @block.scalar
        def _(act):
            stage_keys(act, 0)
            with act.Fori(0, SBH - 1) as it:
                head_a(act, it, False)
            head_a(act, SBH - 1, True)


def stage_merge(nc, k, b, stream, n0):
    names = ("ready", "taken_a", "taken_v", "gates", "part", "mixed", "hi_done", "lo_done")
    s = {n: k.sem(f"mg_{n}") for n in names}
    TURNS, PAIRS = 2, 2
    per = UNITS_MERGE // TURNS

    with nc.Block() as block:
        @block.sync
        def _(sp):
            with sp.Fori(0, TURNS) as it:
                for u in range(per):
                    load_unit(sp, k, n0 + u + 2, stream(n0 + u + 2 + per * it), it=it, per=per)

        @block.tensor
        def _(pe):
            with pe.Fori(0, TURNS) as it:
                for pr in range(PAIRS):
                    for u in range(3):
                        n = n0 + 3 * pr + u
                        unit_ready(pe, k, n, it, per)
                        for g in range(2 if u == 2 else 1):
                            for m in range(2):
                                slot = 2 * u + 2 * g + m
                                done = PAIRS * it + pr
                                if u < 2:
                                    pe.wait_ge(s["taken_a"], 4 * done)
                                else:
                                    pe.wait_ge(s["taken_v"], 4 * done)
                                _, outs = tile_out(k, slot, SEQ)
                                if u < 2:
                                    w, xh, xl = unit_tiles(k, n, 0, KT, 256, m), k.hhi, k.hlo
                                elif g == 0:
                                    w, xh, xl = unit_tiles(k, n, 0, 4, 256, m), b.onhi, b.onlo
                                else:
                                    w, xh, xl = unit_tiles(k, n, 1024, 4, 256, m), b.oshi, b.oslo
                                last = dense_tile(pe, k, outs, w, xh, xl, SEQ)
                                last.then_inc(s["ready"], 1)

        @block.scalar
        def _(act):
            split_hi(act, k, n0)
            split_hi(act, k, n0 + 1)

            def turn(it, last_turn):
                for pr in range(PAIRS):
                    base = PAIRS * it + pr
                    for u in range(3):
                        if u < 2:
                            for m in range(2):
                                i = 2 * u + m
                                act.wait_ge(s["ready"], 8 * base + i + 1)
                                if i == 0:
                                    act.wait_ge(s["taken_v"], 4 * base)
                                act.activation(b.gt[:, i, :], k.ps[:, i * 512:(i + 1) * 512],
                                               ACT.Sigmoid).then_inc(s["taken_a"], 1)
                        else:
                            for m in range(2):
                                act.wait_ge(s["mixed"], 2 * base + m + 1)
                                act.activation(b.mhi[:, 4 * it + 2 * pr + m, :], b.mt[:, m, :],
                                               ACT.Copy).then_inc(s["hi_done"], 1)
                        if not (last_turn and 3 * pr + u + 2 > per):
                            split_hi(act, k, n0 + 3 * pr + u + 2, (s["ready"], 8 * base + (2, 4, 8)[u]), it=it, per=per)

            with act.Fori(0, TURNS - 1) as it:
                turn(it, False)
            turn(TURNS - 1, True)

        @block.vector
        def _(dve):
            split_lo(dve, k, n0)
            split_lo(dve, k, n0 + 1)

            def turn(it, last_turn):
                for pr in range(PAIRS):
                    base = PAIRS * it + pr
                    for u in range(3):
                        if u == 2:
                            for m in range(2):
                                dve.wait_ge(s["ready"], 8 * base + 5 + m)
                                dve.wait_ge(s["taken_a"], 4 * base + 4)
                                dve.tensor_tensor(b.gt[:, m, :], k.ps[:, (4 + m) * 512:(5 + m) * 512], b.gt[:, m, :],
                                                  ALU.mult).then_inc(s["taken_v"], 1)
                            for m in range(2):
                                dve.wait_ge(s["ready"], 8 * base + 7 + m)
                                dve.wait_ge(s["taken_v"], 4 * base + 2)
                                dve.tensor_tensor(b.mt[:, m, :], k.ps[:, (6 + m) * 512:(7 + m) * 512], b.gt[:, 2 + m, :],
                                                  ALU.mult).then_inc(s["part"], 1)
                            for m in range(2):
                                dve.wait_ge(s["part"], 2 * base + m + 1)
                                dve.tensor_tensor(b.mt[:, m, :], b.mt[:, m, :], b.gt[:, m, :],
                                                  ALU.add).then_inc(s["mixed"], 1)
                            for m in range(2):
                                dve.wait_ge(s["hi_done"], 2 * base + m + 1)
                                i = 4 * it + 2 * pr + m
                                dve.tensor_tensor(b.mlo[:, i, :], b.mt[:, m, :], b.mhi[:, i, :].bitcast(F32),
                                                  ALU.subtract).then_inc(s["lo_done"], 1)
                            dve.wait_ge(s["lo_done"], 2 * base + 2)
                            dve.sem_inc(s["taken_v"], 2)
                        if not (last_turn and 3 * pr + u + 2 > per):
                            split_lo(dve, k, n0 + 3 * pr + u + 2, it=it, per=per)

            with dve.Fori(0, TURNS - 1) as it:
                turn(it, False)
            turn(TURNS - 1, True)
    return n0 + UNITS_MERGE


def stage_project(nc, k, name, stream, n0, xhi, xlo, y, tok, last_unit, y_norm=None, split=0):
    ready, taken = k.sem(f"{name}_ready"), k.sem(f"{name}_taken")
    ring = 4
    with nc.Block() as block:
        @block.sync
        def _(sp):
            for n in range(n0 + 2, min(n0 + 4 + 2, last_unit)):
                load_unit(sp, k, n, stream(n))

        @block.tensor
        def _(pe):
            for j in range(KT):
                if j % 2 == 0:
                    unit_ready(pe, k, n0 + j // 2)
                if j >= ring:
                    pe.wait_ge(taken, j - ring + 1)
                _, outs = tile_out(k, j % ring, tok)
                last = dense_tile(pe, k, outs, unit_tiles(k, n0 + j // 2, 0, KT, 256, j % 2), xhi, xlo, tok)
                last.then_inc(ready, 1)
                if y_norm and j >= 2:
                    y_norm.pe_add(pe, j - 2)
            if y_norm:
                y_norm.pe_add(pe, KT - 2)
                y_norm.pe_add(pe, KT - 1)

        @block.vector
        def _(dve):
            for u in range(split, 5):
                split_lo(dve, k, n0 + u)

        @block.scalar
        def _(act):
            for u in range(split, 2):
                split_hi(act, k, n0 + u)
            if y_norm:
                y_norm.act_table(act)
            for j in range(KT):
                act.wait_ge(ready, j + 1)
                base, _ = tile_out(k, j % ring, tok)
                act.activation(y[:, j, 0:tok], k.ps[:, base:base + tok], ACT.Copy).then_inc(taken, 1)
                if y_norm:
                    act.wait_ge(taken, j + 1)
                    y_norm.act_square(act, j)
                if j % 2 and j // 2 + 2 < 5:
                    split_hi(act, k, n0 + j // 2 + 2, (ready, j + 1))
    return n0 + 4


def stage_mlp(nc, k, name, stream, n0, y, hid_hi, hid_lo, tok, post, pre, last_unit, y_norm=None, post_norm=None,
              ada=None):
    names = ("ready", "relu", "squared", "hid_hi", "hid_lo", "added")
    s = {n: k.sem(f"{name}_{n}") for n in names}
    if ada:
        loaded = [k.sem(f"{name}_ada_loaded{i}") for i in range(2 * ADA_PER)]
        names = ("hi", "lo", "used", "rows", "turned", "out")
        m = {n: k.sem(f"{name}_ada_{n}") for n in names}
    HALVES = 2 * ADA_PER
    n_post = post_norm or Norm(k, f"{name}_p", y, KT, tok, 1)
    res = Residual(k, f"{name}_r", n_post, k.x, post)
    n_pre = Norm(k, f"{name}_q", k.x, KT, tok, 5)
    normed = Normed(k, f"{name}_h", n_pre, k.hhi, k.hlo, pre)
    ring = 4
    T1, T2 = 4, KT
    last_u = n0 + UNITS_FF

    with nc.Block() as block:
        @block.sync
        def _(sp):
            def load_half(it, j):
                sp.dma_start(ada.raw[j], ada.src(HALVES * it + j)).then_inc(loaded[j], 16)

            if ada:
                for j in range(HALVES):
                    load_half(0, j)
            with sp.Fori(0, FF_GROUPS - 1) as it:
                for u in range(4):
                    load_unit(sp, k, n0 + u + 2, stream(n0 + u + 2 + 4 * it), it=it, per=4)
                if ada:
                    for j in range(HALVES):
                        sp.wait_ge(m["used"], HALVES * it + j + 1)
                        load_half(it + 1, j)
            for n in range(last_u - 2, min(last_u + 2, last_unit)):
                load_unit(sp, k, n, stream(n))

        @block.gpsimd
        def _(pool):
            res.pool(pool)
            if ada:
                with pool.Fori(0, FF_GROUPS) as it:
                    for j in range(HALVES):
                        pool.wait_ge(m["hi"], HALVES * it + j + 1)
                        pool.tensor_tensor(ada.lo[j], ada.raw[j], ada.hi[:, j % 3, :].bitcast(F32),
                                           ALU.subtract).then_inc(m["lo"], 1)

        @block.tensor
        def _(pe):
            if post_norm is None:
                n_post.pe_all(pe)
            else:
                n_post.pe_spread(pe)
            n_pre.pe_all(pe)
            unit_ready(pe, k, n0)
            first_tiles(pe, k, n0, 256, 2, tok, lambda i: normed.pe_wait(pe, i), s["ready"])

            def half(it, n):
                if n % 2 == 0:
                    pe.wait_ge(m["rows"], ADA_PER * it + n // 2)
                pe.wait_ge(m["lo"], HALVES * it + n + 1)
                out = k.ps[0:4, 3072:3328]
                for i in range(4):
                    kt, cols = 4 * (n % 2) + i, slice(i * 256, (i + 1) * 256)
                    pe.matmul(out, k.cv_parts[:, kt, :], ada.hi[:, n % 3, cols], start=kt == 0, stop=False)
                    last = pe.matmul(out, k.cv_parts[:, kt, :], ada.lo[n][:, cols], start=False, stop=kt == KT - 1)
                last.then_inc(m["used"], 1)

            def turn_rows(it, j):
                if j == 0:
                    pe.wait_ge(m["out"], it)
                pe.wait_ge(m["rows"], ADA_PER * it + j + 1)
                for t in range(2):
                    c = 3584 + 4 * j + 2 * t
                    last = pe.matmul(k.ps[:, c:c + 2], ada.row[:, j % 2, t * P:(t + 1) * P], k.c["pairs"][0:4, 0:2],
                                     start=True, stop=True)
                last.then_inc(m["turned"], 1)

            def group(it, first, last_group=False):
                for j in range(2 if first else 0, T1 + T2):
                    u = j // 2 if j < T1 else 2 + (j - T1) // 4
                    n = n0 + u
                    if j in (0, 2, 4, 8):
                        unit_ready(pe, k, n, it, 4)
                    if j < T1:
                        if not first:
                            pe.wait_ge(s["added"], T2 * it - (T1 - 1 - j))
                    elif j < 2 * T1:
                        pe.wait_ge(s["relu"], T1 * it + (j - T1) + 1)
                    else:
                        pe.wait_ge(s["added"], T2 * it + j - 2 * T1 + 1)
                    _, outs = tile_out(k, j % ring, tok)
                    if j < T1:
                        last = dense_tile(pe, k, outs, unit_tiles(k, n, 0, KT, 256, j % 2), k.hhi, k.hlo, tok)
                    else:
                        last = dense_tile(pe, k, outs, unit_tiles(k, n, 0, 4, 512, (j - T1) % 4), hid_hi, hid_lo, tok,
                                          (lambda i: pe.wait_ge(s["hid_lo"], T1 * it + i + 1)) if j == T1 else None)
                    last.then_inc(s["ready"], 1)
                    if ada and T1 <= j < T1 + HALVES:
                        half(it, j - T1)
                    if ada and j in (7, 9, 11):
                        turn_rows(it, (j - 7) // 2)
                    if last_group and y_norm and not ada and j >= T1 + 2:
                        y_norm.pe_add(pe, j - T1 - 2)
                if last_group and y_norm:
                    for t in range(0 if ada else KT - 2, KT):
                        y_norm.pe_add(pe, t)

            group(0, True)
            with pe.Fori(1, FF_GROUPS - 1) as it:
                group(it, False)
            group(FF_GROUPS - 1, False, True)

        @block.scalar
        def _(act):
            if post_norm is None:
                n_post.act_all(act)
            else:
                n_post.act_root(act)
            n_pre.act_all(act, res.wait)
            normed.act(act)

            def half_hi(it, n):
                act.wait_ge(loaded[n], 16 * (it + 1))
                if n >= 3:
                    act.wait_ge(m["used"], HALVES * it + n - 2)
                act.activation(ada.hi[:, n % 3, :], ada.raw[n], ACT.Copy).then_inc(m["hi"], 1)

            def rows(it, j):
                act.wait_ge(m["used"], HALVES * it + 2 * j + 2)
                if j == 2:
                    act.wait_ge(m["turned"], ADA_PER * it + 1)
                act.activation(ada.row[:, j % 2, :], k.ps[0:4, 3072:3328], ACT.Copy).then_inc(m["rows"], 1)

            def group(it, last_group):
                def hidden_hi(j):
                    act.wait_ge(s["squared"], T1 * it + j + 1)
                    act.activation(hid_hi[:, j, 0:tok], k.sqt[:, j % 2, 0:tok], ACT.Copy).then_inc(s["hid_hi"], 1)

                for j in range(T1):
                    act.wait_ge(s["ready"], (T1 + T2) * it + j + 1)
                    base, _ = tile_out(k, j % ring, tok)
                    if j >= 2:
                        act.wait_ge(s["hid_lo"], T1 * it + j - 1)
                    act.activation(k.sqt[:, j % 2, 0:tok], k.ps[:, base:base + tok], ACT.Relu).then_inc(s["relu"], 1)
                    hidden_hi(j)
                    if j % 2:
                        split_hi(act, k, n0 + j // 2 + 2, (s["ready"], (T1 + T2) * it + j + 1), it=it, per=4)
                    if ada and j < 3:
                        half_hi(it, j)
                if ada:
                    rows(it, 0)
                    half_hi(it, 3)
                    half_hi(it, 4)
                    rows(it, 1)
                    half_hi(it, 5)
                if not last_group:
                    split_hi(act, k, n0 + 4, (s["ready"], (T1 + T2) * it + 8), it=it, per=4)
                if ada:
                    rows(it, 2)
                if not last_group:
                    split_hi(act, k, n0 + 5, (s["ready"], (T1 + T2) * it + 12), it=it, per=4)
                if ada:
                    act.wait_ge(m["turned"], ADA_PER * (it + 1))
                    act.activation(k.mod[:, bass.ds((FF_GROUPS * ada.layer + it) * 4 * ADA_PER, 4 * ADA_PER)],
                                   k.ps[:, 3584:3584 + 4 * ADA_PER], ACT.Copy).then_inc(m["out"], 1)

            with act.Fori(0, FF_GROUPS - 1) as it:
                group(it, False)
            group(FF_GROUPS - 1, True)
            if y_norm:
                y_norm.act_table(act)
                for t in range(KT):
                    act.wait_ge(s["added"], T2 * (FF_GROUPS - 1) + t + 1)
                    y_norm.act_square(act, t)

        @block.vector
        def _(dve):
            n_post.dve_all(dve)
            res.dve(dve)
            split_first(dve, k, n0 + 1, 1)
            n_pre.dve_all(dve)
            normed.dve(dve)

            def group(it, first, last_group):
                for j in range(T1):
                    dve.wait_ge(s["relu"], T1 * it + j + 1)
                    sq = k.sqt[:, j % 2, 0:tok]
                    dve.tensor_tensor(sq, sq, sq, ALU.mult).then_inc(s["squared"], 1)
                    dve.wait_ge(s["hid_hi"], T1 * it + j + 1)
                    dve.tensor_tensor(hid_lo[:, j, 0:tok], sq, hid_hi[:, j, 0:tok].bitcast(F32),
                                      ALU.subtract).then_inc(s["hid_lo"], 1)
                    if j % 2:
                        split_lo(dve, k, n0 + j // 2 + 2, it=it, per=4)
                for j in range(T2):
                    dve.wait_ge(s["ready"], (T1 + T2) * it + T1 + j + 1)
                    base, _ = tile_out(k, (T1 + j) % ring, tok)
                    src = k.ps[:, base:base + tok]
                    if first:
                        dve.tensor_copy(y[:, j, 0:tok], src).then_inc(s["added"], 1)
                    else:
                        dve.tensor_tensor(y[:, j, 0:tok], src, y[:, j, 0:tok], ALU.add).then_inc(s["added"], 1)
                    if j % 4 == 3 and not last_group:
                        split_lo(dve, k, n0 + 4 + j // 4, it=it, per=4)

            group(0, True, False)
            with dve.Fori(1, FF_GROUPS - 1) as it:
                group(it, False, False)
            group(FF_GROUPS - 1, False, True)
    return last_u


def stage_residual(nc, k, name, y, tok, post, y_norm=None):
    norm = y_norm or Norm(k, f"{name}_p", y, KT, tok, 5)
    res = Residual(k, f"{name}_r", norm, k.x, post)
    with nc.Block() as block:
        @block.tensor
        def _(pe):
            if y_norm is None:
                norm.pe_all(pe)
            else:
                norm.pe_spread(pe)

        @block.scalar
        def _(act):
            if y_norm is None:
                norm.act_all(act)
            else:
                norm.act_root(act)

        @block.vector
        def _(dve):
            norm.dve_all(dve)
            res.dve(dve)

        @block.gpsimd
        def _(pool):
            res.pool(pool)


def stage_rope_tables(nc, k, b, positions, inv_freq, inputs):
    loaded, chain, sined = k.sem("rt_loaded"), k.sem("rt_chain"), k.sem("rt_sin")
    inputs_loaded, silu = k.sem("inputs_loaded"), k.sem("silu_done")
    two_pi = 2 * np.pi
    c1 = float(np.float32(6.28125))
    c2 = float(np.round((two_pi - c1) * 2 ** 21) / 2 ** 21)
    c3 = float(np.float32(two_pi - c1 - c2))
    with nc.Block() as block:
        @block.sync
        def _(sp):
            sp.dma_start(b.pos_i, positions.partition_broadcast(P)).then_inc(loaded, 16)
            sp.dma_start(b.inv, inv_freq).then_inc(loaded, 16)
            for dst, src in inputs:
                sp.dma_start(dst, src).then_inc(inputs_loaded, 16)
            sp.wait_ge(inputs_loaded, 16 * len(inputs))

        @block.vector
        def _(dve):
            n = 0

            def link(ins):
                nonlocal n
                n += 1
                ins.then_inc(chain, 1)
                dve.wait_ge(chain, n)

            ang, turns = k.sqt[:, 0, 0:SEQ], k.sqt[:, 1, 0:SEQ]
            dve.wait_ge(loaded, 32)
            link(dve.tensor_copy(turns, b.pos_i))
            link(dve.tensor_scalar(ang, turns, b.inv, None, ALU.mult))
            for i, (dst, shift) in enumerate(((b.sin, 0.0), (b.cos, float(np.pi / 2)))):
                link(dve.tensor_scalar(turns, ang, 1.0 / two_pi, shift / two_pi, ALU.mult, ALU.add))
                link(dve.tensor_copy(b.pos_i, turns))
                link(dve.tensor_copy(turns, b.pos_i))
                link(dve.scalar_tensor_tensor(dst, turns, -c1, ang, ALU.mult, ALU.add))
                link(dve.scalar_tensor_tensor(dst, turns, -c2, dst, ALU.mult, ALU.add))
                link(dve.scalar_tensor_tensor(dst, turns, -c3, dst, ALU.mult, ALU.add))
                link(dve.tensor_scalar(dst, dst, shift, None, ALU.add))
                link(dve.tensor_scalar(dst, dst, float(np.float32(np.pi)) , -float(np.float32(np.pi)), ALU.min, ALU.max))
            dve.sem_inc(sined, 1)
            dve.wait_ge(silu, 2)
            dve.tensor_tensor(k.cv_parts[:, :, 2:4], k.cv, k.cv_parts[:, :, 0:2].bitcast(F32), ALU.subtract)

        @block.scalar
        def _(act):
            act.wait_ge(sined, 1)
            act.activation(b.sin, b.sin, ACT.Sin)
            act.activation(b.cos, b.cos, ACT.Sin)
            act.wait_ge(inputs_loaded, 16 * len(inputs))
            act.activation(k.cv, k.cv, ACT.Silu).then_inc(silu, 1)
            act.wait_ge(silu, 1)
            act.activation(k.cv_parts[:, :, 0:2], k.cv, ACT.Copy).then_inc(silu, 1)



U_DOWN, U_GATE = 3, 1
U_GLA = 4
UNITS_2 = U_DOWN + 1 + MH + 4 + UNITS_FF + U_GATE + U_GLA * GH + UNITS_FF
MLA_SCALE = float(192 ** -0.5)


def stage_modulation(nc, k, b, a, stream):
    loaded, biased, scales = k.sem("mod_loaded"), k.sem("mod_biased"), k.sem("mod_scales")
    with nc.Block() as block:
        @block.sync
        def _(sp):
            for dst, src in ((b.ada_b, a["ada_b"]), (b.g, a["norm_g2"]), (b.axial, a["axial"]), (b.g_q, a["g_q"]),
                             (b.g_kv, a["g_kv"]), (b.g_o, a["g_o"])):
                sp.dma_start(dst, src).then_inc(loaded, 16)
            load_unit(sp, k, 0, stream(0))
            load_unit(sp, k, 1, stream(1))

        @block.vector
        def _(dve):
            dve.wait_ge(loaded, 96)
            dve.tensor_tensor(b.mod, b.mod, b.ada_b.unsqueeze(3).to_broadcast([P, ADA_TURNS, KT, 2]),
                              ALU.add).then_inc(biased, 1)
            dve.wait_ge(biased, 1)
            for l in range(DEPTH):
                for j, (m, plus) in enumerate(((1, 1.0), (2, 0.0), (4, 1.0), (5, 0.0))):
                    g = b.g[:, l, j, :].unsqueeze(2).to_broadcast([P, KT, 2])
                    dve.scalar_tensor_tensor(b.sc[:, 4 * l + j, :, :], b.mod[:, 6 * l + m, :, :], plus, g, ALU.add,
                                             ALU.mult).then_inc(scales, 1)
            dve.wait_ge(scales, 4 * DEPTH)


def parts_of(b, layer, norm, tok, shift=None):
    out = []
    for v, (c0, w) in enumerate(((0, SEQ), (SEQ, CTX))):
        if c0 < tok:
            part = (c0, w, b.sc[:, 4 * layer + norm, :, v])
            out.append(part if shift is None else part + (b.mod[:, 6 * layer + shift, :, v],))
    return out


def stage_norm_dense(nc, k, name, stream, n0, n_units, width, cols, out, tok, parts):
    norm = Norm(k, f"{name}_n", k.x, KT, tok, 5)
    normed = Normed(k, f"{name}_h", norm, k.hhi, k.hlo, parts)
    ready, taken = k.sem(f"{name}_ready"), k.sem(f"{name}_taken")
    ring, per = 4, cols // P
    with nc.Block() as block:
        @block.sync
        def _(sp):
            for n in range(n0 + 2, n0 + n_units + 2):
                load_unit(sp, k, n, stream(n))

        @block.tensor
        def _(pe):
            norm.pe_all(pe)
            unit_ready(pe, k, n0)
            first_tiles(pe, k, n0, cols, per, tok, lambda i: normed.pe_wait(pe, i), ready)
            for j in range(per, n_units * per):
                if j % per == 0:
                    unit_ready(pe, k, n0 + j // per)
                if j >= ring:
                    pe.wait_ge(taken, j - ring + 1)
                _, outs = tile_out(k, j % ring, tok)
                last = dense_tile(pe, k, outs, unit_tiles(k, n0 + j // per, 0, KT, cols, j % per), k.hhi, k.hlo, tok)
                last.then_inc(ready, 1)

        @block.vector
        def _(dve):
            split_first(dve, k, n0, min(n_units, 2), width)
            norm.dve_all(dve)
            normed.dve(dve)
            for u in range(2, n_units):
                split_lo(dve, k, n0 + u, width)

        @block.scalar
        def _(act):
            norm.act_all(act)
            normed.act(act)
            for j in range(n_units * per):
                act.wait_ge(ready, j + 1)
                base, _ = tile_out(k, j % ring, tok)
                act.activation(out[:, j, 0:tok], k.ps[:, base:base + tok], ACT.Copy).then_inc(taken, 1)
                if j % per == per - 1 and j // per + 2 < n_units:
                    split_hi(act, k, n0 + j // per + 2, (ready, j + 1), width)
    return n0 + n_units


def stage_norm(nc, k, name, src, kt, hi, lo, scale):
    norm = Norm(k, f"{name}_n", src, kt, TOK, 5)
    normed = Normed(k, f"{name}_h", norm, hi, lo, [(0, TOK, scale, None)])
    with nc.Block() as block:
        @block.tensor
        def _(pe):
            norm.pe_all(pe)

        @block.vector
        def _(dve):
            norm.dve_all(dve)
            normed.dve(dve)

        @block.scalar
        def _(act):
            norm.act_all(act)
            normed.act(act)


def stage_key_rope_values(nc, k, b, src, stream, n0):
    turned, half1, half2 = k.sem("kr_turned"), k.sem("kr_cos"), k.sem("kr_sin")
    ready, taken = k.sem("values_ready"), k.sem("values_taken")
    ring, outs = 4, [(t, g) for t in range(TOK // P) for g in range(2)]
    with nc.Block() as block:
        @block.sync
        def _(sp):
            load_unit(sp, k, n0 + 2, stream(n0 + 2))

        @block.tensor
        def _(pe):
            pe.matmul(k.ps[:, 0:SEQ], k.c["axial_perm"], src[:, 0:SEQ], start=True, stop=True).then_inc(turned, 1)
            unit_ready(pe, k, n0)
            for j, (t, g) in enumerate(outs):
                if j >= ring:
                    pe.wait_ge(taken, j - ring + 1)
                base = (1 + j % ring) * 512
                c = slice(t * P, (t + 1) * P)
                for i in range(2):
                    a = i * 1024 + g * 512
                    w = (k.whi[:, n0 % 2, a:a + 512], k.wlo[:, n0 % 2, a:a + 512])
                    last = mm3(pe, [k.ps[:, base:base + 512]], b.ckv_hi[:, i, c], b.ckv_lo[:, i, c], [w], i == 0, i == 1)
                last.then_inc(ready, 1)

        @block.gpsimd
        def _(pool):
            pool.tensor_tensor(k.sqt[:, 0, 0:SEQ], src[:, 0:SEQ], b.axial[:, 0, :], ALU.mult).then_inc(half1, 1)

        @block.scalar
        def _(act):
            split_hi(act, k, n0)
            act.activation(b.krope[:, SEQ:TOK], src[:, SEQ:TOK], ACT.Copy)
            act.wait_ge(turned, 1)
            act.wait_ge(half1, 1)
            for j, (t, g) in enumerate(outs):
                act.wait_ge(ready, j + 1)
                base = (1 + j % ring) * 512
                act.activation(b.v[:, t, g * 512:(g + 1) * 512], k.ps[:, base:base + 512], ACT.Copy).then_inc(taken, 1)

        @block.vector
        def _(dve):
            dve.wait_ge(turned, 1)
            dve.tensor_tensor(k.acc[:, 0:SEQ], k.ps[:, 0:SEQ], b.axial[:, 1, :], ALU.mult).then_inc(half2, 1)
            split_lo(dve, k, n0)
            dve.wait_ge(half2, 1)
            dve.wait_ge(half1, 1)
            dve.tensor_tensor(b.krope[:, 0:SEQ], k.acc[:, 0:SEQ], k.sqt[:, 0, 0:SEQ], ALU.add)
    return n0 + 1


def stage_latent_attention(nc, k, b, stream, n0):
    names = ("projected", "taken_a", "staged", "raw", "turned", "half1", "half2", "rotated", "scored", "maxed",
             "expd", "scaled", "flipped", "copied_a", "copied_v", "summed", "hi_done", "lo_done", "chain")
    s = {n: k.sem(f"la_{n}") for n in names}
    U = TOK // P
    LINKS = 2 * U
    W_QN, W_QR, W_K = 0, 384, 768

    def keys(u):
        return (0, TOK) if u < QT else (SEQ, CTX)

    def pieces(w):
        return [(0, 512), (512, w - 512)] if w > 512 else [(0, w)]

    with nc.Block() as block:
        @block.sync
        def _(sp):
            with sp.Fori(0, MH // 2) as it:
                for hd in range(2):
                    load_unit(sp, k, n0 + hd + 2, stream(n0 + hd + 2 + 2 * it), it=it, per=2)

        def w_tiles(n, off, kt):
            return [(k.whi[:, n % 2, off + i * P:off + (i + 1) * P], k.wlo[:, n % 2, off + i * P:off + (i + 1) * P])
                    for i in range(kt)]

        def queries(pe, hd, H, it):
            n = n0 + hd
            unit_ready(pe, k, n, it, 2)
            pe.wait_ge(s["expd"], U * H)
            dense_tile(pe, k, tile_out(k, 0, TOK)[1], w_tiles(n, W_QN, 3), b.cq_hi, b.cq_lo, TOK).then_inc(s["projected"], 1)
            dense_tile(pe, k, tile_out(k, 1, TOK)[1], w_tiles(n, W_QR, 3), b.cq_hi, b.cq_lo, TOK).then_inc(s["projected"], 1)

        def head(pe, hd, H, it, last_head):
            n = n0 + hd
            pe.wait_ge(s["taken_a"], 3 * H + 2)
            pe.matmul(k.ps[:, 1024:1536], k.c["axial_perm"], b.qraw, start=True, stop=True).then_inc(s["turned"], 1)
            pe.wait_ge(s["copied_a"], U * H)
            pe.wait_ge(s["copied_v"], QT * H)
            dense_tile(pe, k, tile_out(k, 2, TOK)[1], w_tiles(n, W_K, 2), b.ckv_hi, b.ckv_lo, TOK).then_inc(s["projected"], 1)

            def scores(u):
                k0, w = keys(u)
                c = slice(u * P, (u + 1) * P)
                if u == 0:
                    pe.wait_ge(s["taken_a"], 3 * H + 3)
                    pe.wait_ge(s["rotated"], H + 1)
                else:
                    pe.wait_ge(s["expd"], U * H + max(u - 1, 0))
                base = (u % 2) * 1024
                for p0, pw in pieces(w):
                    out = k.ps[:, base + p0:base + p0 + pw]
                    pe.matmul(out, b.qn[:, c], b.kn[:, k0 + p0:k0 + p0 + pw], start=True, stop=False)
                    last = pe.matmul(out, b.qr[0:64, c], b.krope[0:64, k0 + p0:k0 + p0 + pw], start=False, stop=True)
                last.then_inc(s["scored"], 1)

            def flips(u):
                _, w = keys(u)
                pe.wait_ge(s["scaled"], U * H + u + 1)
                pe.wait_ge(s["copied_a"], U * H + u)
                pe.wait_ge(s["copied_v"], QT * H + min(u, QT))
                for j in range(w // P):
                    last = pe.transpose(k.ps[:, 2048 + j * P:2048 + (j + 1) * P], b.p[:, u % 2, j * P:(j + 1) * P], k.c["ident"])
                last.then_inc(s["flipped"], 1)

            def values(u):
                k0, w = keys(u)
                if u == 0:
                    pe.wait_ge(s["staged"], H + 1)
                    pe.wait_ge(s["lo_done"], H)
                pe.wait_ge(s["copied_a"], U * H + u + 1)
                pe.wait_ge(s["copied_v"], QT * H + min(u + 1, QT))
                for j in range(w // P):
                    last = pe.matmul(k.ps[:, 3072 + u * P:3072 + (u + 1) * P], b.vst[:, k0 // P + j, :],
                                     b.pt[:, u % 2, j * P:(j + 1) * P], start=j == 0, stop=j == w // P - 1)
                last.then_inc(s["summed"], 1)

            scores(0)
            scores(1)
            flips(0)
            for u in range(U):
                if u + 2 < U:
                    scores(u + 2)
                if u == U - 1 and not last_head:
                    queries(pe, (hd + 1) % 2, H + 1, it + (hd + 1) // 2)
                values(u)
                if u + 1 < U:
                    flips(u + 1)

        @block.tensor
        def _(pe):
            queries(pe, 0, 0, 0)
            with pe.Fori(0, MH // 2 - 1) as it:
                for hd in range(2):
                    head(pe, hd, 2 * it + hd, it, False)
            for hd in range(2):
                head(pe, hd, MH - 2 + hd, MH // 2 - 1, hd == 1)

        @block.gpsimd
        def _(pool):
            with pool.Fori(0, MH) as H:
                pool.wait_ge(s["raw"], H + 1)
                pool.tensor_tensor(b.qcos, b.qraw, b.axial[:, 0, :], ALU.mult).then_inc(s["half1"], 1)

        def prepare(dve, H):
            dve.wait_ge(s["summed"], U * H)
            dve.tensor_copy(b.vst, b.v[:, :, bass.ds(H * P, P)]).then_inc(s["staged"], 1)
            dve.wait_ge(s["turned"], H + 1)
            dve.tensor_tensor(k.acc[:, 0:SEQ], k.ps[:, 1024:1536], b.axial[:, 1, :], ALU.mult).then_inc(s["half2"], 1)
            dve.wait_ge(s["half1"], H + 1)
            dve.wait_ge(s["half2"], H + 1)
            dve.tensor_tensor(b.qr[:, 0:SEQ], k.acc[:, 0:SEQ], b.qcos, ALU.add).then_inc(s["rotated"], 1)

        def head_v(dve, hd, H, it, last_head):
            n = 0

            def link(ins):
                nonlocal n
                n += 1
                ins.then_inc(s["chain"], 1)
                dve.wait_ge(s["chain"], LINKS * H + n)

            if not last_head:
                split_lo(dve, k, n0 + hd + 1, MLA_U, it=it, per=2)

            def top(u):
                _, w = keys(u)
                dve.wait_ge(s["scored"], U * H + u + 1)
                base = (u % 2) * 1024
                link(dve.tensor_reduce(b.st[:, u % 2, 0:1], k.ps[:, base:base + w], AX_X, ALU.max))
                dve.tensor_scalar(b.st[:, u % 2, 1:2], b.st[:, u % 2, 0:1], -MLA_SCALE, None, ALU.mult).then_inc(s["maxed"], 1)

            def scale(u):
                _, w = keys(u)
                dve.wait_ge(s["expd"], U * H + u + 1)
                link(dve.reciprocal(b.st[:, u % 2, 3:4], b.st[:, u % 2, 2:3]))
                dve.tensor_scalar(b.p[:, u % 2, 0:w], b.p[:, u % 2, 0:w], b.st[:, u % 2, 3:4], None,
                                  ALU.mult).then_inc(s["scaled"], 1)

            def copy(u):
                if u < QT:
                    dve.wait_ge(s["flipped"], U * H + u + 1)
                    if u >= 2:
                        dve.wait_ge(s["summed"], U * H + u - 1)
                    dve.tensor_copy(b.pt[:, u % 2, 512:TOK], k.ps[:, 2560:2560 + TOK - 512]).then_inc(s["copied_v"], 1)

            top(0)
            top(1)
            scale(0)
            for u in range(U):
                copy(u)
                if u + 1 < U:
                    scale(u + 1)
                if u + 2 < U:
                    top(u + 2)
            if not last_head:
                prepare(dve, H + 1)
            dve.wait_ge(s["hi_done"], H + 1)
            dve.tensor_tensor(k.hlo[:, H, :], k.ps[:, 3072:3072 + TOK], k.hhi[:, H, :].bitcast(F32),
                              ALU.subtract).then_inc(s["lo_done"], 1)
            assert n == LINKS

        @block.vector
        def _(dve):
            split_lo(dve, k, n0, MLA_U)
            prepare(dve, 0)
            with dve.Fori(0, MH // 2 - 1) as it:
                for hd in range(2):
                    head_v(dve, hd, 2 * it + hd, it, False)
            for hd in range(2):
                head_v(dve, hd, MH - 2 + hd, MH // 2 - 1, hd == 1)

        def take_queries(act, H):
            act.wait_ge(s["projected"], 3 * H + 1)
            act.activation(b.qn, k.ps[:, 0:TOK], ACT.Copy).then_inc(s["taken_a"], 1)
            act.wait_ge(s["projected"], 3 * H + 2)
            act.wait_ge(s["rotated"], H)
            act.activation(b.qraw, k.ps[:, 1024:1536], ACT.Copy).then_inc(s["raw"], 1)
            act.activation(b.qr[:, SEQ:TOK], k.ps[:, 1536:1536 + CTX], ACT.Copy).then_inc(s["taken_a"], 1)

        def head_a(act, hd, H, it, last_head):
            act.wait_ge(s["projected"], 3 * H + 3)
            act.activation(b.kn, k.ps[:, 2048:2048 + TOK], ACT.Copy).then_inc(s["taken_a"], 1)
            if not last_head:
                split_hi(act, k, n0 + hd + 1, (s["projected"], 3 * H + 3), MLA_U, it, 2)

            def exps(u):
                _, w = keys(u)
                act.wait_ge(s["maxed"], U * H + u + 1)
                if u >= 2:
                    act.wait_ge(s["flipped"], U * H + u - 1)
                base = (u % 2) * 1024
                act.activation(b.p[:, u % 2, 0:w], k.ps[:, base:base + w], ACT.Exp, bias=b.st[:, u % 2, 1:2],
                               scale=MLA_SCALE, accum_out=b.st[:, u % 2, 2:3]).then_inc(s["expd"], 1)

            def copy(u):
                _, w = keys(u)
                w = min(w, 512)
                act.wait_ge(s["flipped"], U * H + u + 1)
                if u >= 2:
                    act.wait_ge(s["summed"], U * H + u - 1)
                act.activation(b.pt[:, u % 2, 0:w], k.ps[:, 2048:2048 + w], ACT.Copy).then_inc(s["copied_a"], 1)

            exps(0)
            exps(1)
            for u in range(U):
                copy(u)
                if u + 2 < U:
                    exps(u + 2)
            if not last_head:
                take_queries(act, H + 1)
            act.wait_ge(s["summed"], U * (H + 1))
            act.activation(k.hhi[:, H, :], k.ps[:, 3072:3072 + TOK], ACT.Copy).then_inc(s["hi_done"], 1)

        @block.scalar
        def _(act):
            split_hi(act, k, n0, width=MLA_U)
            take_queries(act, 0)
            with act.Fori(0, MH // 2 - 1) as it:
                for hd in range(2):
                    head_a(act, hd, 2 * it + hd, it, False)
            for hd in range(2):
                head_a(act, hd, MH - 2 + hd, MH // 2 - 1, hd == 1)

    return n0 + MH


def stage_gla_heads(nc, k, b, a, stream, n0):
    names = ("small", "zeroed", "projected", "taken_q", "taken_k", "taken_v", "taken_r", "gated", "biased", "absd",
             "exp1", "logd", "ends", "decays", "tilted", "tilted_p", "attended", "masked", "flipped", "turned",
             "state_f", "state_b", "updated_f", "updated_b", "summed", "o_out", "gated_o", "value", "hi_done",
             "lo_done", "ready", "added", "chain")
    s = {n: k.sem(f"gla_{n}") for n in names}
    NCH = TOK // CH
    LAT = SEQ // CH
    seqs = ([8, 9, 10, 11, 0, 1, 2, 3, 4, 5, 6, 7], [11, 10, 9, 8, 7, 6, 5, 4, 3, 2, 1, 0])
    upd = (s["updated_f"], s["updated_b"])
    sta = (s["state_f"], s["state_b"])
    STEPS = NCH - 1
    inv_tau = 1.0 / 16.0
    g, cum, tail = (k.acc, k.diag), (k.sqt[:, 0, :], k.sqt[:, 1, :]), (b.ke[:, 0, :], b.ke[:, 1, :])
    att = (k.acc[:, 0:SEQ], k.diag[:, 0:SEQ])
    chunked = lambda t: t.rearrange("p (c i) -> p c i", i=CH)
    TILES = 7
    V_AT = [512, 768, 0, 256, 1024, 1280]
    R_AT = [1536, 512]
    PS_A, PS_S, PS_O, PS_T = (0, 1024), (512, 1536), (2048, 2560), (2048, 3072)
    BIG = 3e38

    with nc.Block() as block:
        @block.sync
        def _(sp):
            with sp.Fori(0, GH) as it:
                sp.wait_ge(s["biased"], 2 * it)
                sp.dma_start(b.w2s, a["gla_w2"][it]).then_inc(s["small"], 16)
                sp.dma_start(b.bias, a["gla_b"][it]).then_inc(s["small"], 16)
                for u in range(4):
                    load_unit(sp, k, n0 + u + 2, stream(n0 + u + 2 + 4 * it), it=it, per=4)

        @block.tensor
        def _(pe):
            with pe.Fori(0, GH) as it:
                norm = b.o_norm.at(it)
                unit_ready(pe, k, n0, it, 4)
                pe.wait_ge(s["added"], KT * it)
                dense_tile(pe, k, [k.ps[:, 0:512]], unit_tiles(k, n0, 0, KT, P, 0), k.hhi, k.hlo, SEQ).then_inc(s["projected"], 1)
                dense_tile(pe, k, tile_out(k, 1, TOK)[1], unit_tiles(k, n0, 1024, KT, P, 0), k.hhi, k.hlo, TOK).then_inc(s["projected"], 1)
                pe.wait_ge(s["small"], 32 * (it + 1))
                pe.wait_ge(s["lo_done"], 2 * it)
                for d in range(2):
                    for c0, w in chunks(TOK):
                        last = pe.matmul(k.ps[:, 2048 + 1024 * d + c0:2048 + 1024 * d + c0 + w], b.w2s[32 * d:32 * d + 16, :],
                                         b.lr[32 * d:32 * d + 16, c0:c0 + w], start=True, stop=True)
                    last.then_inc(s["gated"], 1)
                unit_ready(pe, k, n0 + 1, it, 4)
                for t in range(6):
                    if t == 2:
                        pe.wait_ge(s["taken_q"], it + 1)
                    if t == 4:
                        pe.wait_ge(s["taken_k"], it + 1)
                    n = n0 + 1
                    for i in range(KT):
                        w = (k.whi[:, n % 2, i * 256:(i + 1) * 256], k.wlo[:, n % 2, i * 256:(i + 1) * 256])
                        last = mm3(pe, [k.ps[:, V_AT[t]:V_AT[t] + 256]], k.hhi[:, i, t * P:(t + 1) * P],
                                   k.hlo[:, i, t * P:(t + 1) * P], [w], i == 0, i == KT - 1)
                    if t % 2:
                        last.then_inc(s["projected"], 1)
                unit_ready(pe, k, n0 + 2, it, 4)
                for m in range(2):
                    if m == 1:
                        pe.wait_ge(s["taken_v"], 3 * it + 1)
                    dense_tile(pe, k, [k.ps[:, R_AT[m]:R_AT[m] + 512]], unit_tiles(k, n0 + 2, 0, KT, 256, m),
                               k.hhi, k.hlo, SEQ).then_inc(s["projected"], 1)
                pe.wait_ge(s["tilted"], 4 * it + 4)
                pe.wait_ge(s["taken_v"], 3 * it + 3)
                for d in range(2):
                    for t in range(QT):
                        c = slice(t * P, (t + 1) * P)
                        last = pe.matmul(k.ps[:, PS_A[d] + t * P:PS_A[d] + (t + 1) * P], b.kt[:, d, c], b.qt[:, d, c],
                                         start=True, stop=True)
                    last.then_inc(s["attended"], 1)
                for d in range(2):
                    pe.wait_ge(s["tilted_p"], 2 * it + d + 1)
                    for t in range(6):
                        last = pe.transpose(k.ps[:, PS_T[d] + t * P:PS_T[d] + (t + 1) * P], b.ke[:, d, t * P:(t + 1) * P], k.c["ident"])
                    last.then_inc(s["flipped"], 1)
                pe.wait_ge(s["turned"], 2 * it + 2)
                pe.wait_ge(s["taken_r"], 2 * it + 2)

                def update(i):
                    for d in range(2):
                        c = seqs[d][i]
                        r = slice(CH * (c % 2), CH * (c % 2) + CH)
                        if i:
                            pe.wait_ge(upd[d], STEPS * it + i)
                        pe.matmul(k.ps[:, PS_S[d]:PS_S[d] + 256], b.ket[r, d, c // 2, :], b.v[r, c // 2, :],
                                  start=True, stop=True).then_inc(sta[d], 1)

                def inter(i):
                    for d in range(2):
                        c = seqs[d][i]
                        pe.wait_ge(upd[d], STEPS * it + i)
                        for vt in range(2):
                            last = pe.matmul(k.ps[:, PS_O[vt] + c * CH:PS_O[vt] + (c + 1) * CH],
                                             b.state[:, d, i % 2, vt * P:(vt + 1) * P], b.qt[:, d, c * CH:(c + 1) * CH],
                                             start=False, stop=d == 1 and i == NCH - 1, skip_group_check=True)
                    return last

                for i in range(NCH):
                    if i == NCH - LAT:
                        pe.wait_ge(s["masked"], it + 1)
                        for vt in range(2):
                            for t in range(QT):
                                pe.matmul(k.ps[:, PS_O[vt] + t * P:PS_O[vt] + (t + 1) * P], b.v[:, t, vt * P:(vt + 1) * P],
                                          att[0][:, t * P:(t + 1) * P], start=t == 0, stop=False, skip_group_check=True)
                    if i < STEPS:
                        update(i)
                    if i >= NCH - LAT:
                        last = inter(i)
                last.then_inc(s["summed"], 1)
                norm.pe_all(pe)
                unit_ready(pe, k, n0 + 3, it, 4)
                for m in range(KT):
                    if m >= 4:
                        pe.wait_ge(s["added"], KT * it + m - 3)
                    last = dense_tile(pe, k, [k.ps[:, (m % 4) * 512:(m % 4) * 512 + 512]],
                                      unit_tiles(k, n0 + 3, 0, 2, 1024, m), b.o_hi, b.o_lo, SEQ,
                                      (lambda i: pe.wait_ge(s["lo_done"], 2 * it + i + 1)) if m == 0 else None)
                    last.then_inc(s["ready"], 1)

        @block.gpsimd
        def _(pool):
            pool.memset(b.y, 0.0).then_inc(s["zeroed"], 1)
            with pool.Fori(0, GH) as it:
                for d in range(2):
                    pool.wait_ge(s["decays"], 2 * it + d + 1)
                    pool.wait_ge(s["taken_k"], it + 1)
                    pool.tensor_tensor(tail[d], tail[d], b.k, ALU.mult).then_inc(s["tilted_p"], 1)

        def turn_v(dve, it, last_turn):
            norm = b.o_norm.at(it)
            n = 0

            def link(ins):
                nonlocal n
                n += 1
                ins.then_inc(s["chain"], 1)
                dve.wait_ge(s["chain"], CHAIN * it + n)

            CHAIN = 9
            for d in range(2):
                dve.wait_ge(s["gated"], 2 * it + d + 1)
                dve.tensor_scalar(g[d], k.ps[:, 2048 + 1024 * d:2048 + 1024 * d + TOK], b.bias[:, d:d + 1], None,
                                  ALU.add).then_inc(s["biased"], 1)
            for d in range(2):
                dve.wait_ge(s["logd"], 2 * it + d + 1)
                link(dve.scalar_tensor_tensor(g[d], g[d], 0.0, tail[d], ALU.min, ALU.subtract))
                link(dve.tensor_tensor_scan(cum[d], b.reset, g[d], 0.0, ALU.mult, ALU.add))
                total = chunked(cum[d])[:, :, CH - 1:CH]
                if d == 0:
                    dve.tensor_tensor(chunked(tail[0]), total.to_broadcast([P, NCH, CH]), chunked(cum[0]),
                                      ALU.subtract).then_inc(s["ends"], 1)
                else:
                    link(dve.tensor_tensor(tail[1], cum[1], g[1], ALU.subtract))
                    dve.tensor_tensor(chunked(b.kt[:, 1, :]), total[:, 0:LAT].to_broadcast([P, LAT, CH]),
                                      chunked(tail[1][:, 0:SEQ]), ALU.subtract).then_inc(s["ends"], 1)
            split_lo(dve, k, n0 + 2, it=it, per=4)
            for d in range(2):
                dve.wait_ge(s["decays"], 2 * it + d + 1)
                dve.wait_ge(s["taken_q"], it + 1)
                dve.wait_ge(s["taken_k"], it + 1)
                dve.tensor_tensor(b.qt[:, d, :], b.qt[:, d, :], b.q, ALU.mult).then_inc(s["tilted"], 1)
                dve.tensor_tensor(b.kt[:, d, :], b.kt[:, d, :], b.k[:, 0:SEQ], ALU.mult).then_inc(s["tilted"], 1)
            for d, mask in enumerate((k.c["gla_f"], k.c["gla_b"])):
                dve.wait_ge(s["attended"], 2 * it + d + 1)
                link(dve.tensor_scalar(att[d], k.ps[:, PS_A[d]:PS_A[d] + SEQ], BIG, -BIG, ALU.min, ALU.max))
                tiles = att[d].rearrange("p (t q) -> p t q", q=P)
                link(dve.tensor_tensor(tiles, tiles, mask.unsqueeze(1).to_broadcast([P, QT, P]), ALU.mult))
            dve.tensor_tensor(att[0], att[0], att[1], ALU.add).then_inc(s["masked"], 1)
            split_lo(dve, k, n0 + 3, it=it, per=4)
            for i in range(STEPS):
                for d in range(2):
                    c = seqs[d][i]
                    dve.wait_ge(sta[d], STEPS * it + i + 1)
                    new = b.state[:, d, (i + 1) % 2, :]
                    src = k.ps[:, PS_S[d]:PS_S[d] + 256]
                    if i == 0:
                        dve.tensor_copy(new, src).then_inc(upd[d], 1)
                    else:
                        dve.wait_ge(upd[d], STEPS * it + i)
                        dve.scalar_tensor_tensor(new, b.state[:, d, i % 2, :], b.decay[:, d, c:c + 1], src, ALU.mult,
                                                 ALU.add).then_inc(upd[d], 1)
            split_lo(dve, k, n0 + 4, it=it, per=4)
            for t in range(2):
                dve.wait_ge(s["taken_r"], 2 * it + t + 1)
                dve.wait_ge(s["o_out"], 2 * it + t + 1)
                dve.scalar_tensor_tensor(b.of[:, t, :], b.of[:, t, :], b.g_o[:, t:t + 1], b.sr[:, t, :], ALU.mult,
                                         ALU.mult).then_inc(s["gated_o"], 1)
            norm.dve_all(dve)
            for t in range(2):
                dve.wait_ge(s["gated_o"], 2 * it + t + 1)
                dve.tensor_tensor(b.of[:, t, :], b.of[:, t, :], norm.rb, ALU.mult).then_inc(s["value"], 1)
            for t in range(2):
                dve.wait_ge(s["hi_done"], 2 * it + t + 1)
                dve.tensor_tensor(b.o_lo[:, t, :], b.of[:, t, :], b.o_hi[:, t, :].bitcast(F32),
                                  ALU.subtract).then_inc(s["lo_done"], 1)
            dve.wait_ge(s["zeroed"], 1)
            for m in range(KT):
                dve.wait_ge(s["ready"], KT * it + m + 1)
                dve.tensor_tensor(b.y[:, m, :], k.ps[:, (m % 4) * 512:(m % 4) * 512 + 512], b.y[:, m, :],
                                  ALU.add).then_inc(s["added"], 1)
            if not last_turn:
                split_lo(dve, k, n0 + 5, it=it, per=4)
            assert n == CHAIN

        @block.vector
        def _(dve):
            split_lo(dve, k, n0)
            split_lo(dve, k, n0 + 1)
            with dve.Fori(0, GH - 1) as it:
                turn_v(dve, it, False)
            turn_v(dve, GH - 1, True)

        def v_pair(act, pair, P0):
            a = V_AT[2 * pair]
            act.wait_ge(s["projected"], P0 + 3 + pair)
            act.activation(b.v[:, 2 * pair:2 * pair + 2, :].rearrange("p a b -> p (a b)"), k.ps[:, a:a + 512],
                           ACT.Copy).then_inc(s["taken_v"], 1)

        def turn_a(act, it, last_turn):
            norm = b.o_norm.at(it)
            P0 = TILES * it
            act.wait_ge(s["projected"], P0 + 1)
            act.activation(b.q, k.ps[:, 0:512], ACT.Copy, scale=float(P ** -0.5)).then_inc(s["taken_q"], 1)
            act.wait_ge(s["projected"], P0 + 2)
            act.activation(b.k, k.ps[:, 1024:1024 + TOK], ACT.Copy).then_inc(s["taken_k"], 1)
            split_hi(act, k, n0 + 2, (s["projected"], P0 + 2), it=it, per=4)
            for d in range(2):
                act.wait_ge(s["biased"], 2 * it + d + 1)
                act.activation(tail[d], g[d], ACT.Abs).then_inc(s["absd"], 1)
            for d in range(2):
                act.wait_ge(s["absd"], 2 * it + d + 1)
                act.activation(tail[d], tail[d], ACT.Exp, scale=-1.0).then_inc(s["exp1"], 1)
            for d in range(2):
                act.wait_ge(s["exp1"], 2 * it + d + 1)
                act.activation(tail[d], tail[d], ACT.Ln, bias=1.0).then_inc(s["logd"], 1)
            v_pair(act, 0, P0)
            for d in range(2):
                act.wait_ge(s["ends"], 2 * it + d + 1)
                cols = chunked(cum[d])[:, :, CH - 1]
                act.activation(b.decay[:, d, :], cols, ACT.Exp, scale=inv_tau)
                src = cum[0][:, 0:SEQ] if d == 0 else b.kt[:, 1, :]
                act.activation(b.qt[:, d, :], src, ACT.Exp, scale=inv_tau)
                act.activation(tail[d], tail[d], ACT.Exp, scale=inv_tau)
                act.activation(b.kt[:, d, :], src, ACT.Exp, scale=-inv_tau).then_inc(s["decays"], 1)
            v_pair(act, 1, P0)
            v_pair(act, 2, P0)
            split_hi(act, k, n0 + 3, (s["projected"], P0 + 5), it=it, per=4)
            for m in range(2):
                act.wait_ge(s["projected"], P0 + 6 + m)
                act.activation(b.sr[:, m, :], k.ps[:, R_AT[m]:R_AT[m] + 512], ACT.Silu).then_inc(s["taken_r"], 1)
            for d in range(2):
                act.wait_ge(s["flipped"], 2 * it + d + 1)
                act.activation(b.ket[:, d, :, :].rearrange("p a b -> p (a b)"), k.ps[:, PS_T[d]:PS_T[d] + TOK],
                               ACT.Copy).then_inc(s["turned"], 1)
            split_hi(act, k, n0 + 4, (s["projected"], P0 + 7), it=it, per=4)
            act.wait_ge(s["summed"], it + 1)
            norm.act_square(act, 0)
            norm.act_square(act, 1)
            norm.act_table(act)
            act.wait_ge(s["lo_done"], 2 * it)
            act.activation(b.of[:, 0, :], k.ps[:, PS_O[0]:PS_O[0] + 512], ACT.Copy).then_inc(s["o_out"], 1)
            act.activation(b.of[:, 1, :], k.ps[:, PS_O[1]:PS_O[1] + 512], ACT.Copy).then_inc(s["o_out"], 1)
            norm.act_root(act)
            for t in range(2):
                act.wait_ge(s["value"], 2 * it + t + 1)
                act.activation(b.o_hi[:, t, :], b.of[:, t, :], ACT.Copy).then_inc(s["hi_done"], 1)
            if not last_turn:
                split_hi(act, k, n0 + 5, (s["ready"], KT * it + KT), it=it, per=4)

        @block.scalar
        def _(act):
            split_hi(act, k, n0)
            split_hi(act, k, n0 + 1)
            with act.Fori(0, GH - 1) as it:
                turn_a(act, it, False)
            turn_a(act, GH - 1, True)

    return n0 + U_GLA * GH


def second_block(nc, k, a):
    at = k.at
    b = Bag()
    stream = lambda n: a["stream2"][n]
    k.hhi, k.hlo = at("h_hi_2", [P, KT, TOK], F32R, 60), at("h_lo_2", [P, KT, TOK], F32R, 84)
    b.axial = at("axial", [P, 2, SEQ], F32, 108)
    b.mod = k.mod.rearrange("p (l t v) -> p l t v", t=KT, v=2)
    b.sc = at("norm_scales", [P, 4 * DEPTH, KT, 2], F32, 112.75)
    b.g_q, b.g_kv, b.g_o = at("g_q", [P, 3], F32, 113.25), at("g_kv", [P, 2], F32, 113.3125), at("g_o", [P, 2], F32, 113.375)
    b.st, b.spare = at("mla_stat", [P, 2, 4], F32, 113.5), at("spare", [P, 1], F32, 113.5625)
    b.ada_b, b.g = at("ada_b", [P, ADA_TURNS, KT], F32, 117), at("norm_g2", [P, DEPTH, 4, KT], F32, 118)
    y = at("y2", [P, KT, TOK], F32, 151)
    down = at("mla_down", [P, 6, TOK], F32, 151)
    b.cq_hi, b.cq_lo = at("cq_hi", [P, 3, TOK], F32R, 114), at("cq_lo", [P, 3, TOK], F32R, 123)
    b.ckv_hi, b.ckv_lo = at("ckv_hi", [P, 2, TOK], F32R, 132), at("ckv_lo", [P, 2, TOK], F32R, 138)
    b.krope = at("k_rope", [P, TOK], F32, 144)
    b.v, b.vst = at("mla_v", [P, TOK // P, MH * P], F32, 147), k.diag.rearrange("p (t n) -> p t n", n=P)
    b.qn, b.qr, b.kn = at("q_nope", [P, TOK], F32, 171), at("q_rope", [P, TOK], F32, 174), at("k_nope", [P, TOK], F32, 177)
    b.qraw, b.qcos = at("q_raw", [P, SEQ], F32, 180), at("q_cos", [P, SEQ], F32, 182)
    b.p, b.pt = k.sqt, at("mla_pt", [P, 2, TOK], F32, 184)
    hid_hi, hid_lo = at("hid_hi2", [P, 4, TOK], F32R, 127), at("hid_lo2", [P, 4, TOK], F32R, 139)

    rings(k, "second", 175)
    stage_modulation(nc, k, b, a, stream)
    n = 0
    with k.sem_scope():
        n = stage_norm_dense(nc, k, "down", stream, n, U_DOWN, UNIT, 256, down, TOK, parts_of(b, 0, 0, TOK, 0))
        stage_norm(nc, k, "cq", down[:, 0:3, :], 3, b.cq_hi, b.cq_lo, b.g_q)
        stage_norm(nc, k, "ckv", down[:, 3:5, :], 2, b.ckv_hi, b.ckv_lo, b.g_kv)
        n = stage_key_rope_values(nc, k, b, down[:, 5, :], stream, n)
        k.whi, k.wlo = at("w_hi_mla", [P, 2, MLA_U], F32R, 191), at("w_lo_mla", [P, 2, MLA_U], F32R, 199)
        n = stage_latent_attention(nc, k, b, stream, n)
        rings(k, "rest", 175)
        n = stage_project(nc, k, "mla_o", stream, n, k.hhi, k.hlo, y, TOK, UNITS_2)
    with k.sem_scope():
        n = stage_mlp(nc, k, "mlp0", stream, n, y, hid_hi, hid_lo, TOK, parts_of(b, 0, 1, TOK), parts_of(b, 0, 2, TOK, 3), UNITS_2)
        stage_residual(nc, k, "mlp0r", y, TOK, parts_of(b, 0, 3, TOK))
    c = Bag()
    c.g_o = b.g_o
    low = at("gate_low", [P, 1, TOK], F32, 114)
    c.lr = low[:, 0, :]
    c.q, c.k, c.v = at("gla_q", [P, SEQ], F32, 117), at("gla_k", [P, TOK], F32, 119), at("gla_v", [P, 6, 256], F32, 122)
    c.sr, c.ke, c.of = at("silu_r", [P, 2, SEQ], F32, 128), at("k_end", [P, 2, TOK], F32, 132), at("gla_o", [P, 2, SEQ], F32, 132)
    c.qt, c.kt = at("q_tilt", [P, 2, SEQ], F32, 138), at("k_tilt", [P, 2, SEQ], F32, 142)
    c.o_hi, c.o_lo = at("gla_o_hi", [P, 2, SEQ], F32R, 138), at("gla_o_lo", [P, 2, SEQ], F32R, 142)
    c.ket, c.state = at("k_end_t", [P, 2, 6, P], F32, 146), at("state", [P, 2, 2, 256], F32, 152)
    c.reset, c.y = at("chunk_reset", [P, TOK], F32, 156), at("y3", [P, KT, SEQ], F32, 159)
    c.w2s, c.bias, c.decay = at("gate2", [64, P], F32, 59.25), at("gate_bias", [P, 2], F32, 59.8125), at("decay", [P, 2, 12], F32, 59.875)
    n = stage_norm_dense(nc, k, "gate1", stream, n, U_GATE, 1024, P, low, TOK,
                         parts_of(b, 1, 0, TOK, 0))
    c.o_norm = Norm(k, "o_norm", k.ps[:, 2048:3072].rearrange("p (t q) -> p t q", q=SEQ), 2, SEQ, 6)
    r_set = k.sem("reset_set")
    with nc.Block() as block:
        @block.vector
        def _(dve):
            dve.memset(c.reset, 1.0).then_inc(r_set, 1)
            dve.wait_ge(r_set, 1)
            dve.memset(c.reset.rearrange("p (c i) -> p c i", i=CH)[:, :, 0:1], 0.0)
    n = stage_gla_heads(nc, k, c, a, stream, n)
    hid_hi, hid_lo = at("hid_hi3", [P, 4, SEQ], F32R, 114), at("hid_lo3", [P, 4, SEQ], F32R, 122)
    y_norm = Norm(k, "mlp1_norm", c.y, KT, SEQ, 5)
    n = stage_mlp(nc, k, "mlp1", stream, n, c.y, hid_hi, hid_lo, SEQ, parts_of(b, 1, 1, SEQ), parts_of(b, 1, 2, SEQ, 3), UNITS_2, y_norm)
    stage_residual(nc, k, "mlp1r", c.y, SEQ, parts_of(b, 1, 3, SEQ), y_norm)
    assert n == UNITS_2


def second_arrays(g, a):
    col = lambda v: np.ascontiguousarray(v.reshape(-1, P).T)
    a["axial"] = axial_table()
    a["cvec"] = np.stack([col(g["c_2"][0]), col(g["c_ctx_2"])], 2)
    a["ada_b"] = np.ascontiguousarray(g["ada_b_2"].reshape(ADA_TURNS, KT, P).transpose(2, 0, 1))
    a["norm_g2"] = np.ascontiguousarray(g["norm_g_2"].reshape(DEPTH, 4, KT, P).transpose(3, 0, 1, 2))
    a["g_q"], a["g_kv"], a["g_o"] = col(g["mla_g_q_2"][0]), col(g["mla_g_kv_2"][0]), col(g["gla_g_o_2"][0])
    a["ada_w"] = np.stack([units(g["ada_w_2"][l], KT, 256, U_ADA).reshape(U_ADA, P, 2, UNIT // 2).transpose(0, 2, 1, 3)
                           .reshape(2 * U_ADA, P, UNIT // 2) for l in range(DEPTH)])
    out = []
    dkv = g["mla_w_dkv_2"][0]
    out.append(units(np.concatenate([g["mla_w_dq_2"][0], dkv, dkv[:, 256:]], 1), KT, 256, U_DOWN))
    uq, ukv = g["mla_w_uq_2"][0], g["mla_w_ukv_2"][0]
    out.append(units(np.concatenate([ukv[:, 256 * h + P:256 * (h + 1)] for h in range(MH)], 1), 2, 1024, 1))
    for h in range(MH):
        q, kv = uq[:, 192 * h:192 * (h + 1)], ukv[:, 256 * h:256 * (h + 1)]
        row = np.concatenate([units(q[:, :P], 3, P, 1), units(np.concatenate([q[:, P:], q[:, P:]], 1), 3, P, 1),
                              units(kv[:, :P], 2, P, 1)], 2)
        out.append(np.concatenate([row, np.zeros((1, P, UNIT - MLA_U), row.dtype)], 2))
    out.append(units(g["mla_w_o_2"][0], KT, 256, 4))
    out.append(mlp_units(g["mlp_w1_2"][0], g["mlp_w2_2"][0]))
    w1 = g["gla_w_gate1_2"][0]
    z = np.zeros((D, 16), w1.dtype)
    gate = units(np.concatenate([w1[0], z, w1[1], z], 1), KT, P, 1)
    out.append(np.concatenate([gate, np.zeros_like(gate)], 2))
    wq, wk, wv, wr, wo = (g[f"gla_w_{c}_2"][0] for c in "qkvro")
    for h in range(GH):
        out.append(np.concatenate([units(w[:, P * h:P * (h + 1)], KT, P, 1) for w in (wq, wk)], 2))
        out.append(units(wv[:, 256 * h:256 * (h + 1)], KT, 256, 1))
        out.append(units(wr[:, 256 * h:256 * (h + 1)], KT, 256, 1))
        out.append(units(wo[256 * h:256 * (h + 1)], 2, 1024, 1))
    out.append(mlp_units(g["mlp_w1_2"][1], g["mlp_w2_2"][1]))
    a["stream2"] = np.concatenate(out)
    assert a["stream2"].shape == (UNITS_2, P, UNIT)
    w2 = g["gla_w_gate2_2"][0]
    low = np.zeros((GH, 64, P), w2.dtype)
    for d in range(2):
        low[:, 32 * d:32 * d + 16] = w2[d].reshape(16, GH, P).transpose(1, 0, 2)
    a["gla_w2"] = low
    a["gla_b"] = np.ascontiguousarray(g["gla_b_gate_2"][0].reshape(2, GH, P).transpose(1, 2, 0))



def rings(k, sec, kb):
    k.whi = k.at(f"w_hi_{sec}", [P, 2, UNIT], F32R, kb)
    k.wlo = k.at(f"w_lo_{sec}", [P, 2, UNIT], F32R, kb + 16)


def first_block(nc, k, a):
    at = k.at
    b = Bag()
    k.hhi, k.hlo = at("h_hi_1", [P, KT, SEQ], F32R, 60), at("h_lo_1", [P, KT, SEQ], F32R, 76)
    b.cos, b.sin = at("rope_cos", [P, SEQ], F32, 92), at("rope_sin", [P, SEQ], F32, 94)
    b.g, b.inv = at("norm_g1", [P, 4, KT], F32, 96), at("rope_inv", [P, 1], F32, 96.25)
    b.pos_i = at("positions_i", [P, SEQ], I32, 97)
    stage_rope_tables(nc, k, b, a["positions"], a["inv_freq"],
                      [(k.x[:, :, 0:SEQ], a["x"]), (k.x[:, :, SEQ:TOK], a["ctx"]), (k.consts, a["consts"]), (k.cv, a["cvec"])])

    b.sbq, b.sbk, b.sbv = at("sbq", [P, 4, SEQ], F32, 97), at("sbk", [P, 4, SEQ], F32, 105), at("sbv", [P, QT, 512], F32, 113)
    b.q, b.kk, b.vv = at("q", [P, 4, SEQ], F32, 121), at("kk", [P, 2, SEQ], F32, 129), at("vv", [P, SEQ], F32, 133)
    b.kv_cmp, b.gate_t = at("kv_cmp", [P, 2, SEQ], F32, 135), at("gate_t", [24, SEQ], F32, 139)
    b.qr, b.kr = at("qr", [P, 4, SEQ], F32, 141), at("kr", [P, 2, SEQ], F32, 149)
    b.v, b.gate = at("v", [P, QT, P], F32, 153), at("gate", [P, QT, 24], F32, 155)
    b.kc, b.vc = at("kc", [P, NCP], F32, 155.5), at("vc", [NCP, 64], F32, 155.75)
    half = CMP_T // 2
    b.w2, b.pe = at("w2", [P, 2, 2, P], F32, 156), at("pe", [P, 2, half], F32, 158)
    b.blk = at("blk", [P, 2, half, NCP], F32, 159)
    b.hid_row, b.cw = at("cmp_hid_row", [NC, 2, 256], F32, 163), at("cmp_w1", [P, UNITS_CMP, UNIT], F32, 175)
    b.hid = at("cmp_hid", [P, 2, 2, NCP], F32, 171)
    b.pct = at("pct", [NCP, HEADS, SEQ], F32, 157)
    b.cst, b.sst = at("cst", [P, 4, HEADS], F32, 173), at("sst", [P, 2, 5, 2], F32, 173.5)
    b.pc = at("pc", [P, QT, HEADS, NCP], F32, 175)
    b.p, b.pt = at("p", [P, 2, 2, SEQ], F32, 175), at("pt", [P, 2, 2, SEQ], F32, 183)
    b.qst, b.pcst = k.diag[:, 0:SEQ], at("pcst", [NC, 2, SEQ], F32, 47)
    b.onhi, b.onlo = at("on_hi", [P, 4, SEQ], F32R, 191), at("on_lo", [P, 4, SEQ], F32R, 199)
    b.sp, b.tot, b.a = at("sp", [P, QT, SEQ], F32, 121), at("tot", [P, QT + 1, SEQ], F32, 129), at("sba", [P, QT, SEQ], F32, 139)
    b.kst, b.vst = at("kst", [P, SEQ], F32, 147), at("vst", [P, QT, P], F32, 149)
    b.oshi, b.oslo = at("os_hi", [P, 4, SEQ], F32R, 175), at("os_lo", [P, 4, SEQ], F32R, 183)
    b.mhi, b.mlo = at("m_hi", [P, KT, SEQ], F32R, 129), at("m_lo", [P, KT, SEQ], F32R, 145)
    b.gt, b.mt = at("gt", [P, 4, SEQ], F32, 161), at("mt", [P, 2, SEQ], F32, 169)
    ada = Bag()
    ada.raw, ada.lo = [], []
    for kb in (145, 191):
        raw, lo = at(f"ada_raw{kb}", [P, 3, UNIT // 2], F32, kb), at(f"ada_lo{kb}", [P, 3, UNIT // 2], F32R, kb)
        ada.raw = [*ada.raw, *(raw[:, i, :] for i in range(3))]
        ada.lo = [*ada.lo, *(lo[:, i, :] for i in range(3))]
    ada.hi, ada.row = at("ada_hi", [P, 3, UNIT // 2], F32R, 177), at("ada_row", [4, 2, 256], F32, 189)
    y = at("y1", [P, KT, SEQ], F32, 161)
    hid_hi, hid_lo = at("hid_hi1", [P, 4, SEQ], F32R, 129), at("hid_lo1", [P, 4, SEQ], F32R, 137)

    with nc.Fori(0, DEPTH) as layer, k.sem_scope(*k.w_loaded, k.w_hi, k.w_lo):
        stream = lambda n: a["stream1"][layer, n]
        ada.layer, ada.src = layer, lambda n: a["ada_w"][layer, n]
        b.g_src = a["norm_g"][layer]
        b.w2_src = [a["cmp_w2"][layer, c] for c in range(2)]
        b.cw_src = [a["cmp_w1"][layer, u] for u in range(UNITS_CMP)]
        b.pe_src = [a["cmp_pe"][layer, c] for c in range(2)]
        rings(k, "qkv", 175)
        n = stage_qkv(nc, k, b, stream, 0)
        stage_rope(nc, k, b)
        stage_compress(nc, k, b)
        stage_cmp_attention(nc, k, b)
        stage_causal_attention(nc, k, b)
        stage_stick_breaking(nc, k, b)
        rings(k, "mix", 97)
        n = stage_merge(nc, k, b, stream, n)
        wo_norm, ff_norm = Norm(k, "wo_norm", y, KT, SEQ, 4), Norm(k, "ff_norm", y, KT, SEQ, 5)
        n = stage_project(nc, k, "wo", stream, n, b.mhi, b.mlo, y, SEQ, UNITS_1, wo_norm, 1)
        n = stage_mlp(nc, k, "ff", stream, n, y, hid_hi, hid_lo, SEQ,
                      [(0, SEQ, b.g[:, 1, :])], [(0, SEQ, b.g[:, 2, :], None)], UNITS_1, ff_norm, wo_norm, ada)
        assert n == UNITS_1
        stage_residual(nc, k, "ffr", y, SEQ, [(0, SEQ, b.g[:, 3, :])], ff_norm)


def build(nc, a):
    with ExitStack() as es:
        k = Bag()
        k.scope = (es, [])

        def sem(name):
            stack, sems = k.scope
            sems.append(stack.enter_context(nc.semaphore(name)))
            return sems[-1]

        @contextmanager
        def sem_scope(*more):
            outer = k.scope
            with ExitStack() as stack:
                k.scope = (stack, [])
                yield
                with nc.Block() as block:
                    @block.sync
                    def _(sp):
                        for s in [*k.scope[1], *more]:
                            sp.sem_clear(s)
                k.scope = outer

        k.sem, k.sem_scope = sem, sem_scope
        k.w_loaded = [sem(f"w_loaded{i}") for i in range(2)]
        k.w_hi, k.w_lo = sem("w_hi"), sem("w_lo")
        k.ps = es.enter_context(nc.psum_tensor("ps", [P, 4096], F32))[:]
        origin = -(-nc.sbuf_base // 32) * 32

        def at(name, shape, dt, kb):
            return nc.alloc_sbuf_tensor_at(name, shape, dt, offset=origin + int(kb * 1024))[:]

        k.at = at
        k.consts = consts = at("consts", [P, len(CONSTS) * P], F32, 0)
        k.c = {n: consts[:, i * P:(i + 1) * P] for i, n in enumerate(CONSTS)}
        k.c["eps"], k.c["pairs"] = k.c["small"][:, 0:1], k.c["small"][:, 1:3]
        k.cv_parts = at("cvec_parts", [P, KT, 4], F32R, 59.375)
        k.x = at("x", [P, KT, TOK], F32, 7)
        k.raw = at("w_raw", [P, 2, UNIT], F32, 31)
        k.sqt, k.acc, k.diag = at("sq", [P, 2, TOK], F32, 47), at("acc", [P, TOK], F32, 53), at("diag", [P, TOK], F32, 56)
        k.nst, k.root = at("norm_stat", [P, 8], F32, 59), k.acc[0:1, :]

        k.tiny = at("tiny", [P, 1], F32, 207.75)
        k.cv, k.mod = at("cvec", [P, KT, 2], F32, 59.25), at("mod", [P, ADA_TURNS * KT * 2], F32, 207)

        first_block(nc, k, a)
        second_block(nc, k, a)

        stored = sem("stored")
        with nc.Block() as block:
            @block.sync
            def _(sp):
                sp.dma_start(a["out"], k.x[:, :, 0:SEQ]).then_inc(stored, 16)
                sp.wait_ge(stored, 16)


def feature_major(t):
    n, d = t.shape
    return np.ascontiguousarray(t.T.reshape(d // P, P, n).transpose(1, 0, 2))


def units(w, kt, cols, n):
    w = np.concatenate([w, np.zeros((w.shape[0], n * cols - w.shape[1]), w.dtype)], 1) if w.shape[1] < n * cols else w
    return w.reshape(kt, P, n, cols).transpose(2, 1, 0, 3).reshape(n, P, kt * cols)


def mlp_units(w1, w2):
    out = []
    for g in range(FF_GROUPS):
        out.append(units(w1[:, 512 * g:512 * (g + 1)], KT, 256, 2))
        out.append(units(w2[512 * g:512 * (g + 1)], 4, 512, 2))
    return np.concatenate(out)


def stream_1(w_in, w_nsa_o, w_sb_o, w_out, w_ff1, w_ff2):
    pad = np.zeros((D, 104), w_in.dtype)
    qkv = np.concatenate([w_in[:, :920], pad, w_in[:, 920:2456]], 1)
    out = [units(qkv, KT, 256, UNITS_QKV)]
    gates = units(w_in[:, 2456:], KT, 256, 8)
    no, so = units(w_nsa_o, 4, 256, 4), units(w_sb_o, 4, 256, 4)
    for pr in range(4):
        out.append(np.stack([gates[pr], gates[4 + pr], np.concatenate([no[pr], so[pr]], 1)]))
    out.append(units(w_out, KT, 256, 4))
    out.append(mlp_units(w_ff1, w_ff2))
    out = np.concatenate(out)
    assert out.shape == (UNITS_1, P, UNIT)
    return out


def host_arrays(i):
    g = {n: np.asarray(v) for n, v in i.items()}
    a = {}
    a["x"] = feature_major(g["x"][0])
    a["ctx"] = feature_major(g["ctx_2"][0])
    a["positions"] = np.ascontiguousarray(g["positions"][0])
    a["consts"] = const_table()
    a["inv_freq"] = inv_freq_column()
    a["norm_g"] = np.ascontiguousarray(g["norm_g"].reshape(DEPTH, 4, KT, P).transpose(0, 3, 1, 2))
    a["cmp_pe"] = np.ascontiguousarray(g["cmp_pe"].reshape(DEPTH, 2, 16, P).transpose(0, 1, 3, 2))
    a["cmp_w1"] = g["cmp_w1"].reshape(DEPTH, UNITS_CMP, 8, P, 256).transpose(0, 1, 3, 2, 4).reshape(DEPTH, UNITS_CMP, P, UNIT)
    a["cmp_w2"] = g["cmp_w2"]
    a["stream1"] = np.stack([stream_1(*(g[n][l] for n in ("w_in", "w_nsa_o", "w_sb_o", "w_out", "w_ff1", "w_ff2")))
                             for l in range(DEPTH)])
    second_arrays(g, a)
    return a


def kernel(**inputs):
    import concourse.bacc as _bacc
    from concourse.bass_utils import run_bass_kernel_spmd as _run

    nc = _bacc.Bacc("TRN2", target_bir_lowering=False, num_devices=1)
    arrays = {f"in_{n}": np.ascontiguousarray(v) for n, v in host_arrays(inputs).items()}
    a = {n[3:]: nc.dram_tensor(n, v.shape, mybir.dt.from_np(v.dtype), kind="ExternalInput").ap() for n, v in arrays.items()}
    a["out"] = nc.dram_tensor("out", (P, KT, SEQ), F32, kind="ExternalOutput").ap()
    build(nc, a)
    r = _run(nc, [arrays], core_ids=[0])
    got = r.results[0]["out"]
    return np.ascontiguousarray(got.transpose(1, 0, 2).reshape(D, SEQ).T).reshape(1, SEQ, D)
```
